# Optimizing a Trainium2 kernel written in Bass

```python
import jax, jax.numpy as jnp
from jax import lax
import numpy as np
import math

D_MODEL = 2048
BATCH = 1
SEQ = 256
DEPTH = 1

N_HEADS = 8
N_KV_HEADS = 2
HEAD_DIM = 128
ATTN_WIDTH = N_HEADS * HEAD_DIM
KV_WIDTH = N_KV_HEADS * HEAD_DIM
ROPE_THETA = 500000.0
ROPE_FRACTION = 4
IDX_HEADS = 16
IDX_DIM = 64
TOPK_MAX = 256
Q_BLOCK = 128
POOL_GROUPS = 4
POOL_WINDOWS = (2, 4, 8, 16)
POOL_WIDTH = D_MODEL - ATTN_WIDTH
POOL_GROUP_DIM = POOL_WIDTH // POOL_GROUPS
MIX_WIDTH = ATTN_WIDTH + POOL_WIDTH
N_EXPERT_GROUPS = 4
EXPERTS_PER_GROUP = 8
N_EXPERTS = N_EXPERT_GROUPS * EXPERTS_PER_GROUP
EXPERT_TOPK = 2
D_EXPERT = 512
NORM_EPS = 1e-6
PROJ_SPLITS = (ATTN_WIDTH, KV_WIDTH, KV_WIDTH, IDX_HEADS * IDX_DIM, IDX_DIM, IDX_HEADS, POOL_WIDTH)
PROJ_WIDTH = sum(PROJ_SPLITS)


def rmsnorm(x, g):
    xf = x.astype(jnp.float32)
    y = xf * lax.rsqrt(jnp.mean(xf * xf, axis=-1, keepdims=True) + NORM_EPS)
    return y.astype(x.dtype) * g

def modulate(xn, shift, scale):
    return xn * (1.0 + scale[:, None, :]) + shift[:, None, :]

def rope_partial(x, pos):
    d = x.shape[-1]
    rd = d // ROPE_FRACTION
    half = rd // 2
    inv = jnp.float32(ROPE_THETA) ** (-(jnp.arange(half, dtype=jnp.float32) * 2.0) / rd)
    ang = pos[:, None] * inv[None, :]
    cos = jnp.cos(ang)[None, :, None, :]
    sin = jnp.sin(ang)[None, :, None, :]
    xr = x[..., :rd].astype(jnp.float32)
    x1, x2 = xr[..., :half], xr[..., half:]
    rot = jnp.concatenate([x1 * cos - x2 * sin, x2 * cos + x1 * sin], axis=-1).astype(x.dtype)
    return jnp.concatenate([rot, x[..., rd:]], axis=-1)

def dsa_attention(q, k, v, qi, ki, wi):
    B, S = q.shape[0], q.shape[1]
    n_sel = min(TOPK_MAX, S // 4)
    nb = S // Q_BLOCK
    rep = N_HEADS // N_KV_HEADS

    def to_blocks(a):
        return jnp.moveaxis(a.reshape((B, nb, Q_BLOCK) + a.shape[2:]), 1, 0)

    t_blocks = jnp.arange(S, dtype=jnp.int32).reshape(nb, Q_BLOCK)
    s_pos = jnp.arange(S, dtype=jnp.int32)
    b_ix = jnp.arange(B)[:, None, None]
    idx_scale = (IDX_DIM ** -0.5) * (IDX_HEADS ** -0.5)
    attn_scale = HEAD_DIM ** -0.5
    kif = ki.astype(jnp.float32)

    def one_block(args):
        qb, qib, wib, tb = args
        logits = jnp.einsum('bthd,bsd->bths', qib.astype(jnp.float32), kif)
        score = jnp.einsum('bths,bth->bts', jax.nn.relu(logits), wib.astype(jnp.float32)) * idx_scale
        causal = s_pos[None, :] <= tb[:, None]
        score = jnp.where(causal[None], score, -jnp.inf)
        _, sel = lax.top_k(score, n_sel)
        valid = sel <= tb[None, :, None]
        kg = k[b_ix, sel].astype(jnp.float32)
        vg = v[b_ix, sel].astype(jnp.float32)
        qg = qb.reshape(B, Q_BLOCK, N_KV_HEADS, rep, HEAD_DIM).astype(jnp.float32)
        s = jnp.einsum('btgrd,btkgd->btgrk', qg, kg) * attn_scale
        s = jnp.where(valid[:, :, None, None, :], s, -jnp.inf)
        p = jax.nn.softmax(s, axis=-1)
        o = jnp.einsum('btgrk,btkgd->btgrd', p, vg).astype(qb.dtype)
        return o.reshape(B, Q_BLOCK, ATTN_WIDTH)

    out = lax.map(one_block, (to_blocks(q), to_blocks(qi), to_blocks(wi), t_blocks))
    return jnp.moveaxis(out, 0, 1).reshape(B, S, ATTN_WIDTH)

def multiscale_pool(p, w_pool, pool_scale):
    B, S = p.shape[0], p.shape[1]
    pg = p.reshape(B, S, POOL_GROUPS, POOL_GROUP_DIM).astype(jnp.float32)
    cs = jnp.cumsum(pg, axis=1)
    cs_pad = jnp.pad(cs, ((0, 0), (1, 0), (0, 0), (0, 0)))
    win = jnp.array(POOL_WINDOWS, dtype=jnp.int32)
    t = jnp.arange(S, dtype=jnp.int32)[:, None]
    lo = jnp.maximum(t + 1 - win[None, :], 0)
    lag = cs_pad[:, lo, jnp.arange(POOL_GROUPS)[None, :], :]
    count = jnp.minimum(t + 1, win[None, :]).astype(jnp.float32)
    mixed = (cs - lag) / count[None, :, :, None] - pg
    y = jnp.einsum('bsgc,gcd->bsgd', mixed.astype(p.dtype), w_pool) * pool_scale
    return y.reshape(B, S, POOL_WIDTH)

def hier_moe(h, w_grp, w_exp, w1, w3, w2):
    B, S, D = h.shape
    ht = h.reshape(-1, D)
    pg = jax.nn.softmax((ht @ w_grp).astype(jnp.float32), axis=-1)
    g_sel = jnp.argmax(pg, axis=-1)
    p_g = jnp.max(pg, axis=-1)
    el = (ht @ w_exp).astype(jnp.float32).reshape(-1, N_EXPERT_GROUPS, EXPERTS_PER_GROUP)
    el_sel = jnp.take_along_axis(el, g_sel[:, None, None], axis=1)[:, 0]
    pe = jax.nn.softmax(el_sel, axis=-1)
    top_p, top_i = lax.top_k(pe, EXPERT_TOPK)
    top_w = top_p / jnp.sum(top_p, axis=-1, keepdims=True) * p_g[:, None]
    eid = g_sel[:, None] * EXPERTS_PER_GROUP + top_i
    combine = jnp.einsum('tke,tk->te', jax.nn.one_hot(eid, N_EXPERTS, dtype=jnp.float32), top_w)
    y = jnp.zeros((ht.shape[0], D), jnp.float32)
    for e in range(N_EXPERTS):
        a = jax.nn.silu(ht @ w1[e]) * (ht @ w3[e])
        y = y + combine[:, e:e + 1] * (a @ w2[e]).astype(jnp.float32)
    return y.astype(h.dtype).reshape(B, S, D)

def first_inputs(seed: int = 0) -> dict:
    key = jax.random.key(seed)
    ks = jax.random.split(key, 20)
    f32 = jnp.float32
    L, D = DEPTH, D_MODEL
    nrm = lambda k, shape, s: jax.random.normal(k, shape, f32) * s
    return {
        "x": nrm(ks[0], (BATCH, SEQ, D), 1.0),
        "c": nrm(ks[1], (BATCH, D), 1.0),
        "w_ada": nrm(ks[2], (L, D, 6 * D), 0.5 * D ** -0.5),
        "b_ada": nrm(ks[3], (L, 6 * D), 0.02),
        "norm1_g": 1.0 + nrm(ks[4], (L, D), 0.02),
        "w_in": nrm(ks[5], (L, D, PROJ_WIDTH), D ** -0.5),
        "q_norm_g": 1.0 + nrm(ks[6], (L, HEAD_DIM), 0.02),
        "k_norm_g": 1.0 + nrm(ks[7], (L, HEAD_DIM), 0.02),
        "w_pool": nrm(ks[8], (L, POOL_GROUPS, POOL_GROUP_DIM, POOL_GROUP_DIM), POOL_GROUP_DIM ** -0.5),
        "pool_scale": 1.0 + nrm(ks[9], (L, POOL_GROUPS, POOL_GROUP_DIM), 0.02),
        "w_out": nrm(ks[10], (L, MIX_WIDTH, D), MIX_WIDTH ** -0.5),
        "norm2_g": 1.0 + nrm(ks[11], (L, D), 0.02),
        "w_grp": nrm(ks[12], (L, D, N_EXPERT_GROUPS), D ** -0.5),
        "w_exp": nrm(ks[13], (L, D, N_EXPERTS), D ** -0.5),
        "w1": nrm(ks[14], (L, N_EXPERTS, D, D_EXPERT), D ** -0.5),
        "w3": nrm(ks[15], (L, N_EXPERTS, D, D_EXPERT), D ** -0.5),
        "w2": nrm(ks[16], (L, N_EXPERTS, D_EXPERT, D), D_EXPERT ** -0.5),
    }

def first_block(x, c, w_ada, b_ada, norm1_g, w_in, q_norm_g, k_norm_g, w_pool, pool_scale,
              w_out, norm2_g, w_grp, w_exp, w1, w3, w2):
    B, S, D = x.shape
    pos = jnp.arange(S, dtype=jnp.float32)
    offsets = [int(o) for o in np.cumsum(PROJ_SPLITS)[:-1]]
    for l in range(DEPTH):
        ada = jax.nn.silu(c) @ w_ada[l] + b_ada[l]
        sh1, sc1, gt1, sh2, sc2, gt2 = jnp.split(ada, 6, axis=-1)
        h = modulate(rmsnorm(x, norm1_g[l]), sh1, sc1)
        proj = h @ w_in[l]
        q, k, v, qi, ki, wi, p = jnp.split(proj, offsets, axis=-1)
        q = rope_partial(rmsnorm(q.reshape(B, S, N_HEADS, HEAD_DIM), q_norm_g[l]), pos)
        k = rope_partial(rmsnorm(k.reshape(B, S, N_KV_HEADS, HEAD_DIM), k_norm_g[l]), pos)
        v = v.reshape(B, S, N_KV_HEADS, HEAD_DIM)
        qi = rope_partial(qi.reshape(B, S, IDX_HEADS, IDX_DIM), pos)
        ki = rope_partial(ki.reshape(B, S, 1, IDX_DIM), pos)[:, :, 0]
        attn_out = dsa_attention(q, k, v, qi, ki, wi)
        pool_out = multiscale_pool(p, w_pool[l], pool_scale[l])
        mix = jnp.concatenate([attn_out, pool_out], axis=-1) @ w_out[l]
        x = x + gt1[:, None, :] * mix
        h2 = modulate(rmsnorm(x, norm2_g[l]), sh2, sc2)
        x = x + gt2[:, None, :] * hier_moe(h2, w_grp[l], w_exp[l], w1[l], w3[l], w2[l])
    return x


DEPTH_2 = 2

BLOCK = 128

LRU_WIDTH = 1024
LRU_BLOCKS = 8
LRU_BLOCK_DIM = LRU_WIDTH // LRU_BLOCKS
CONV_WIDTH = 4
LRU_C = 8.0
SWA_Q_HEADS = 16
SWA_KV_HEADS = 2
SWA_HEAD_DIM = 64
SWA_GROUP = SWA_Q_HEADS // SWA_KV_HEADS
SWA_WIDTH = SWA_Q_HEADS * SWA_HEAD_DIM
SWA_KV_WIDTH = SWA_KV_HEADS * SWA_HEAD_DIM
WINDOW = 128
EVEN_SPLITS = [LRU_WIDTH, LRU_WIDTH, SWA_WIDTH, SWA_KV_WIDTH, SWA_KV_WIDTH, SWA_WIDTH]
EVEN_IN = sum(EVEN_SPLITS)
EVEN_MIX = LRU_WIDTH + SWA_WIDTH

MLA_HEADS = 8
MLA_Q_RANK = 768
MLA_KV_RANK = 512
MLA_NOPE = 128
MLA_ROPE = 64
MLA_V = 128
MLA_WIDTH = MLA_HEADS * MLA_V
ROPE_THETA_2 = 10000.0
DIFF_HEADS = 8
DIFF_QK = 64
DIFF_V = 2 * DIFF_QK
DIFF_QK_WIDTH = DIFF_HEADS * 2 * DIFF_QK
DIFF_WIDTH = DIFF_HEADS * DIFF_V
DIFF_LAYER_IDX = 1
DIFF_LAMBDA_INIT = 0.8 - 0.6 * math.exp(-0.3 * DIFF_LAYER_IDX)
ODD_SPLITS = [MLA_Q_RANK, MLA_KV_RANK, MLA_ROPE, MLA_WIDTH,
              DIFF_QK_WIDTH, DIFF_QK_WIDTH, DIFF_WIDTH, DIFF_WIDTH]
ODD_IN = sum(ODD_SPLITS)
ODD_MIX = MLA_WIDTH + DIFF_WIDTH


def rmsnorm_2(x, g):
    xf = x.astype(jnp.float32)
    y = xf * lax.rsqrt(jnp.mean(xf * xf, axis=-1, keepdims=True) + NORM_EPS)
    return (y * g.astype(jnp.float32)).astype(x.dtype)

def split_cols(z, sizes):
    idx = [int(i) for i in np.cumsum(sizes)[:-1]]
    return jnp.split(z, idx, axis=-1)

def rope(x, pos):
    half = x.shape[-1] // 2
    freq = ROPE_THETA_2 ** (-jnp.arange(half, dtype=jnp.float32) / half)
    ang = pos.astype(jnp.float32)[:, None] * freq[None, :]
    cos = jnp.cos(ang)[:, None, :]
    sin = jnp.sin(ang)[:, None, :]
    xf = x.astype(jnp.float32)
    x1, x2 = xf[..., :half], xf[..., half:]
    return jnp.concatenate([x1 * cos - x2 * sin, x1 * sin + x2 * cos], axis=-1).astype(x.dtype)

def causal_depthwise_conv(x, w, b):
    y = lax.conv_general_dilated(
        x, w[:, None, :].astype(x.dtype), window_strides=(1,),
        padding=[(CONV_WIDTH - 1, 0)], dimension_numbers=("NWC", "WIO", "NWC"),
        feature_group_count=x.shape[-1])
    return y + b

def rg_lru(x, gx_w, gx_b, ga_w, ga_b, lru_lambda):
    B, S, _ = x.shape
    xb = x.reshape(B, S, LRU_BLOCKS, LRU_BLOCK_DIM)
    gate_i = jax.nn.sigmoid(jnp.einsum("bsnd,nde->bsne", xb, gx_w) + gx_b).reshape(B, S, LRU_WIDTH)
    gate_r = jax.nn.sigmoid(jnp.einsum("bsnd,nde->bsne", xb, ga_w) + ga_b).reshape(B, S, LRU_WIDTH)
    log_a = -LRU_C * jax.nn.softplus(-lru_lambda.astype(jnp.float32)) * gate_r.astype(jnp.float32)
    a = jnp.exp(log_a)
    mult = jnp.sqrt(-jnp.expm1(2.0 * log_a))
    u = mult * gate_i.astype(jnp.float32) * x.astype(jnp.float32)

    def combine(c1, c2):
        a1, b1 = c1
        a2, b2 = c2
        return a1 * a2, a2 * b1 + b2

    _, h = lax.associative_scan(combine, (a, u), axis=1)
    return h.astype(x.dtype)

def sliding_window_gqa_sinks(q, k, v, sinks):
    B, S = q.shape[:2]
    nb = S // BLOCK
    qb = q.reshape(B, nb, BLOCK, SWA_KV_HEADS, SWA_GROUP, SWA_HEAD_DIM)

    def band(t):
        tp = jnp.pad(t, ((0, 0), (BLOCK, 0), (0, 0), (0, 0)))
        cur = tp[:, BLOCK:].reshape(B, nb, BLOCK, SWA_KV_HEADS, SWA_HEAD_DIM)
        prev = tp[:, :S].reshape(B, nb, BLOCK, SWA_KV_HEADS, SWA_HEAD_DIM)
        return jnp.concatenate([prev, cur], axis=2)

    kb, vb = band(k), band(v)
    s = jnp.einsum("bnqhgd,bnkhd->bnhgqk", qb, kb).astype(jnp.float32) * (SWA_HEAD_DIM ** -0.5)
    n = jnp.arange(nb)[:, None, None]
    qi = jnp.arange(BLOCK)[None, :, None]
    ki = jnp.arange(2 * BLOCK)[None, None, :]
    rel = qi + BLOCK - ki
    kpos = n * BLOCK - BLOCK + ki
    mask = (rel >= 0) & (rel < WINDOW) & (kpos >= 0)
    s = jnp.where(mask[None, :, None, None], s, -jnp.inf)
    sink = sinks.astype(jnp.float32).reshape(1, 1, SWA_KV_HEADS, SWA_GROUP, 1, 1)
    m = jnp.maximum(jnp.max(s, axis=-1, keepdims=True), sink)
    p = jnp.exp(s - m)
    p = p / (jnp.sum(p, axis=-1, keepdims=True) + jnp.exp(sink - m))
    o = jnp.einsum("bnhgqk,bnkhd->bnqhgd", p.astype(vb.dtype), vb)
    return o.reshape(B, S, SWA_WIDTH)

def sweep_query_blocks(block_fn, q):
    B, S = q.shape[:2]
    nb = S // BLOCK
    qb = jnp.moveaxis(q.reshape((B, nb, BLOCK) + q.shape[2:]), 1, 0)

    def body(args):
        qblk, n = args
        return block_fn(qblk, n * BLOCK + jnp.arange(BLOCK))

    o = lax.map(body, (qb, jnp.arange(nb)))
    o = jnp.moveaxis(o, 0, 1)
    return o.reshape((B, S) + o.shape[3:])

def causal_mla_attention(q, k, v):
    S = k.shape[1]
    kpos = jnp.arange(S)
    scale = (MLA_NOPE + MLA_ROPE) ** -0.5

    def block_fn(qblk, qpos):
        s = jnp.einsum("bqhd,bkhd->bhqk", qblk, k).astype(jnp.float32) * scale
        s = jnp.where(kpos[None, :] <= qpos[:, None], s, -jnp.inf)
        p = jax.nn.softmax(s, axis=-1)
        return jnp.einsum("bhqk,bkhd->bqhd", p.astype(v.dtype), v)

    return sweep_query_blocks(block_fn, q)

def causal_diff_attention(q, k, v, lam):
    S = k.shape[1]
    kpos = jnp.arange(S)
    scale = DIFF_QK ** -0.5

    def block_fn(qblk, qpos):
        s = jnp.einsum("bqhcd,bkhcd->bchqk", qblk, k).astype(jnp.float32) * scale
        s = jnp.where(kpos[None, :] <= qpos[:, None], s, -jnp.inf)
        p = jax.nn.softmax(s, axis=-1)
        a = p[:, 0] - lam * p[:, 1]
        return jnp.einsum("bhqk,bkhd->bqhd", a.astype(v.dtype), v)

    return sweep_query_blocks(block_fn, q)

def even_layer(h, w_in, conv_w, conv_b, gx_w, gx_b, ga_w, ga_b, lru_lambda, sinks, w_out):
    B, S, _ = h.shape
    z = h @ w_in
    lru_x, lru_gate, q, k, v, swa_gate = split_cols(z, EVEN_SPLITS)
    lru_x = causal_depthwise_conv(lru_x, conv_w, conv_b)
    y_a = rg_lru(lru_x, gx_w, gx_b, ga_w, ga_b, lru_lambda) * jax.nn.silu(lru_gate)
    q = q.reshape(B, S, SWA_Q_HEADS, SWA_HEAD_DIM)
    k = k.reshape(B, S, SWA_KV_HEADS, SWA_HEAD_DIM)
    v = v.reshape(B, S, SWA_KV_HEADS, SWA_HEAD_DIM)
    y_b = sliding_window_gqa_sinks(q, k, v, sinks) * jax.nn.silu(swa_gate)
    return jnp.concatenate([y_a, y_b], axis=-1) @ w_out

def odd_layer(h, w_in, q_norm, w_uq, kv_norm, w_ukv, lambda_q1, lambda_k1, lambda_q2, lambda_k2,
              subln, w_out):
    B, S, _ = h.shape
    pos = jnp.arange(S)
    z = h @ w_in
    c_q, c_kv, k_rope, mla_gate, dq, dk, dv, diff_gate = split_cols(z, ODD_SPLITS)
    q = (rmsnorm_2(c_q, q_norm) @ w_uq).reshape(B, S, MLA_HEADS, MLA_NOPE + MLA_ROPE)
    q = jnp.concatenate([q[..., :MLA_NOPE], rope(q[..., MLA_NOPE:], pos)], axis=-1)
    kv = (rmsnorm_2(c_kv, kv_norm) @ w_ukv).reshape(B, S, MLA_HEADS, MLA_NOPE + MLA_V)
    k_nope, v_c = kv[..., :MLA_NOPE], kv[..., MLA_NOPE:]
    k_r = rope(k_rope.reshape(B, S, 1, MLA_ROPE), pos)
    k_c = jnp.concatenate([k_nope, jnp.broadcast_to(k_r, (B, S, MLA_HEADS, MLA_ROPE))], axis=-1)
    y_c = causal_mla_attention(q, k_c, v_c).reshape(B, S, MLA_WIDTH) * jax.nn.silu(mla_gate)
    qd = dq.reshape(B, S, DIFF_HEADS, 2, DIFF_QK)
    kd = dk.reshape(B, S, DIFF_HEADS, 2, DIFF_QK)
    vd = dv.reshape(B, S, DIFF_HEADS, DIFF_V)
    lam = (jnp.exp(jnp.sum(lambda_q1.astype(jnp.float32) * lambda_k1.astype(jnp.float32)))
           - jnp.exp(jnp.sum(lambda_q2.astype(jnp.float32) * lambda_k2.astype(jnp.float32)))
           + DIFF_LAMBDA_INIT)
    od = causal_diff_attention(qd, kd, vd, lam)
    od = rmsnorm_2(od, subln) * (1.0 - DIFF_LAMBDA_INIT)
    y_d = od.reshape(B, S, DIFF_WIDTH) * jax.nn.silu(diff_gate)
    return jnp.concatenate([y_c, y_d], axis=-1) @ w_out

def second_inputs(seed: int = 0) -> dict:
    key = jax.random.key(seed)
    ks = jax.random.split(key, 32)
    f32 = jnp.float32

    def dense(k, shape, fan_in):
        return jax.random.normal(k, shape, f32) * (fan_in ** -0.5)

    def gain(k, shape):
        return 1.0 + 0.05 * jax.random.normal(k, shape, f32)

    def small(k, shape, s=0.02):
        return s * jax.random.normal(k, shape, f32)

    u = jax.random.uniform(ks[10], (LRU_WIDTH,), f32, minval=0.9, maxval=0.999)
    a_base = u ** (1.0 / LRU_C)
    lru_lambda = jnp.log(a_base) - jnp.log1p(-a_base)

    return {
        "x": jax.random.normal(ks[0], (BATCH, SEQ, D_MODEL), f32),
        "norm_gains": gain(ks[1], (DEPTH_2, D_MODEL)),
        "final_norm_gain": gain(ks[2], (D_MODEL,)),
        "l0_w_in": dense(ks[3], (D_MODEL, EVEN_IN), D_MODEL),
        "l0_conv_w": dense(ks[4], (CONV_WIDTH, LRU_WIDTH), CONV_WIDTH),
        "l0_conv_b": small(ks[5], (LRU_WIDTH,)),
        "l0_gate_x_w": dense(ks[6], (LRU_BLOCKS, LRU_BLOCK_DIM, LRU_BLOCK_DIM), LRU_BLOCK_DIM),
        "l0_gate_x_b": small(ks[7], (LRU_BLOCKS, LRU_BLOCK_DIM)),
        "l0_gate_a_w": dense(ks[8], (LRU_BLOCKS, LRU_BLOCK_DIM, LRU_BLOCK_DIM), LRU_BLOCK_DIM),
        "l0_gate_a_b": small(ks[9], (LRU_BLOCKS, LRU_BLOCK_DIM)),
        "l0_lru_lambda": lru_lambda,
        "l0_sinks": 0.5 * jax.random.normal(ks[11], (SWA_Q_HEADS,), f32),
        "l0_w_out": dense(ks[12], (EVEN_MIX, D_MODEL), EVEN_MIX),
        "l1_w_in": dense(ks[13], (D_MODEL, ODD_IN), D_MODEL),
        "l1_q_norm": gain(ks[14], (MLA_Q_RANK,)),
        "l1_w_uq": dense(ks[15], (MLA_Q_RANK, MLA_HEADS * (MLA_NOPE + MLA_ROPE)), MLA_Q_RANK),
        "l1_kv_norm": gain(ks[16], (MLA_KV_RANK,)),
        "l1_w_ukv": dense(ks[17], (MLA_KV_RANK, MLA_HEADS * (MLA_NOPE + MLA_V)), MLA_KV_RANK),
        "l1_lambda_q1": small(ks[18], (DIFF_QK,), 0.1),
        "l1_lambda_k1": small(ks[19], (DIFF_QK,), 0.1),
        "l1_lambda_q2": small(ks[20], (DIFF_QK,), 0.1),
        "l1_lambda_k2": small(ks[21], (DIFF_QK,), 0.1),
        "l1_subln": gain(ks[22], (DIFF_V,)),
        "l1_w_out": dense(ks[23], (ODD_MIX, D_MODEL), ODD_MIX),
    }

def second_block(x, norm_gains, final_norm_gain,
              l0_w_in, l0_conv_w, l0_conv_b, l0_gate_x_w, l0_gate_x_b, l0_gate_a_w, l0_gate_a_b,
              l0_lru_lambda, l0_sinks, l0_w_out,
              l1_w_in, l1_q_norm, l1_w_uq, l1_kv_norm, l1_w_ukv,
              l1_lambda_q1, l1_lambda_k1, l1_lambda_q2, l1_lambda_k2, l1_subln, l1_w_out):
    even_params = (l0_w_in, l0_conv_w, l0_conv_b, l0_gate_x_w, l0_gate_x_b, l0_gate_a_w,
                   l0_gate_a_b, l0_lru_lambda, l0_sinks, l0_w_out)
    odd_params = (l1_w_in, l1_q_norm, l1_w_uq, l1_kv_norm, l1_w_ukv, l1_lambda_q1, l1_lambda_k1,
                  l1_lambda_q2, l1_lambda_k2, l1_subln, l1_w_out)
    for layer in range(DEPTH_2):
        h = rmsnorm_2(x, norm_gains[layer])
        if layer % 2 == 0:
            x = x + even_layer(h, *even_params)
        else:
            x = x + odd_layer(h, *odd_params)
    return rmsnorm_2(x, final_norm_gain)


def setup_inputs(seed=0):
    out = dict(first_inputs(seed))
    for name, value in second_inputs(seed + 1).items():
        if name != "x":
            out[name + "_2"] = value
    return out


def reference(
    x, c, w_ada, b_ada, norm1_g, w_in, q_norm_g, k_norm_g, w_pool, pool_scale, w_out, norm2_g,
    w_grp, w_exp, w1, w3, w2, norm_gains_2, final_norm_gain_2, l0_w_in_2, l0_conv_w_2,
    l0_conv_b_2, l0_gate_x_w_2, l0_gate_x_b_2, l0_gate_a_w_2, l0_gate_a_b_2, l0_lru_lambda_2,
    l0_sinks_2, l0_w_out_2, l1_w_in_2, l1_q_norm_2, l1_w_uq_2, l1_kv_norm_2, l1_w_ukv_2,
    l1_lambda_q1_2, l1_lambda_k1_2, l1_lambda_q2_2, l1_lambda_k2_2, l1_subln_2, l1_w_out_2,
):
    x = first_block(
        x, c, w_ada, b_ada, norm1_g, w_in, q_norm_g, k_norm_g, w_pool, pool_scale, w_out,
        norm2_g, w_grp, w_exp, w1, w3, w2,
    )
    return second_block(
        x, norm_gains_2, final_norm_gain_2, l0_w_in_2, l0_conv_w_2, l0_conv_b_2, l0_gate_x_w_2,
        l0_gate_x_b_2, l0_gate_a_w_2, l0_gate_a_b_2, l0_lru_lambda_2, l0_sinks_2, l0_w_out_2,
        l1_w_in_2, l1_q_norm_2, l1_w_uq_2, l1_kv_norm_2, l1_w_ukv_2, l1_lambda_q1_2,
        l1_lambda_k1_2, l1_lambda_q2_2, l1_lambda_k2_2, l1_subln_2, l1_w_out_2,
    )


_drawn_inputs = setup_inputs


def setup_inputs(seed=0):
    import zlib

    import numpy as np

    out = dict(_drawn_inputs(seed))
    spreads = {}
    factors = {'norm1_g': 5.511,
     'q_norm_g': 8.0,
     'k_norm_g': 8.0,
     'pool_scale': 5.719,
     'norm2_g': 3.677,
     'l0_gate_x_b_2': 64.0,
     'l0_gate_a_b_2': 64.0,
     'l0_sinks_2': 7.796,
     'l1_q_norm_2': 8.0,
     'l1_kv_norm_2': 8.0,
     'l1_lambda_q1_2': 21.667,
     'l1_lambda_q2_2': 17.362,
     'l1_subln_2': 36.375,
     'l0_conv_b_2': 3.555}
    for name, (base, spread) in spreads.items():
        noise = np.random.default_rng([zlib.crc32(name.encode()), seed]).standard_normal(out[name].shape)
        drawn = base * np.exp(spread * noise) if base else spread * noise
        out[name] = __import__('jax').numpy.asarray(drawn.astype(out[name].dtype))
    for name, factor in factors.items():
        out[name] = (out[name] * factor).astype(out[name].dtype)
    return out
```

```python
from contextlib import ExitStack

import numpy as np

import concourse.bass as bass
from concourse import mybir

ALU = mybir.AluOpType
ACT = mybir.ActivationFunctionType
AX = mybir.AxisListType
F32 = mybir.dt.float32
I32 = mybir.dt.int32

P = 128
D = 2048
S = 256
NT = S // P
KD = D // P
EPS = 1e-6
UNIT = 2048
RING = 8
SLOTS = 12
NEG = -1.0e38
TAKEN = -3.0e38
N_EXPERTS, N_GROUPS, PER_GROUP, DE = 32, 4, 8, 512
CAP = 32
MAX_TILES = 2 * S // CAP + N_EXPERTS - 1
LAMBDA_INIT = 0.8 - 0.6 * float(np.exp(-0.3))
LRU_C = 8.0
POOL_WINDOWS = (2, 4, 8, 16)

COLS = {}


def _cols():
    at = 0
    for name, n in (("c", 16), ("b_ada", 96), ("norm1_g", 16), ("q_norm_g", 1), ("k_norm_g", 1),
                    ("pool_scale", 8), ("norm2_g", 16), ("gain0", 16), ("gain1", 16), ("gain_f", 16),
                    ("conv_w", 32), ("conv_b", 8), ("gx_b", 8), ("ga_b", 8), ("lam", 8),
                    ("q_norm", 6), ("kv_norm", 4), ("subln", 1), ("sinks", 16), ("dl", 256)):
        COLS[name] = (at, n)
        at += n
    return at


NCOLS = _cols()

CONST = {}


def _const_cols():
    at = 0
    for name, n in (("ident", 128), ("tri", 128), ("rot1", 128), ("rot2", 128), ("rot3", 128),
                    ("cos1", 256), ("sin1", 256), ("cos2", 256), ("sin2", 256), ("cos3", 256),
                    ("sin3", 256), ("causal", 512), ("band", 256), ("icount", 64), ("slot", 128),
                    ("group", 4), ("rev", 8), ("tile", 48), ("cap", 8)):
        CONST[name] = (at, n)
        at += n
    return at


NCONST = _const_cols()


def constants():
    t = np.zeros((P, NCONST), np.float32)

    def put(name, a):
        lo, n = CONST[name]
        t[:, lo:lo + n] = np.asarray(a, np.float32).reshape(P, n)

    p = np.arange(P)
    put("ident", np.eye(P))
    put("tri", p[:, None] < p[None, :])
    pos = np.arange(S, dtype=np.float32)
    for n, (head, rd, theta) in enumerate(((128, 32, 500000.0), (64, 16, 500000.0), (64, 64, 10000.0))):
        half = rd // 2
        rot = np.zeros((P, P))
        cos, sin = np.ones((P, S)), np.zeros((P, S))
        j = np.arange(half, dtype=np.float32)
        if n < 2:
            inv = np.float32(theta) ** (-(j * np.float32(2.0)) / np.float32(rd))
        else:
            inv = np.float32(theta) ** (-j / np.float32(half))
        ang = (pos[None, :] * inv.astype(np.float32)[:, None]).astype(np.float32)
        for b in range(0, P, head):
            for q in range(half):
                rot[b + half + q, b + q] = -1.0
                rot[b + q, b + half + q] = 1.0
                for r in (b + q, b + half + q):
                    cos[r], sin[r] = np.cos(ang[q]), np.sin(ang[q])
        put(f"rot{n + 1}", rot)
        put(f"cos{n + 1}", cos)
        put(f"sin{n + 1}", sin)
    q = p[:, None, None] + P * np.arange(NT)[None, :, None]
    k = np.arange(S)[None, None, :]
    put("causal", np.where(k <= q, 0.0, NEG))
    put("band", np.where((k <= q) & (q - k < 128), 0.0, NEG)[:, 1])
    tok = np.arange(16)
    put("icount", np.broadcast_to(np.stack([1.0 / np.minimum(tok + 1, w) for w in POOL_WINDOWS])[None], (P, 4, 16)))
    put("slot", np.broadcast_to(np.tile(np.arange(CAP), P // CAP)[None], (P, P)))
    put("group", (p[:, None] // CAP) == np.arange(P // CAP)[None])
    put("rev", np.broadcast_to(np.arange(8, 0, -1)[None], (P, 8)))
    put("tile", np.broadcast_to(np.arange(48)[None], (P, 48)))
    put("cap", np.broadcast_to(CAP * np.arange(8)[None], (P, 8)))
    return t


class Order:

    def __init__(self):
        self.steps = {"pe": [], "act": [], "dve": []}
        self.at = {"pe": {}, "act": {}, "dve": {}}
        self.units = []
        self.unit_of = {}
        self.acc = []
        self.misc = []
        self.lagged = []

    def add(self, engine, *step):
        assert step not in self.at[engine], step
        self.steps[engine].append(step)
        self.at[engine][step] = len(self.steps[engine])

    def unit(self, key, floats, step):
        self.unit_of[key] = len(self.units)
        self.units.append((key, floats, step))

    def tick(self):
        now, self.lagged = self.lagged, []
        for n, what, x in now:
            if n > 1:
                self.lagged.append((n - 1, what, x))
            else:
                what(x)

    def drain(self):
        while self.lagged:
            self.tick()

    def proj(self, x, floats=UNIT, post=None, unit=None):
        if unit is None:
            self.unit(x, floats, ("proj", x))
        else:
            k = self.unit_of[unit]
            self.units[k] = (unit, self.units[k][1], ("proj", x))
        self.add("pe", "proj", x)
        self.acc.append(("proj", x))
        self.add("act", "evac", x)
        self.tick()
        if post == "nr":
            self.lagged.append((1, self.norm_head, x))
            self.lagged.append((2, self.rotate, x))
        if post == "r":
            self.lagged.append((1, self.rotate, x))
        if post == "res":
            self.add("dve", "res", x)
            self.add("act", "sq", x)
            self.lagged.append((2, self.sum_squares, x))

    def sum_squares(self, x):
        self.add("pe", "ss", x)

    def norm_head(self, x):
        self.add("pe", "nrm", x)
        self.misc.append(("nrm", x))
        self.add("dve", "nrm", x)
        self.add("act", "sqrt", x)
        self.add("dve", "qn", x)

    def rotate(self, x):
        self.add("pe", "rot", x)
        self.misc.append(("rot", x))
        self.add("dve", "rot", x)

    def scores(self, j):
        self.add("pe", "S", j)
        self.add("dve", "soft", j)
        self.add("act", "exp", j)
        self.add("dve", "scale", j)

    def turn(self, j):
        self.add("pe", "T", j)
        self.add("act", "pt", j)

    def values(self, j):
        self.add("pe", "O", j)
        self.add("dve", "out", j)


def order_a():
    o = Order()
    o.add("dve", "setup")
    o.add("act", "silu_c")
    o.add("dve", "spread_c")
    o.add("act", "sqx")
    o.add("pe", "ssx")
    o.misc.append(("ssx",))
    o.add("dve", "ssx")
    o.add("act", "sqrtx")
    o.add("dve", "xr")

    def ada(b):
        for q in range(4):
            o.unit(("ada", b, q), UNIT, ("ada", b))
        o.add("pe", "ada", b)
        o.acc.append(("ada", b))
        o.add("act", "evac", ("ada", b))

    def ada_t(b):
        o.add("pe", "adaT", b)
        o.misc.append(("adaT", b))
        o.add("dve", "adaT", b)

    for b in range(8):
        ada(b)
        if b:
            ada_t(b - 1)
    ada_t(7)
    o.add("dve", "h1")
    rest = [(("k", 0), UNIT, "nr"), (("k", 1), UNIT, "nr"), (("v", 0), UNIT, None), (("v", 1), UNIT, None),
            (("ki", 0), UNIT, "r"), (("wi", 0), 256, None)]
    rest += [(("qi", n), UNIT, "r") for n in range(8)] + [(("q", n), UNIT, "nr") for n in range(8)]
    b = 8
    idx = [(qt, c) for qt in range(2) for c in range(8)]
    for x, floats, post in rest:
        o.proj(x, floats, post)
        if x == ("wi", 0):
            o.add("dve", "wi")
        if b < 24:
            ada(b)
            if b > 8:
                ada_t(b - 1)
            b += 1
        if x[0] == "q":
            for _ in range(2):
                i = idx.pop(0)
                o.add("pe", "idx", i)
                o.acc.append(("idx", i))
                o.add("act", "evac", ("idx", i))
                o.add("dve", "idx", i)
    ada_t(23)
    o.add("dve", "cols")
    o.add("dve", "topk", 0)
    o.proj(("p", 0))
    o.proj(("p", 1))
    o.drain()
    o.scores(0)
    o.add("dve", "pool", 0)
    o.proj(("p", 2))
    o.turn(0)
    o.scores(1)
    o.proj(("p", 3))
    o.values(0)
    o.turn(1)
    o.add("dve", "topk", 1)
    o.add("dve", "pool", 1)
    o.proj(("p", 4))
    o.values(1)
    o.scores(2)
    o.proj(("p", 5))
    o.turn(2)
    o.scores(3)
    o.add("dve", "pool", 2)
    o.proj(("p", 6))
    o.values(2)
    o.turn(3)
    o.proj(("p", 7))
    o.values(3)
    o.add("dve", "pool", 3)
    for g in range(4):
        for dc in range(2):
            o.add("pe", "pmm", (g, dc))
            o.acc.append(("pmm", (g, dc)))
            o.add("act", "evac", ("pmm", (g, dc)))
    o.misc.append(("ssum", "wo"))
    for n in range(KD):
        o.proj(("wo", n), post="res")
    o.drain()
    o.add("dve", "ssum", "wo")
    o.add("act", "sqrtn", "wo")
    o.add("dve", "h", "wo")
    o.add("pe", "router")
    o.acc.append(("router",))
    o.add("act", "evac", ("router",))
    o.add("dve", "top1")
    o.add("act", "pexp")
    o.add("dve", "top2")
    o.add("pe", "cum")
    o.misc.append(("cum",))
    o.add("dve", "place")
    for tt in range(NT):
        for q in range(4):
            o.add("pe", "h2t", (tt, q))
            o.acc.append(("h2t", (tt, q)))
            o.add("act", "evac", ("h2t", (tt, q)))
    return o


def order_bc():
    o = Order()
    o.add("dve", "softplus0")
    o.add("act", "softplus1")
    o.add("dve", "softplus2")
    o.add("act", "lambda")
    o.add("dve", "lambda")
    o.misc.append(("ssum", "moe"))
    for n in range(KD):
        o.add("dve", "res", ("moe", n))
        o.add("act", "sq", ("moe", n))
        o.add("pe", "ss", ("moe", n))
    o.add("dve", "ssum", "moe")
    o.add("act", "sqrtn", "moe")
    o.add("dve", "h", "moe")
    for n in range(2):
        o.proj(("bk", n))
    for n in range(2):
        o.proj(("bv", n))
    for n in range(8):
        o.proj(("bq", n))
    jobs = [("b", g, hh, qt) for g in range(2) for hh in range(2) for qt in range(2)]
    rest = [("bs", n) for n in range(8)] + [("lx", n) for n in range(8)] + [("lg", n) for n in range(8)]
    stages = []
    for i in range(len(jobs) + 2):
        if i >= 2:
            stages.append((o.values, jobs[i - 2]))
        if 1 <= i <= len(jobs):
            stages.append((o.turn, jobs[i - 1]))
        if i < len(jobs):
            stages.append((o.scores, jobs[i]))
    ready = []

    def lru_gates(n):
        o.add("pe", "lgate", n)
        o.acc.append(("lgate", n))
        o.add("act", "evac", ("lgate", n))
        o.add("dve", "lruA", n)
        o.add("act", "lruB", n)
        o.add("dve", "lruC", n)
        o.add("act", "lruD", n)
        o.add("dve", "lruE", n)

    for k, x in enumerate(rest):
        o.proj(x)
        if k >= 2:
            for _ in range(2):
                if stages:
                    what, j = stages.pop(0)
                    what(j)
        if x[0] == "lx":
            o.add("dve", "conv", x[1])
        if x[0] == "lg":
            lru_gates(x[1])
    while stages:
        what, j = stages.pop(0)
        what(j)
    o.misc.append(("ssum", "wb"))
    for n in range(KD):
        o.proj(("wb", n), post="res")
    o.drain()
    o.add("dve", "ssum", "wb")
    o.add("act", "sqrtn", "wb")
    o.add("dve", "h", "wb")
    o.misc.append(("ssum", "cq"))
    for n in range(6):
        o.proj(("cq", n))
        o.lagged.append((1, o.sum_squares, ("cq", n)))
    o.drain()
    o.add("dve", "ssum", "cq")
    o.add("act", "sqrtn", "cq")
    o.misc.append(("ssum", "ckv"))
    for n in range(4):
        o.proj(("ckv", n))
        o.lagged.append((1, o.sum_squares, ("ckv", n)))
        if n == 0:
            o.add("dve", "cqn")
    o.drain()
    o.add("dve", "ssum", "ckv")
    o.add("act", "sqrtn", "ckv")
    o.add("dve", "ckvn")
    o.proj(("kr", 0), post="r")
    for n in range(8):
        o.proj(("dk", n))
    for n in range(8):
        o.proj(("dq", n))
    for n in range(8):
        o.proj(("dv", n))
    djobs = [("d", p, qt) for p in range(4) for qt in range(2)]
    stages = []

    def dkz(p):
        o.add("dve", "dkz", p)

    def dnorm(p):
        o.add("act", "dsq", p)
        o.add("pe", "dn", p)
        o.misc.append(("dn", p))
        o.add("dve", "dn", p)
        o.add("act", "dsqrt", p)
        o.add("dve", "dfin", p)

    for i in range(len(djobs) + 2):
        if i >= 2:
            stages.append((o.values, djobs[i - 2]))
            if djobs[i - 2][2] == 1:
                stages.append((dnorm, djobs[i - 2][1]))
        if 1 <= i <= len(djobs):
            stages.append((o.turn, djobs[i - 1]))
        if i < len(djobs):
            if djobs[i][2] == 0:
                stages.append((dkz, djobs[i][1]))
            stages.append((o.scores, djobs[i]))

    def some(n):
        for _ in range(n):
            if stages:
                what, j = stages.pop(0)
                what(j)

    for n in range(8):
        o.proj(("dg", n))
        some(2)
    for n in range(8):
        o.proj(("mg", n))
        some(2)
    some(len(stages))
    mjobs = [("m", hg, qt) for hg in range(2) for qt in range(2)]

    def q_up(u):
        o.unit(("uq", u), 2 * 6 * P, None)
        for c in (2 * u, 2 * u + 1):
            o.proj(("qn", c) if c < 8 else ("qr", c - 8), post=None if c < 8 else "r", unit=("uq", u))

    def kv_up(u):
        o.unit(("ukv", u), UNIT, None)
        for c in (2 * u, 2 * u + 1):
            o.proj(("kn", c), unit=("ukv", u))
        for c in (2 * u, 2 * u + 1):
            o.proj(("vm", c), unit=("ukv", u))

    for u in (4, 5, 0, 1):
        q_up(u)
    for u in (0, 1):
        kv_up(u)
    o.drain()
    o.scores(mjobs[0])
    q_up(2)
    o.turn(mjobs[0])
    o.scores(mjobs[1])
    q_up(3)
    o.values(mjobs[0])
    o.turn(mjobs[1])
    kv_up(2)
    o.values(mjobs[1])
    kv_up(3)
    o.scores(mjobs[2])
    o.scores(mjobs[3])
    o.turn(mjobs[2])
    o.values(mjobs[2])
    o.turn(mjobs[3])
    o.values(mjobs[3])
    o.misc.append(("ssum", "wc"))
    for n in range(KD):
        o.proj(("wc", n), post="res")
    o.drain()
    o.add("dve", "ssum", "wc")
    o.add("act", "sqrtn", "wc")
    o.add("dve", "h", "wc")
    return o


A = order_a()
BC = order_bc()


def program(nc, t):
    with ExitStack() as ctx:
        def sb(name, shape, dt=F32):
            return ctx.enter_context(nc.sbuf_tensor(name, shape, dt))

        def sem(name):
            return ctx.enter_context(nc.semaphore(name))

        ring = sb("ring", [P, SLOTS, UNIT])
        X = sb("X", [P, KD, S])
        H = sb("H", [P, KD, S])
        low = sb("low", [P, 48, S])
        cst = sb("cst", [P, NCONST])
        col = sb("col", [P, NCOLS])
        SB = sb("SB", [P, 2, 4, S])
        PTS = sb("PTS", [P, NT, 4, P])
        ones = sb("ones", [P, P])
        ada = sb("ada", [P, 96])
        small = sb("small", [P, 256])
        sti = sb("sti", [P, 64], I32)

        high = ring[:, RING:SLOTS, :].rearrange("p a (b s) -> p (a b) s", s=S)

        def W(a, n=1):
            if a >= 48:
                return high[:, a - 48:a - 48 + n, :]
            assert a + n <= 48
            return low[:, a:a + n, :]

        def K(name, lo=0, n=None):
            at, size = CONST[name]
            return cst[:, at + lo:at + lo + (size - lo if n is None else n)]

        def C(name, lo=0, n=None):
            at, size = COLS[name]
            return col[:, at + lo:at + lo + (size - lo if n is None else n)]

        acc = [ctx.enter_context(nc.psum_tensor(f"acc{i}", [P, 512], F32)) for i in range(2)]
        psS = ctx.enter_context(nc.psum_tensor("psS", [P, 4, S], F32))
        psT = ctx.enter_context(nc.psum_tensor("psT", [P, NT, 4, P], F32))
        psO = ctx.enter_context(nc.psum_tensor("psO", [P, 4, P], F32))
        psM = ctx.enter_context(nc.psum_tensor("psM", [P, 512], F32))
        bankS = [psS[:, 0:2, :].rearrange("p a b -> p (a b)"), psS[:, 2:4, :].rearrange("p a b -> p (a b)")]
        bankT = [psT[:, n, :, :].rearrange("p a b -> p (a b)") for n in range(2)]
        bankO = psO[:, :, :].rearrange("p a b -> p (a b)")

        table_in = sem("table_in")
        aux_in = sem("aux_in")
        unit_in = [[sem(f"unit_in{k}_{i}") for i in range(RING)] for k in range(2)]
        done = [{e: sem(f"{e}_done{k}") for e in ("pe", "act", "dve")} for k in range(2)]
        act_link, dve_link = sem("act_link"), sem("dve_link")
        tile_in = [sem(f"tile_in{i}") for i in range(SLOTS)]
        moe = {n: sem(n) for n in ("pick_ready", "g_full", "g_copied", "gt_full", "xg_ready", "w_used",
                                   "h_copied", "ht_full", "hs_ready", "silu_done", "at_ready", "oe_ready",
                                   "sct_full", "sct_copied", "scj_ready", "scw_ready", "y_full", "y_added",
                                   "j_ready", "pick_half", "weigh_half", "h3_ready")}
        out_done = sem("out_done")

        MIX = 0
        aQ, aK, aV, aQI, aKI, aAD, aKR, aWR, aRT, aT2 = 16, 24, 26, 28, 36, 38, 42, 43, 46, 47
        aPR, aPS, aSC, aWK, aMB, aRL, aSQ, aPW, aTM = 28, 48, 52, 54, 56, 58, 62, 64, 72
        mYT, mH2, mGS, mXG, mHS, mOE, mST, mSJ, mSW = 0, 16, 32, 34, 36, 40, 42, 43, 47
        bK, bV, bQ, bLX, bGW, bY, bGI, bGR, bLA, bTH, bHH = 16, 20, 22, 30, 38, 48, 56, 58, 60, 62, 64
        cQN, cKN, cVM, cQR, cKR, cCQ, cCKV, cDZ, cOR, cDS = 16, 24, 32, 40, 44, 48, 54, 58, 62, 66
        cDQ, cDK, cDV = 16, 24, 32
        dTM, dSQ, dRT, dT2, dKX = 68, 70, 72, 73, 74
        V_a = W(aV, 2).rearrange("p k (g d) -> p k g d", d=P)
        V_b = W(bV, 2).rearrange("p k (g d) -> p k g d", d=P)
        V_c = W(cVM, 8).rearrange("p a s -> p (a s)").rearrange("p (k h d) -> p k h d", k=NT, d=P)
        PW = W(aPW, 8).rearrange("p a s -> p (a s)").rearrange("p (g k d) -> p g k d", g=4, k=2)
        GW = W(bGW, 8).rearrange("p a s -> p (a s)").rearrange("p (w n d) -> p w n d", w=2, n=8)
        WR = W(aWR, 3).rearrange("p a s -> p (a s)")[:, 0:KD * 36].rearrange("p (k n) -> p k n", n=36)
        AD = W(aAD, 4).rearrange("p (b a) s -> p b (a s)", b=2)
        cB = SB[:, 0, 0:2, :].rearrange("p a s -> p (a s)").rearrange("p (k m) -> p k m", m=CAP)
        S1, S2 = 0, 1

        cs, g1, g2, sub = small[:, 0:16], small[:, 16:32], small[:, 32:48], small[:, 48:49]
        lamn, wi, top = small[:, 49:50], small[:, 64:96], small[:, 96:112]
        lam2 = small[:, 50:56]
        jst = small[:, 112:144].rearrange("p (b k h) -> p b k h", b=2, k=4)
        cL, tsp = small[:, 144:152], small[:, 152:192]
        wis = small[:, 208:240]
        pos_w = small[:, 192:200]
        sh1, sc1, gt1, sh2, sc2, gt2 = (ada[:, 16 * n:16 * n + 16] for n in range(6))

        scr = SB[:, :, :, :].rearrange("p a b s -> p (a b s)")
        SG = scr[:, 0:64].rearrange("p (t c) -> p t c", t=NT)
        SG2 = scr[:, 64:128].rearrange("p (t c) -> p t c", t=NT)
        J = scr[:, 128:256]
        SWA_ = scr[:, 256:512].rearrange("p (t c) -> p t c", t=NT)
        H1T = scr[:, 512:640].rearrange("p (c m) -> p c m", m=CAP)
        H3T = scr[:, 640:768].rearrange("p (c m) -> p c m", m=CAP)
        AT = scr[:, 768:896].rearrange("p (c m) -> p c m", m=CAP)
        SL1 = scr[:, 896:1024].rearrange("p (c m) -> p c m", m=CAP)

        ident = K("ident")

        def jobs_of(o):
            return [s[1] for s in o.steps["pe"] if s[0] == "S"]

        def keys_of(j):
            return P * ((j[-1] if isinstance(j, tuple) else j // 2) + 1)

        def qt_of(j):
            return j[-1] if isinstance(j, tuple) else j // 2

        def rot_of(x):
            return {"k": "rot1", "q": "rot1", "ki": "rot2", "qi": "rot2"}.get(x[0], "rot3")

        def rot_chunk(x):
            at = {"k": aK, "q": aQ, "ki": aKR, "qi": aQI, "kr": dKX, "qr": cQR}[x[0]]
            return W(at + x[1])[:, 0, :]

        def pooled(g):
            return W(aPR + 2 * g, 2)

        rt = W(48, 14).rearrange("p a s -> p (a s)")
        LG = rt[:, 0:72].rearrange("p (t n) -> p t n", t=NT)
        gd, gk, goh = (rt[:, 80 + 8 * n:88 + 8 * n].rearrange("p (t n) -> p t n", t=NT) for n in range(3))
        r1 = rt[:, 112:144].rearrange("p (k t) -> p k t", t=NT)
        els, els2, ek, oh1, oh2 = (rt[:, 160 + 16 * n:176 + 16 * n].rearrange("p (t n) -> p t n", t=NT) for n in range(5))
        sel = rt[:, 256:320].rearrange("p (t g e) -> p t g e", t=NT, g=4)
        A12 = rt[:, 320:448].rearrange("p (k t g e) -> p k t g e", k=2, t=NT, g=4)
        MM = rt[:, 448:512].rearrange("p (t n) -> p t n", t=NT)
        cumS = rt[:, 512:608]
        nt, incl, excl, zero32 = (rt[:, 608 + 32 * n:640 + 32 * n] for n in range(4))
        cmp8 = rt[:, 768:1024].rearrange("p (e c) -> p e c", c=8)
        slotp = rt[:, 1024:1088].rearrange("p (t n) -> p t n", t=NT)
        tmp2 = rt[:, 1088:1216].rearrange("p (k t n) -> p k t n", k=2, t=NT)
        eid = rt[:, 1216:1280]
        cmp48 = rt[:, 1536:3072].rearrange("p (i e) -> p i e", e=32)

        def M_of(tt):
            return MM[:, tt, :]

        block = ctx.enter_context(nc.Block())

        @block.sync
        def _(sp):
            sp.dma_start(cst[:, :], t["const"]).then_inc(table_in, 16)
            sp.dma_start(col[:, :], t["cols"]).then_inc(table_in, 16)
            sp.dma_start(X[:, :, :], t["xT"]).then_inc(table_in, 16)

            def stream(k, o, src):
                for u, (key, floats, step) in enumerate(o.units):
                    if u >= RING:
                        sp.wait_ge(done[k]["pe"], o.at["pe"][o.units[u - RING][2]])
                    sp.dma_start(ring[:, u % RING, 0:floats], src[u, :, 0:floats]).then_inc(unit_in[k][u % RING], 16)
                    if k == 0 and u == RING - 1:
                        sp.dma_start(PW.rearrange("p g k d -> p (g k d)"), t["w_pool"]).then_inc(aux_in, 16)
                        sp.dma_start(WR.rearrange("p k n -> p (k n)"), t["w_route"]).then_inc(aux_in, 16)

            stream(0, A, t["stream_a"])
            sp.wait_ge(done[0]["dve"], A.at["dve"][("place",)])
            sp.wait_ge(done[0]["act"], len(A.steps["act"]))
            sp.wait_ge(done[0]["pe"], len(A.steps["pe"]))
            tiles = sp.value_load(sti[0:1, 48:49], min_val=1, max_val=MAX_TILES)

            def load_tile(i, first):
                e = sp.value_load(sti[0:1, 0:1] if first else sti[0:1, bass.ds(i, 1)], min_val=0, max_val=N_EXPERTS - 1)
                for s in range(SLOTS):
                    if not first:
                        sp.wait_ge(moe["w_used"], i * SLOTS + (s + 1 - SLOTS))
                    src = (t["w1"], t["w3"], t["w2"])[s // 4]
                    sp.dma_start(ring[:, s, :],
                                 src[bass.ds(e, 1), s % 4, :, :].rearrange("e p n -> (e p) n")).then_inc(tile_in[s], 16)

            load_tile(0, True)
            with sp.Fori(1, tiles) as i:
                load_tile(i, False)
            sp.wait_ge(moe["y_added"], tiles * 8 + 10)
            sp.dma_start(GW.rearrange("p w n d -> p (w n d)"), t["w_gates"]).then_inc(aux_in, 16)
            stream(1, BC, t["stream_bc"])
            sp.wait_ge(done[1]["dve"], BC.at["dve"][("h", "wc")])
            sp.dma_start(t["out"], H[:, :, :]).then_inc(out_done, 16)
            sp.wait_ge(out_done, 16)

        @block.tensor
        def _(pe):
            def needs(k, engine, o, *step):
                pe.wait_ge(done[k][engine], o.at[engine][step])

            def unit(k, o, key):
                u = o.unit_of[key]
                pe.wait_ge(unit_in[k][u % RING], 16 * (u // RING + 1))
                return ring[:, u % RING, :]

            def attention(k, o, kind, j, jobs):
                n = jobs.index(j)
                qt, nk = qt_of(j), keys_of(j)
                q = slice(P * qt, P * qt + P)
                if kind == "S":
                    if n:
                        needs(k, "dve", o, "soft", jobs[n - 1])
                    if k == 0:
                        g = j % 2
                        for h in range(4):
                            mm = pe.matmul(psS[:, h, 0:nk], W(aQ + 4 * g + h)[:, 0, q], W(aK + g)[:, 0, 0:nk],
                                           start=True, stop=True)
                    elif j[0] == "b":
                        _, g, hh, _ = j
                        for c in range(2):
                            mm = pe.matmul(psS[:, 2 * c:2 * c + 2, 0:nk], W(bQ + 4 * g + 2 * hh + c)[:, 0, q],
                                           W(bK + 2 * g, 2)[:, :, 0:nk], start=True, stop=True)
                    elif j[0] == "d":
                        needs(k, "dve", o, "dkz", j[1])
                        for c in range(2):
                            mm = pe.matmul(psS[:, 2 * c:2 * c + 2, 0:nk], W(cDQ + 2 * j[1] + c)[:, 0, q],
                                           W(cDZ + 2 * c, 2)[:, :, 0:nk], start=True, stop=True)
                    else:
                        for c in range(4):
                            h = 4 * j[1] + c
                            pe.matmul(psS[:, c, 0:nk], W(cQN + h)[:, 0, q], W(cKN + h)[:, 0, 0:nk],
                                      start=True, stop=False)
                            mm = pe.matmul(psS[:, c, 0:nk], W(cQR + h // 2)[:, 0, q],
                                           W(cKR + h % 2)[:, 0, 0:nk], start=False, stop=True)
                if kind == "T":
                    needs(k, "dve", o, "scale", j)
                    if n:
                        needs(k, "act", o, "pt", jobs[n - 1])
                    heads = 2 if k and j[0] == "d" else 4
                    for kt in range(qt + 1):
                        for h in range(heads):
                            src = 2 * h if heads == 2 else h
                            mm = pe.transpose(psT[:, kt, h, :], SB[:, n % 2, src, P * kt:P * kt + P], ident)
                if kind == "O":
                    needs(k, "act", o, "pt", j)
                    if n:
                        needs(k, "dve", o, "out", jobs[n - 1])
                    if k == 0 or j[0] == "b":
                        v = V_a[:, :, j % 2, :] if k == 0 else V_b[:, :, j[1], :]
                        for kt in range(qt + 1):
                            mm = pe.matmul(psO[:, :, :], v[:, kt, :], PTS[:, kt, :, :], start=(kt == 0), stop=(kt == qt))
                    else:
                        heads = 2 if j[0] == "d" else 4
                        for h in range(heads):
                            for kt in range(qt + 1):
                                mm = pe.matmul(psO[:, h, :], V_c[:, kt, heads * j[1] + h, :], PTS[:, kt, h, :],
                                               start=(kt == 0), stop=(kt == qt))
                mm.then_inc(done[k]["pe"], 1)

            def product(k, o, x, bank):
                name, n = x
                src, nk, base = H, KD, None
                if name in ("wo", "wb", "wc"):
                    base, nk = MIX, KD
                elif name in ("qn", "qr"):
                    base, nk = cCQ, 6
                elif name in ("kn", "vm"):
                    base, nk = cCKV, 4
                if name in ("qn", "qr"):
                    c = n if name == "qn" else 8 + n
                    slot = unit(k, o, ("uq", c // 2))[:, 6 * P * (c % 2):6 * P * (c % 2 + 1)]
                elif name in ("kn", "vm"):
                    c = n % 2 if name == "kn" else 2 + n % 2
                    slot = unit(k, o, ("ukv", n // 2))[:, 4 * P * c:4 * P * (c + 1)]
                else:
                    slot = unit(k, o, x)[:, 0:256 if name == "wi" else UNIT]
                w = slot.rearrange("p (k m) -> p k m", k=nk)

                def rows(c):
                    return H[:, c, :] if base is None else W(base + c)[:, 0, :]

                if name in ("v", "wi", "bv", "dv", "vm"):
                    m = w.shape[2]
                    for tt in range(NT):
                        for c in range(nk):
                            mm = pe.matmul(bank[:, m * tt:m * tt + m], rows(c)[:, P * tt:P * tt + P], w[:, c, :],
                                           start=(c == 0), stop=(c == nk - 1))
                else:
                    for c in range(nk):
                        mm = pe.matmul(bank[:, 0:S], w[:, c, :], rows(c), start=(c == 0), stop=(c == nk - 1))
                mm.then_inc(done[k]["pe"], 1)

            READ = {"ssx": "ssx", "adaT": "adaT", "nrm": "nrm", "rot": "rot", "cum": "place", "ssum": "ssum", "dn": "dn"}
            FIRST_SS = {("wo", 0): "wo", ("moe", 0): "moe", ("wb", 0): "wb", ("cq", 0): "cq", ("ckv", 0): "ckv",
                        ("wc", 0): "wc"}
            LAST = {"cq": 5, "ckv": 3}

            def run(k, o):
                jobs = jobs_of(o)
                nr = [s[1] for s in o.steps["pe"] if s[0] == "nrm"]

                def bank_of(step):
                    n = o.acc.index(step)
                    if n >= 2:
                        needs(k, "act", o, "evac", o.acc[n - 2][1] if o.acc[n - 2][0] == "proj" else o.acc[n - 2])
                    return acc[n % 2]

                def misc_free(item):
                    n = o.misc.index(item)
                    if n:
                        prev = o.misc[n - 1]
                        needs(k, "dve", o, READ[prev[0]], *prev[1:])

                for step in o.steps["pe"]:
                    what = step[0]
                    if what in ("S", "T", "O"):
                        attention(k, o, what, step[1], jobs)
                        continue
                    if what == "proj":
                        x = step[1]
                        if x in (("k", 0),):
                            needs(k, "dve", o, "h1")
                        if x == ("wo", 0):
                            needs(k, "dve", o, "out", 3)
                            needs(k, "act", o, "evac", ("pmm", (3, 1)))
                        if x == ("bk", 0):
                            needs(k, "dve", o, "h", "moe")
                        if x == ("wb", 0):
                            needs(k, "dve", o, "out", jobs[7])
                            needs(k, "dve", o, "lruE", 7)
                        if x == ("cq", 0):
                            needs(k, "dve", o, "h", "wb")
                        if x == ("qr", 0):
                            needs(k, "dve", o, "cqn")
                        if x == ("kn", 0):
                            needs(k, "dve", o, "ckvn")
                        if x == ("wc", 0):
                            needs(k, "dve", o, "out", jobs[-1])
                            needs(k, "dve", o, "dfin", 3)
                        product(k, o, x, bank_of(step))
                        continue
                    if what == "ada":
                        if step[1] == 0:
                            needs(k, "dve", o, "spread_c")
                        bank = bank_of(step)
                        for q in range(4):
                            w = unit(k, o, ("ada", step[1], q)).rearrange("p (c n) -> p c n", c=4)
                            for c in range(4):
                                mm = pe.matmul(bank[CAP * c:CAP * c + CAP, :], cB[:, 4 * q + c, :], w[:, c, :],
                                               start=(q == 0), stop=(q == 3), tile_position=(0, CAP * c))
                    elif what == "adaT":
                        needs(k, "act", o, "evac", ("ada", step[1]))
                        misc_free(step)
                        for c in range(4):
                            mm = pe.transpose(psM[:, P * c:P * c + P], AD[:, step[1] % 2, P * c:P * c + P], ident)
                    elif what == "ssx":
                        needs(k, "dve", o, "setup")
                        needs(k, "act", o, "sqx")
                        for c in range(KD):
                            mm = pe.matmul(psM[:, 0:S], ones[:, :], H[:, c, :], start=(c == 0), stop=(c == KD - 1))
                    elif what == "ss":
                        x = step[1]
                        if x in FIRST_SS:
                            misc_free(("ssum", x[0]))
                        needs(k, "act", o, "evac" if x[0] in ("cq", "ckv") else "sq", x)
                        sq = aSQ if k == 0 else dSQ
                        mm = pe.matmul(psM[:, 0:S], ones[:, :], W(sq + x[1] % 2)[:, 0, :], start=(x[1] == 0),
                                       stop=(x[1] == LAST.get(x[0], KD - 1)))
                    elif what == "nrm":
                        x = step[1]
                        misc_free(step)
                        needs(k, "act", o, "evac", x)
                        mm = pe.matmul(psM[:, 0:S], ones[:, :], W(aSQ + nr.index(x) % 2)[:, 0, :], start=True, stop=True)
                    elif what == "rot":
                        x = step[1]
                        misc_free(step)
                        if x[0] in ("k", "q"):
                            needs(k, "dve", o, "qn", x)
                        else:
                            needs(k, "act", o, "evac", x)
                        mm = pe.matmul(psM[:, 0:S], K(rot_of(x)), rot_chunk(x), start=True, stop=True)
                    elif what == "idx":
                        qt, c = step[1]
                        if c == 0 and qt == 0:
                            needs(k, "dve", o, "rot", ("qi", 7))
                        bank = bank_of(step)
                        nk = P * (qt + 1)
                        mm = pe.matmul(bank[:, 0:2 * nk].rearrange("p (a s) -> p a s", a=2),
                                       W(aQI + c)[:, 0, P * qt:P * qt + P], W(aKI, 2)[:, :, 0:nk], start=True, stop=True)
                    elif what == "pmm":
                        g, dc = step[1]
                        needs(k, "dve", o, "pool", g)
                        if (g, dc) == (0, 0):
                            pe.wait_ge(aux_in, 32)
                        bank = bank_of(step)
                        for c in range(2):
                            mm = pe.matmul(bank[:, 0:S], PW[:, g, c, P * dc:P * dc + P], pooled(g)[:, c, :],
                                           start=(c == 0), stop=(c == 1))
                    elif what == "router":
                        needs(k, "dve", o, "h", "wo")
                        bank = bank_of(step)
                        for tt in range(NT):
                            for c in range(KD):
                                mm = pe.matmul(bank[:, 36 * tt:36 * tt + 36], H[:, c, P * tt:P * tt + P], WR[:, c, :],
                                               start=(c == 0), stop=(c == KD - 1))
                    elif what == "cum":
                        misc_free(step)
                        needs(k, "dve", o, "top2")
                        tri = K("tri")
                        pe.matmul(psM[:, 0:32], tri, M_of(0), start=True, stop=True)
                        pe.matmul(psM[:, 32:64], ones[:, :], M_of(0), start=True, stop=False)
                        pe.matmul(psM[:, 32:64], tri, M_of(1), start=False, stop=True)
                        pe.matmul(psM[:, 64:96], ones[:, :], M_of(0), start=True, stop=False)
                        mm = pe.matmul(psM[:, 64:96], ones[:, :], M_of(1), start=False, stop=True)
                    elif what == "h2t":
                        tt, q = step[1]
                        bank = bank_of(step)
                        for c in range(4):
                            mm = pe.transpose(bank[:, P * c:P * c + P], H[:, 4 * q + c, P * tt:P * tt + P], ident)
                    elif what == "lgate":
                        n = step[1]
                        if n == 0:
                            pe.wait_ge(aux_in, 48)
                        needs(k, "dve", o, "conv", n)
                        bank = bank_of(step)
                        for g in range(2):
                            mm = pe.matmul(bank[:, S * g:S * g + S], GW[:, g, n, :], W(bY + n)[:, 0, :],
                                           start=True, stop=True)
                    elif what == "dn":
                        p = step[1]
                        misc_free(step)
                        needs(k, "act", o, "dsq", p)
                        mm = pe.matmul(psM[:, :], ones[:, :], W(cDS, 2)[:, :, :], start=True, stop=True)
                    else:
                        raise AssertionError(step)
                    mm.then_inc(done[k]["pe"], 1)

            pe.wait_ge(table_in, 48)
            run(0, A)

            needs(0, "dve", A, "place")
            needs(0, "act", A, "evac", ("h2t", (1, 3)))
            tiles = pe.value_load(sti[0:1, 48:49], min_val=1, max_val=MAX_TILES)
            bG, bGT, bH, bHT, bW2, bY2 = acc[0][:, :], acc[1][:, :], bankS, bankT, bankO, psM[:, :]
            ybank = [bY2, bGT]
            GS = W(mGS, 2).rearrange("p a s -> p (a s)")
            XG = W(mXG, 2).rearrange("p a s -> p (a s)").rearrange("p (c n m) -> p c n m", c=4, m=CAP)
            HS = W(mHS, 4).rearrange("p (b a) s -> p b (a s)", b=2)
            OE = W(mOE, 2).rearrange("p a s -> p (a s)")
            SJ = W(mSJ, 4)
            SW = W(mSW).rearrange("p a s -> p (a s)").rearrange("p (t c) -> p t c", t=NT)
            H2 = W(mH2, 16).rearrange("p a s -> p (a s)").rearrange("p (t d) -> p t d", t=NT)

            def gather(i):
                pe.wait_ge(moe["pick_ready"], i + 1)
                for tt in range(NT):
                    for n in range(4):
                        mm = pe.matmul(bG[CAP * n:CAP * n + CAP, :], SG[:, tt, :], H2[:, tt, 512 * n:512 * n + 512],
                                       start=(tt == 0), stop=(tt == NT - 1), tile_position=(0, CAP * n))
                mm.then_inc(moe["g_full"], 1)

            def gather_t(i):
                pe.wait_ge(moe["g_copied"], i + 1)
                for c in range(4):
                    mm = pe.transpose(bGT[:, P * c:P * c + P], GS[:, P * c:P * c + P], ident)
                mm.then_inc(moe["gt_full"], 1)

            def spread(i):
                pe.wait_ge(moe["scw_ready"], i + 1)
                for tt in range(NT):
                    mm = pe.transpose(bG[:, P * tt:P * tt + P], SW[:, tt, :], ident)
                mm.then_inc(moe["sct_full"], 1)

            def scatter(i):
                pe.wait_ge(moe["oe_ready"], i + 1)
                pe.wait_ge(moe["scj_ready"], i + 1)
                for m in range(8):
                    c, half = m // 2, m % 2
                    pe.wait_ge(moe["y_added"], i * 8 + m + 1)
                    pe.matmul(ybank[m % 2], OE[:, P * c:P * c + P], SJ[:, 2 * half:2 * half + 2, :],
                              start=True, stop=True).then_inc(moe["y_full"], 1)

            gather(0)
            gather_t(0)
            with pe.Fori(0, tiles) as i:
                pe.wait_ge(moe["xg_ready"], i + 1)
                pe.wait_ge(moe["h_copied"], i * 2 + 1)
                for s in range(8):
                    pe.wait_ge(tile_in[s], i * 16 + 16)
                    for c in range(4):
                        k = 4 * (s % 4) + c
                        mm = pe.matmul(bH[s // 4][CAP * c:CAP * c + CAP, :], XG[:, k % 4, k // 4, :],
                                       ring[:, s, 512 * c:512 * c + 512], start=(s % 4 == 0), stop=(s % 4 == 3),
                                       tile_position=(0, CAP * c))
                    mm.then_inc(moe["w_used"], 1)
                pe.wait_ge(moe["sct_copied"], i + 1)
                gather(i + 1)
                pe.wait_ge(moe["h_copied"], i * 2 + 3)
                pe.wait_ge(moe["at_ready"], i + 1)
                for b in range(2):
                    for c in range(4):
                        mm = pe.transpose(bHT[b][:, P * c:P * c + P], HS[:, b, P * c:P * c + P], ident)
                mm.then_inc(moe["ht_full"], 1)
                scatter(i)
                pe.wait_ge(moe["at_ready"], i + 2)
                for s in range(8, 12):
                    pe.wait_ge(tile_in[s], i * 16 + 16)
                    for c in range(4):
                        mm = pe.matmul(bW2[CAP * c:CAP * c + CAP, :], AT[:, s - 8, :], ring[:, s, 512 * c:512 * c + 512],
                                       start=(s == 8), stop=(s == 11), tile_position=(0, CAP * c))
                    mm.then_inc(moe["w_used"], 1)
                pe.wait_ge(moe["y_added"], i * 8 + 10)
                gather_t(i + 1)
                spread(i)
            scatter(tiles)
            run(1, BC)

        @block.scalar
        def _(act):
            link = [0]

            def then(ins):
                link[0] += 1
                ins.then_inc(act_link, 1)
                act.wait_ge(act_link, link[0])

            def run(k, o):
                jobs = jobs_of(o)
                count = 0
                nr = [s[1] for s in o.steps["pe"] if s[0] == "nrm"]
                idx = [s[1] for s in o.steps["pe"] if s[0] == "idx"]

                def needs(engine, *step):
                    act.wait_ge(done[k][engine], o.at[engine][step])

                def evac(x):
                    item = ("proj", x) if ("proj", x) in o.at["pe"] else x
                    bank = acc[o.acc.index(item) % 2]
                    needs("pe", *item)
                    name, n = x if len(x) > 1 else (x[0], 0)
                    a = bank[:, 0:S]
                    if name == "ada":
                        if n >= 2:
                            needs("pe", "adaT", n - 2)
                        return act.activation(AD[:, n % 2, :], bank[:, :], ACT.Copy)
                    if name in ("k", "q"):
                        i = nr.index(x)
                        if i >= 2:
                            needs("pe", "nrm", nr[i - 2])
                        act.activation(rot_chunk(x), a, ACT.Copy)
                        return act.activation(W(aSQ + i % 2)[:, 0, :], a, ACT.Square)
                    if name in ("qi", "ki", "qr"):
                        return act.activation(rot_chunk(x), a, ACT.Copy)
                    if name == "kr":
                        return act.activation(rot_chunk(x), a, ACT.Copy)
                    if name in ("v", "bv", "dv", "vm"):
                        v = {"v": V_a, "bv": V_b}.get(name, V_c)
                        return act.activation(v[:, :, n, :], a.rearrange("p (k d) -> p k d", k=NT), ACT.Copy)
                    if name == "wi":
                        return act.activation(wi, bank[:, 0:32], ACT.Copy)
                    if name == "idx":
                        qt, c = n
                        i = idx.index(n)
                        if i >= 2:
                            needs("dve", "idx", idx[i - 2])
                        nk = P * (qt + 1)
                        return act.activation(W(aRL + 2 * (i % 2), 2)[:, :, 0:nk],
                                              bank[:, 0:2 * nk].rearrange("p (a s) -> p a s", a=2), ACT.Relu)
                    if name == "p":
                        needs("pe", "idx", idx[-1])
                        return act.activation(W(aPR + n)[:, 0, :], a, ACT.Copy)
                    if name == "pmm":
                        c = 2 * n[0] + n[1]
                        return act.activation(W(MIX + 8 + c)[:, 0, :], a, ACT.Copy, scale=C("pool_scale", c, 1))
                    if name in ("wo", "wb", "wc"):
                        if n >= 2:
                            needs("dve", "res", (name, n - 2))
                        tm = W((aTM if k == 0 else dTM) + n % 2)[:, 0, :]
                        if name == "wo":
                            return act.activation(tm, a, ACT.Copy, scale=gt1[:, n:n + 1])
                        return act.activation(tm, a, ACT.Copy)
                    if name == "router":
                        return act.activation(rt[:, 0:72], bank[:, 0:72], ACT.Copy)
                    if name == "h2t":
                        tt, q = n
                        H2 = W(mH2, 16).rearrange("p a s -> p (a s)").rearrange("p (t d) -> p t d", t=NT)
                        return act.activation(H2[:, tt, 512 * q:512 * q + 512], bank[:, :], ACT.Copy)
                    if name == "bk":
                        z = W(bK + 2 * n, 2)
                        act.activation(z[0:64, 0, :], bank[0:64, 0:S], ACT.Copy)
                        return act.activation(z[64:128, 1, :], bank[64:128, 0:S], ACT.Copy)
                    if name == "bq":
                        return act.activation(W(bQ + n)[:, 0, :], a, ACT.Copy)
                    if name == "lx":
                        return act.activation(W(bLX + n)[:, 0, :], a, ACT.Copy)
                    if name == "lg":
                        return act.activation(W(MIX + n)[:, 0, :], a, ACT.Silu)
                    if name in ("bs", "dg"):
                        if name == "dg" and n == 0:
                            needs("pe", "proj", ("wb", KD - 1))
                        return act.activation(W(MIX + 8 + n)[:, 0, :], a, ACT.Silu)
                    if name == "mg":
                        return act.activation(W(MIX + n)[:, 0, :], a, ACT.Silu)
                    if name == "lgate":
                        if n >= 2:
                            needs("dve", "lruE", n - 2)
                        act.activation(W(bGI + n % 2)[:, 0, :], a, ACT.Sigmoid, bias=C("gx_b", n, 1))
                        return act.activation(W(bGR + n % 2)[:, 0, :], bank[:, S:2 * S], ACT.Sigmoid, bias=C("ga_b", n, 1))
                    if name in ("cq", "ckv"):
                        if n >= 2:
                            needs("pe", "ss", (name, n - 2))
                        act.activation(W((cCQ if name == "cq" else cCKV) + n)[:, 0, :], a, ACT.Copy)
                        return act.activation(W(dSQ + n % 2)[:, 0, :], a, ACT.Square)
                    if name in ("dk", "dq"):
                        return act.activation(W((cDK if name == "dk" else cDQ) + n)[:, 0, :], a, ACT.Copy)
                    if name in ("qn", "kn"):
                        return act.activation(W((cQN if name == "qn" else cKN) + n)[:, 0, :], a, ACT.Copy)
                    raise AssertionError(x)

                for step in o.steps["act"]:
                    what = step[0]
                    if count:
                        act.wait_ge(done[k]["act"], count)
                    if what == "evac":
                        ins = evac(step[1])
                    elif what == "silu_c":
                        ins = act.activation(cs, C("c"), ACT.Silu)
                    elif what == "sqx":
                        ins = act.activation(H[:, :, :], X[:, :, :], ACT.Square)
                    elif what == "sqrtx":
                        needs("dve", "ssx")
                        ins = act.activation(W(aRT)[:, 0, :], W(aRT)[:, 0, :], ACT.Sqrt)
                    elif what == "sqrt":
                        needs("dve", "nrm", step[1])
                        ins = act.activation(W(aRT)[:, 0, :], W(aRT)[:, 0, :], ACT.Sqrt)
                    elif what == "sqrtn":
                        needs("dve", "ssum", step[1])
                        r = W(aRT if k == 0 else dRT)[:, 0, :]
                        ins = act.activation(r, r, ACT.Sqrt)
                    elif what == "sq":
                        x = step[1]
                        n = x[1]
                        needs("dve", "res", x)
                        if n >= 2:
                            needs("pe", "ss", (x[0], n - 2))
                        sq = aSQ if k == 0 else dSQ
                        ins = act.activation(W(sq + n % 2)[:, 0, :], X[:, n, :], ACT.Square)
                    elif what == "exp":
                        j = step[1]
                        n, nk = jobs.index(j), keys_of(j)
                        needs("dve", "soft", j)
                        st = jst[:, n % 2, :, :]
                        for h in range(4):
                            s = SB[:, n % 2, h, 0:nk]
                            ins = act.activation(s, s, ACT.Exp, bias=st[:, 1, h:h + 1], accum_out=st[:, 2, h:h + 1])
                        if k and j[0] == "b":
                            ins = act.activation(st[:, 3, :], st[:, 3, :], ACT.Exp)
                    elif what == "pt":
                        j = step[1]
                        n = jobs.index(j)
                        needs("pe", "T", j)
                        if n:
                            needs("pe", "O", jobs[n - 1])
                        heads = 2 if k and j[0] == "d" else 4
                        qt = qt_of(j)
                        ins = act.activation(PTS[:, 0:qt + 1, 0:heads, :], psT[:, 0:qt + 1, 0:heads, :], ACT.Copy)
                    elif what == "pexp":
                        needs("dve", "top1")
                        act.activation(gk, gd, ACT.Exp)
                        ins = act.activation(r1[:, 5, :], r1[:, 4, :], ACT.Exp)
                    elif what == "softplus1":
                        needs("dve", "softplus0")
                        ins = act.activation(tsp[:, 8:16], tsp[:, 0:8], ACT.Exp)
                    elif what == "lambda":
                        needs("dve", "softplus2")
                        ins = act.activation(lam2[:, 2:4], lam2[:, 0:2], ACT.Exp)
                    elif what == "lruB":
                        n = step[1]
                        needs("dve", "lruA", n)
                        act.activation(W(bLA + n % 2)[:, 0, :], W(bGR + n % 2)[:, 0, :], ACT.Exp, scale=-1.0)
                        ins = act.activation(W(bTH + n % 2)[:, 0, :], W(bGR + n % 2)[:, 0, :], ACT.Tanh)
                    elif what == "lruD":
                        n = step[1]
                        needs("dve", "lruC", n)
                        ins = act.activation(W(bTH + n % 2)[:, 0, :], W(bTH + n % 2)[:, 0, :], ACT.Sqrt)
                    elif what == "dsq":
                        p = step[1]
                        needs("dve", "out", ("d", p, 1))
                        if p:
                            needs("pe", "dn", p - 1)
                        ins = act.activation(W(cDS, 2), W(cOR + 2 * (p % 2), 2), ACT.Square)
                    elif what == "dsqrt":
                        needs("dve", "dn", step[1])
                        ins = act.activation(W(cDS, 2), W(cDS, 2), ACT.Sqrt)
                    else:
                        raise AssertionError(step)
                    ins.then_inc(done[k]["act"], 1)
                    count += 1

            act.wait_ge(table_in, 48)
            run(0, A)
            act.wait_ge(done[0]["act"], len(A.steps["act"]))
            act.wait_ge(done[0]["dve"], A.at["dve"][("place",)])
            tiles = act.value_load(sti[0:1, 48:49], min_val=1, max_val=MAX_TILES)
            GS = W(mGS, 2).rearrange("p a s -> p (a s)")
            XG = W(mXG, 2).rearrange("p a s -> p (a s)")
            HS = W(mHS, 4).rearrange("p (b a) s -> p b (a s)", b=2)
            OE = W(mOE, 2).rearrange("p a s -> p (a s)")
            ST = W(mST).rearrange("p a s -> p (a s)")

            def copy_gather(i, first=False):
                act.wait_ge(moe["g_full"], i + 1)
                if not first:
                    act.wait_ge(moe["gt_full"], i)
                act.activation(GS, acc[0][:, :], ACT.Copy).then_inc(moe["g_copied"], 1)

            def copy_inputs(i):
                act.wait_ge(moe["gt_full"], i + 1)
                act.activation(XG, acc[1][:, :], ACT.Copy).then_inc(moe["xg_ready"], 1)

            copy_gather(0, True)
            copy_inputs(0)
            with act.Fori(0, tiles) as i:
                for b in range(2):
                    act.wait_ge(moe["w_used"], i * 12 + 4 * (b + 1))
                    if b == 0:
                        act.wait_ge(moe["ht_full"], i + 1)
                    act.activation(HS[:, b, :], bankS[b], ACT.Copy).then_inc(moe["h_copied"], 1)
                copy_gather(i + 1)
                act.wait_ge(moe["hs_ready"], i + 1)
                act.activation(SL1, H1T, ACT.Silu).then_inc(moe["silu_done"], 1)
                act.wait_ge(moe["w_used"], i * 12 + 12)
                act.wait_ge(moe["y_full"], i * 8 + 8)
                act.activation(OE, bankO, ACT.Copy).then_inc(moe["oe_ready"], 1)
                copy_inputs(i + 1)
                act.wait_ge(moe["sct_full"], i + 1)
                act.wait_ge(moe["scj_ready"], i + 1)
                act.activation(ST, acc[0][:, 0:S], ACT.Copy).then_inc(moe["sct_copied"], 1)
            act.wait_ge(moe["y_added"], tiles * 8 + 10)
            run(1, BC)

        @block.vector
        def _(dve):
            link = [0]

            def then(ins):
                link[0] += 1
                ins.then_inc(dve_link, 1)
                dve.wait_ge(dve_link, link[0])

            def shifted_add(out, a, d):
                dve.tensor_copy(out[:, :, 0:d], a[:, :, 0:d])
                then(dve.tensor_tensor(out[:, :, d:S], a[:, :, d:S], a[:, :, 0:S - d], ALU.add))

            def first_max(x, m, key, one, n, lead):
                then(dve.tensor_tensor(key, x, m[:, :, None].to_broadcast([P, NT, n]), ALU.is_equal))
                then(dve.tensor_tensor(key, key, lead[:, None, :].to_broadcast([P, NT, n]), ALU.mult))
                then(dve.tensor_reduce(r1[:, 7, :], key, AX.X, ALU.max))
                then(dve.tensor_tensor(one, key, r1[:, 7, :][:, :, None].to_broadcast([P, NT, n]), ALU.is_equal))

            def run(k, o):
                jobs = jobs_of(o)
                count = 0
                idx = [s[1] for s in o.steps["pe"] if s[0] == "idx"]
                RT = W(aRT if k == 0 else dRT)[:, 0, :]
                T2 = W(aT2 if k == 0 else dT2)[:, 0, :]

                def needs(engine, *step):
                    dve.wait_ge(done[k][engine], o.at[engine][step])

                def softmax_head(j):
                    n, nk, qt = jobs.index(j), keys_of(j), qt_of(j)
                    st = jst[:, n % 2, :, :]
                    s = SB[:, n % 2, :, 0:nk]
                    needs("pe", "S", j)
                    if n >= 2:
                        needs("pe", "T", jobs[n - 2])
                    if k == 0:
                        scale, mask = P ** -0.5, W(aMB + qt)[:, 0, 0:nk]
                    elif j[0] == "b":
                        scale, mask = 64 ** -0.5, K("band") if qt else K("causal", 0, nk)
                    elif j[0] == "d":
                        scale, mask = 64 ** -0.5, K("causal", S * qt, nk)
                    else:
                        scale, mask = 192 ** -0.5, K("causal", S * qt, nk)
                    then(dve.scalar_tensor_tensor(out=s, in0=psS[:, :, 0:nk], scalar=scale,
                                                  in1=mask[:, None, :].to_broadcast([P, 4, nk]),
                                                  op0=ALU.mult, op1=ALU.add))
                    then(dve.tensor_reduce(st[:, 0, :], s, AX.X, ALU.max))
                    if k and j[0] == "b":
                        sink = C("sinks", 8 * j[1] + 4 * j[2], 4)
                        then(dve.tensor_tensor(st[:, 0, :], st[:, 0, :], sink, ALU.max))
                        dve.tensor_tensor(st[:, 3, :], sink, st[:, 0, :], ALU.subtract)
                    return dve.tensor_scalar(st[:, 1, :], st[:, 0, :], -1.0, None, ALU.mult)

                def softmax_tail(j):
                    n, nk = jobs.index(j), keys_of(j)
                    st = jst[:, n % 2, :, :]
                    needs("act", "exp", j)
                    if k and j[0] == "b":
                        then(dve.tensor_tensor(st[:, 2, :], st[:, 2, :], st[:, 3, :], ALU.add))
                    then(dve.reciprocal(st[:, 0, :], st[:, 2, :]))
                    if k and j[0] == "d":
                        then(dve.tensor_tensor(st[:, 1, :], st[:, 0, :], lamn.to_broadcast([P, 4]), ALU.mult))
                        for h in range(2):
                            a, b = SB[:, n % 2, 2 * h, 0:nk], SB[:, n % 2, 2 * h + 1, 0:nk]
                            ins = dve.tensor_scalar(a, a, st[:, 0, 2 * h:2 * h + 1], None, ALU.mult)
                        then(ins)
                        for h in range(2):
                            a, b = SB[:, n % 2, 2 * h, 0:nk], SB[:, n % 2, 2 * h + 1, 0:nk]
                            ins = dve.scalar_tensor_tensor(out=a, in0=b, scalar=st[:, 1, 2 * h + 1:2 * h + 2], in1=a,
                                                           op0=ALU.mult, op1=ALU.add)
                        return ins
                    for h in range(4):
                        a = SB[:, n % 2, h, 0:nk]
                        ins = dve.tensor_scalar(a, a, st[:, 0, h:h + 1], None, ALU.mult)
                    return ins

                def attention_out(j):
                    n, qt = jobs.index(j), qt_of(j)
                    q = slice(P * qt, P * qt + P)
                    needs("pe", "O", j)
                    if k == 0:
                        return dve.tensor_copy(W(MIX + 4 * (j % 2), 4)[:, :, q], psO[:, :, :])
                    if j[0] == "b":
                        for half in range(2):
                            r = slice(64 * half, 64 * half + 64)
                            mix = W(MIX + 8 + 4 * j[1] + 2 * j[2], 2)[r, :, q]
                            ins = dve.tensor_tensor(mix, psO[r, half:4:2, :], mix, ALU.mult)
                        return ins
                    if j[0] == "d":
                        return dve.tensor_copy(W(cOR + 2 * (j[1] % 2), 2)[:, :, q], psO[:, 0:2, :])
                    mix = W(MIX + 4 * j[1], 4)[:, :, q]
                    return dve.tensor_tensor(mix, psO[:, :, :], mix, ALU.mult)

                def rms(n, width):
                    return dve.tensor_scalar(RT, psM[:, 0:S], 1.0 / width, EPS, ALU.mult, ALU.add)

                for step in o.steps["dve"]:
                    what = step[0]
                    if count:
                        dve.wait_ge(done[k]["dve"], count)
                    if what == "setup":
                        dve.memset(ones[:, :], 1.0)
                        dve.memset(W(aKI, 2), 0.0)
                        ins = dve.memset(W(aSC, 2), 0.0)
                    elif what == "spread_c":
                        needs("act", "silu_c")
                        ins = dve.tensor_copy(cB, cs[:, :, None].to_broadcast([P, KD, CAP]))
                    elif what == "ssx":
                        needs("pe", "ssx")
                        ins = rms(0, D)
                    elif what == "xr":
                        needs("act", "sqrtx")
                        then(dve.reciprocal(RT, RT))
                        ins = dve.tensor_tensor(H[:, :, :], X[:, :, :], RT[:, None, :].to_broadcast([P, KD, S]), ALU.mult)
                    elif what == "adaT":
                        b = step[1]
                        needs("pe", "adaT", b)
                        a = ada[:, 4 * b:4 * b + 4]
                        then(dve.tensor_reduce(a, psM[:, :].rearrange("p (c r m) -> p c r m", c=4, m=CAP)[:, :, :, 0],
                                               AX.X, ALU.add))
                        ins = dve.tensor_tensor(a, a, C("b_ada", 4 * b, 4), ALU.add)
                    elif what == "h1":
                        then(dve.scalar_tensor_tensor(out=g1, in0=sc1, scalar=1.0, in1=C("norm1_g"), op0=ALU.add, op1=ALU.mult))
                        for c in range(KD):
                            ins = dve.tensor_scalar(H[:, c, :], H[:, c, :], g1[:, c:c + 1], sh1[:, c:c + 1], ALU.mult, ALU.add)
                    elif what == "cols":
                        ins = dve.scalar_tensor_tensor(out=g2, in0=sc2, scalar=1.0, in1=C("norm2_g"), op0=ALU.add, op1=ALU.mult)
                    elif what == "wi":
                        needs("act", "evac", ("wi", 0))
                        ins = dve.tensor_scalar(wis, wi, (64 ** -0.5) * (16 ** -0.5), None, ALU.mult)
                    elif what == "nrm":
                        needs("pe", "nrm", step[1])
                        ins = rms(0, P)
                    elif what == "qn":
                        x = step[1]
                        needs("act", "sqrt", x)
                        then(dve.reciprocal(RT, RT))
                        g = C("k_norm_g" if x[0] == "k" else "q_norm_g")
                        z = rot_chunk(x)
                        ins = dve.scalar_tensor_tensor(out=z, in0=z, scalar=g, in1=RT, op0=ALU.mult, op1=ALU.mult)
                    elif what == "rot":
                        x = step[1]
                        r = rot_of(x)[-1]
                        z = rot_chunk(x)
                        needs("pe", "rot", x)
                        dve.tensor_tensor(T2, psM[:, 0:S], K("sin" + r), ALU.mult)
                        then(dve.tensor_tensor(z, z, K("cos" + r), ALU.mult))
                        if x[0] in ("ki", "kr"):
                            kz = W(aKI if x[0] == "ki" else cKR, 2)
                            dve.tensor_tensor(kz[0:64, 0, :], z[0:64, :], T2[0:64, :], ALU.add)
                            ins = dve.tensor_tensor(kz[64:128, 1, :], z[64:128, :], T2[64:128, :], ALU.add)
                        else:
                            ins = dve.tensor_tensor(z, z, T2, ALU.add)
                    elif what == "idx":
                        qt, c = step[1]
                        needs("act", "evac", ("idx", step[1]))
                        nk = P * (qt + 1)
                        sc = W(aSC + qt)[:, 0, 0:nk]
                        for h in range(2):
                            at = 16 * qt + 2 * c + h
                            ins = dve.scalar_tensor_tensor(out=sc, in0=W(aRL + 2 * (idx.index(step[1]) % 2) + h)[:, 0, 0:nk],
                                                           scalar=wis[:, at:at + 1], in1=sc, op0=ALU.mult, op1=ALU.add)
                            if h == 0:
                                then(ins)
                    elif what == "topk":
                        qt = step[1]
                        nk = P * (qt + 1)
                        wk, causal = W(aWK + qt)[:, 0, 0:nk], K("causal", S * qt, nk)
                        then(dve.tensor_tensor(wk, W(aSC + qt)[:, 0, 0:nk], causal, ALU.add))
                        for r in range(8):
                            m8 = top[:, 8 * (r % 2):8 * (r % 2) + 8]
                            then(dve.max(m8, wk))
                            then(dve.match_replace(wk, m8, wk, TAKEN))
                        mb = W(aMB + qt)[:, 0, 0:nk]
                        then(dve.tensor_scalar(mb, wk, 2 * NEG, NEG, ALU.is_gt, ALU.mult))
                        ins = dve.tensor_tensor(mb, mb, causal, ALU.add)
                    elif what == "pool":
                        g = step[1]
                        win = POOL_WINDOWS[g]
                        p = W(aPR + 2 * g, 2)
                        needs("act", "evac", ("p", 2 * g + 1))
                        a, b = W(aPS, 2), W(aPS + 2, 2)
                        shifted_add(a, p, 1)
                        d = 2
                        while d < win:
                            shifted_add(b, a, d)
                            a, b = b, a
                            d *= 2
                        dve.tensor_tensor(b[:, :, 0:16], a[:, :, 0:16],
                                          K("icount", 16 * g, 16)[:, None, :].to_broadcast([P, 2, 16]), ALU.mult)
                        then(dve.tensor_scalar(b[:, :, 16:S], a[:, :, 16:S], 1.0 / win, None, ALU.mult))
                        ins = dve.tensor_tensor(p, b, p, ALU.subtract)
                    elif what == "soft":
                        ins = softmax_head(step[1])
                    elif what == "scale":
                        ins = softmax_tail(step[1])
                    elif what == "out":
                        ins = attention_out(step[1])
                    elif what == "res":
                        name, n = step[1]
                        if name == "moe":
                            ins = dve.scalar_tensor_tensor(out=X[:, n, :], in0=W(mYT + n)[:, 0, :], scalar=gt2[:, n:n + 1],
                                                           in1=X[:, n, :], op0=ALU.mult, op1=ALU.add)
                        else:
                            needs("act", "evac", step[1])
                            tm = W((aTM if k == 0 else dTM) + n % 2)[:, 0, :]
                            ins = dve.tensor_tensor(X[:, n, :], X[:, n, :], tm, ALU.add)
                    elif what == "ssum":
                        name = step[1]
                        width = {"cq": 768, "ckv": 512}.get(name, D)
                        needs("pe", "ss", (name, width // P - 1))
                        ins = rms(0, width)
                    elif what in ("h", "cqn", "ckvn"):
                        name = step[1] if what == "h" else what[:-1]
                        if name == "wb":
                            dve.memset(W(cDZ, 4), 0.0)
                            dve.memset(W(cKR, 2), 0.0)
                        needs("act", "sqrtn", name)
                        then(dve.reciprocal(RT, RT))
                        if what == "h":
                            g = {"wo": g2, "moe": C("gain0"), "wb": C("gain1"), "wc": C("gain_f")}[name]
                            for c in range(KD):
                                ins = dve.scalar_tensor_tensor(out=H[:, c, :], in0=X[:, c, :], scalar=g[:, c:c + 1],
                                                               in1=RT, op0=ALU.mult, op1=ALU.mult)
                            if name == "wo":
                                then(ins)
                                for c in range(KD):
                                    ins = dve.tensor_scalar(H[:, c, :], H[:, c, :], sh2[:, c:c + 1], None, ALU.add)
                        else:
                            g, at, n = (C("q_norm"), cCQ, 6) if name == "cq" else (C("kv_norm"), cCKV, 4)
                            for c in range(n):
                                z = W(at + c)[:, 0, :]
                                ins = dve.scalar_tensor_tensor(out=z, in0=z, scalar=g[:, c:c + 1], in1=RT,
                                                               op0=ALU.mult, op1=ALU.mult)
                    elif what == "top1":
                        needs("act", "evac", ("router",))
                        gl = LG[:, :, 0:4]
                        then(dve.tensor_reduce(r1[:, 0, :], gl, AX.X, ALU.max))
                        dve.tensor_tensor(gd, gl, r1[:, 0, :][:, :, None].to_broadcast([P, NT, 4]), ALU.subtract)
                        first_max(gl, r1[:, 0, :], gk, goh, 4, K("rev", 4, 4))
                        for g in range(4):
                            ins = dve.tensor_tensor(sel[:, :, g, :], LG[:, :, 4 + 8 * g:12 + 8 * g],
                                                    goh[:, :, g:g + 1].to_broadcast([P, NT, 8]), ALU.mult)
                        then(ins)
                        then(dve.tensor_tensor(els, sel[:, :, 0, :], sel[:, :, 1, :], ALU.add))
                        then(dve.tensor_tensor(els, els, sel[:, :, 2, :], ALU.add))
                        then(dve.tensor_tensor(els, els, sel[:, :, 3, :], ALU.add))
                        then(dve.tensor_reduce(r1[:, 1, :], els, AX.X, ALU.max))
                        first_max(els, r1[:, 1, :], ek, oh1, 8, K("rev"))
                        then(dve.scalar_tensor_tensor(out=els2, in0=oh1, scalar=TAKEN, in1=els, op0=ALU.mult, op1=ALU.add))
                        then(dve.tensor_reduce(r1[:, 2, :], els2, AX.X, ALU.max))
                        first_max(els2, r1[:, 2, :], ek, oh2, 8, K("rev"))
                        ins = dve.tensor_tensor(r1[:, 4, :], r1[:, 2, :], r1[:, 1, :], ALU.subtract)
                    elif what == "top2":
                        needs("act", "pexp")
                        then(dve.tensor_reduce(r1[:, 3, :], gk, AX.X, ALU.add))
                        then(dve.tensor_scalar(r1[:, 6, :], r1[:, 5, :], 1.0, None, ALU.add))
                        then(dve.tensor_tensor(r1[:, 6, :], r1[:, 6, :], r1[:, 3, :], ALU.mult))
                        then(dve.reciprocal(pos_w[:, 4:6], r1[:, 6, :]))
                        dve.tensor_tensor(pos_w[:, 6:8], pos_w[:, 4:6], r1[:, 5, :], ALU.mult)
                        for kk, one in enumerate((oh1, oh2)):
                            for g in range(4):
                                ins = dve.tensor_tensor(A12[:, kk, :, g, :], one, goh[:, :, g:g + 1].to_broadcast([P, NT, 8]),
                                                        ALU.mult)
                        then(ins)
                        ins = dve.tensor_tensor(MM.rearrange("p t n -> p (t n)"),
                                                A12[:, 0].rearrange("p t g e -> p (t g e)"),
                                                A12[:, 1].rearrange("p t g e -> p (t g e)"), ALU.add)
                    elif what == "place":
                        needs("pe", "cum")
                        dve.memset(zero32, 0.0)
                        then(dve.tensor_copy(cumS, psM[:, 0:96]))
                        cnt = cumS[:, 64:96]
                        then(dve.tensor_tensor(cmp8, cnt[:, :, None].to_broadcast([P, 32, 8]),
                                               K("cap")[:, None, :].to_broadcast([P, 32, 8]), ALU.is_gt))
                        then(dve.tensor_reduce(nt, cmp8, AX.X, ALU.add))
                        then(dve.tensor_tensor_scan(incl, nt, zero32, 0.0, ALU.add, ALU.add))
                        then(dve.tensor_tensor(excl, incl, nt, ALU.subtract))
                        for tt in range(NT):
                            ins = dve.scalar_tensor_tensor(out=slotp[:, tt, :], in0=excl, scalar=float(CAP),
                                                           in1=cumS[:, 32 * tt:32 * tt + 32], op0=ALU.mult, op1=ALU.add)
                        then(ins)
                        for kk in range(2):
                            ins = dve.tensor_tensor(tmp2[:, kk].rearrange("p t n -> p (t n)"),
                                                    A12[:, kk].rearrange("p t g e -> p (t g e)"),
                                                    slotp.rearrange("p t n -> p (t n)"), ALU.mult)
                        then(ins)
                        for kk in range(2):
                            dve.tensor_reduce(pos_w[:, 2 * kk:2 * kk + 2], tmp2[:, kk], AX.X, ALU.add)
                        then(dve.tensor_tensor(cmp48, incl[:, None, :].to_broadcast([P, 48, 32]),
                                               K("tile")[:, :, None].to_broadcast([P, 48, 32]), ALU.is_le))
                        dve.tensor_copy(eid[:, 48:49], incl[:, 31:32])
                        then(dve.tensor_reduce(eid[:, 0:48], cmp48, AX.X, ALU.add))
                        ins = dve.tensor_copy(sti[:, 0:49], eid[:, 0:49])
                    elif what == "softplus0":
                        dve.memset(W(bK, 4), 0.0)
                        then(dve.tensor_scalar(tsp[:, 16:24], C("lam"), -1.0, None, ALU.mult))
                        then(dve.tensor_tensor(tsp[:, 24:32], tsp[:, 16:24], C("lam"), ALU.max))
                        ins = dve.tensor_scalar(tsp[:, 0:8], tsp[:, 24:32], -1.0, None, ALU.mult)
                    elif what == "softplus2":
                        needs("act", "softplus1")
                        e, y, y2, pl = tsp[:, 8:16], tsp[:, 24:32], tsp[:, 32:40], tsp[:, 0:8]
                        then(dve.tensor_scalar(y2, e, 2.0, None, ALU.add))
                        then(dve.reciprocal(y2, y2))
                        then(dve.tensor_tensor(y, e, y2, ALU.mult))
                        then(dve.tensor_tensor(y2, y, y, ALU.mult))
                        then(dve.memset(pl, 1.0 / 17))
                        for m in (15, 13, 11, 9, 7, 5, 3, 1):
                            then(dve.tensor_tensor(pl, pl, y2, ALU.mult))
                            then(dve.tensor_scalar(pl, pl, 1.0 / m, None, ALU.add))
                        then(dve.tensor_tensor(pl, pl, y, ALU.mult))
                        then(dve.tensor_scalar(tsp[:, 16:24], tsp[:, 16:24], 0.0, None, ALU.max))
                        then(dve.scalar_tensor_tensor(out=cL, in0=pl, scalar=2.0, in1=tsp[:, 16:24], op0=ALU.mult, op1=ALU.add))
                        dl = C("dl").rearrange("p (a b d) -> p a b d", a=2, b=2)
                        prod = W(bY)[:, 0, 0:128].rearrange("p (a d) -> p a d", a=2)
                        dve.tensor_scalar(cL, cL, LRU_C, None, ALU.mult)
                        then(dve.tensor_tensor(prod, dl[:, :, 0, :], dl[:, :, 1, :], ALU.mult))
                        ins = dve.tensor_reduce(lam2[:, 0:2], prod, AX.X, ALU.add)
                    elif what == "lambda":
                        needs("act", "lambda")
                        dve.tensor_scalar(sub, C("subln"), 1.0 - LAMBDA_INIT, None, ALU.mult)
                        then(dve.tensor_tensor(lamn, lam2[:, 3:4], lam2[:, 2:3], ALU.subtract))
                        ins = dve.tensor_scalar(lamn, lamn, -LAMBDA_INIT, None, ALU.add)
                    elif what == "conv":
                        n = step[1]
                        needs("act", "evac", ("lx", n))
                        x, y = W(bLX + n)[:, 0, :], W(bY + n)[:, 0, :]
                        cw = C("conv_w", 4 * n, 4)
                        then(dve.tensor_scalar(y, x, cw[:, 3:4], C("conv_b", n, 1), ALU.mult, ALU.add))
                        for d in (1, 2, 3):
                            ins = dve.scalar_tensor_tensor(out=y[:, d:S], in0=x[:, 0:S - d], scalar=cw[:, 3 - d:4 - d],
                                                           in1=y[:, d:S], op0=ALU.mult, op1=ALU.add)
                            if d < 3:
                                then(ins)
                    elif what == "lruA":
                        n = step[1]
                        needs("act", "evac", ("lgate", n))
                        g = W(bGR + n % 2)[:, 0, :]
                        dve.tensor_tensor(W(bGI + n % 2)[:, 0, :], W(bGI + n % 2)[:, 0, :], W(bY + n)[:, 0, :], ALU.mult)
                        ins = dve.tensor_scalar(g, g, cL[:, n:n + 1], None, ALU.mult)
                    elif what == "lruC":
                        n = step[1]
                        needs("act", "lruB", n)
                        a, th, q = W(bLA + n % 2)[:, 0, :], W(bTH + n % 2)[:, 0, :], W(bGR + n % 2)[:, 0, :]
                        then(dve.tensor_tensor(q, a, a, ALU.mult))
                        ins = dve.scalar_tensor_tensor(out=th, in0=q, scalar=1.0, in1=th, op0=ALU.add, op1=ALU.mult)
                    elif what == "lruE":
                        n = step[1]
                        needs("act", "lruD", n)
                        gi, th, a, h = (W(z + n % 2)[:, 0, :] for z in (bGI, bTH, bLA, bHH))
                        then(dve.tensor_tensor(gi, gi, th, ALU.mult))
                        then(dve.tensor_tensor_scan(h, a, gi, 0.0, ALU.mult, ALU.add))
                        mix = W(MIX + n)[:, 0, :]
                        ins = dve.tensor_tensor(mix, mix, h, ALU.mult)
                    elif what == "dkz":
                        p = step[1]
                        needs("act", "evac", ("dk", 2 * p + 1))
                        if p:
                            needs("pe", "S", ("d", p - 1, 1))
                        for h in range(2):
                            z = W(cDZ + 2 * h, 2)
                            src = W(cDK + 2 * p + h)[:, 0, :]
                            dve.tensor_copy(z[0:64, 0, :], src[0:64, :])
                            ins = dve.tensor_copy(z[64:128, 1, :], src[64:128, :])
                    elif what == "dn":
                        needs("pe", "dn", step[1])
                        ins = dve.tensor_scalar(W(cDS, 2), psM[:, :].rearrange("p (a s) -> p a s", a=2), 1.0 / P, EPS,
                                                ALU.mult, ALU.add)
                    elif what == "dfin":
                        p = step[1]
                        needs("act", "dsqrt", p)
                        r, z, mix = W(cDS, 2), W(cOR + 2 * (p % 2), 2), W(MIX + 8 + 2 * p, 2)
                        then(dve.reciprocal(r, r))
                        then(dve.scalar_tensor_tensor(out=z, in0=z, scalar=sub, in1=r, op0=ALU.mult, op1=ALU.mult))
                        ins = dve.tensor_tensor(mix, mix, z, ALU.mult)
                    else:
                        raise AssertionError(step)
                    ins.then_inc(done[k]["dve"], 1)
                    count += 1

            dve.wait_ge(table_in, 48)
            run(0, A)
            dve.wait_ge(done[0]["dve"], len(A.steps["dve"]))
            dve.wait_ge(done[0]["pe"], len(A.steps["pe"]))
            tiles = dve.value_load(sti[0:1, 48:49], min_val=1, max_val=MAX_TILES)
            OE = W(mOE, 2).rearrange("p a s -> p (a s)")
            ST = W(mST).rearrange("p a s -> p (a s)")
            SJ = W(mSJ, 4)
            SW = W(mSW).rearrange("p a s -> p (a s)").rearrange("p (t c) -> p t c", t=NT)
            YT = W(mYT, 16)
            slot, weight = (lambda kk, tt: pos_w[:, 2 * kk + tt:2 * kk + tt + 1]), (lambda kk, tt: pos_w[:, 4 + 2 * kk + tt:5 + 2 * kk + tt])
            dve.memset(OE, 0.0).then_inc(moe["oe_ready"], 1)
            dve.memset(SJ, 0.0).then_inc(moe["scj_ready"], 1)
            dve.memset(YT[:, 0:8, :], 0.0).then_inc(moe["y_added"], 1)
            dve.memset(YT[:, 8:16, :], 0.0).then_inc(moe["y_added"], 1)
            dve.memset(AT, 0.0).then_inc(moe["at_ready"], 1)
            dve.memset(H1T, 0.0).then_inc(moe["ht_full"], 1)
            dve.memset(H3T, 0.0).then_inc(moe["h_copied"], 1)
            dve.memset(SL1, 0.0).then_inc(moe["sct_copied"], 1)
            dve.tensor_copy(J, K("slot")).then_inc(moe["j_ready"], 1)

            def pick(i, first=False):
                dve.wait_ge(moe["j_ready"], i + 1)
                if not first:
                    dve.wait_ge(moe["g_full"], i)
                for tt in range(NT):
                    dve.tensor_scalar(SG2[:, tt, :], J[:, 0:CAP], slot(0, tt), None, ALU.is_equal)
                    ins = dve.tensor_scalar(SG[:, tt, :], J[:, 0:CAP], slot(1, tt), None, ALU.is_equal)
                ins.then_inc(moe["pick_half"], 1)
                dve.wait_ge(moe["pick_half"], i + 1)
                dve.tensor_tensor(SG, SG, SG2, ALU.add).then_inc(moe["pick_ready"], 1)

            def weigh(i, first=False):
                if not first:
                    dve.wait_ge(moe["sct_full"], i)
                for tt in range(NT):
                    dve.tensor_scalar(SWA_[:, tt, :], J, slot(0, tt), weight(0, tt), ALU.is_equal, ALU.mult)
                    ins = dve.tensor_scalar(SW[:, tt, :], J, slot(1, tt), weight(1, tt), ALU.is_equal, ALU.mult)
                ins.then_inc(moe["weigh_half"], 1)
                dve.wait_ge(moe["weigh_half"], i + 1)
                dve.tensor_tensor(SW, SW, SWA_, ALU.add).then_inc(moe["scw_ready"], 1)
                dve.wait_ge(moe["scw_ready"], i + 1)
                dve.tensor_scalar(J, J, float(CAP), None, ALU.add).then_inc(moe["j_ready"], 1)

            def add_out(m, i):
                c, half = m // 2, m % 2
                y = YT[:, 8 * half + c:8 * half + c + 5:4, :]
                src = [psM, acc[1]][m % 2][:, :].rearrange("p (a s) -> p a s", a=2)
                dve.wait_ge(moe["y_full"], i * 8 + m + 1)
                dve.tensor_tensor(y, src, y, ALU.add).then_inc(moe["y_added"], 1)

            pick(0, True)
            weigh(0, True)
            dve.wait_ge(moe["y_added"], 2)
            with dve.Fori(0, tiles) as i:
                pick(i + 1)
                dve.wait_ge(moe["ht_full"], i + 2)
                dve.wait_ge(moe["at_ready"], i + 1)
                dve.tensor_reduce(H1T, psT[:, 0, :, :].rearrange("p c (r m) -> p c m r", m=CAP), AX.X, ALU.add)\
                    .then_inc(moe["hs_ready"], 1)
                dve.tensor_reduce(H3T, psT[:, 1, :, :].rearrange("p c (r m) -> p c m r", m=CAP), AX.X, ALU.add)\
                    .then_inc(moe["h3_ready"], 1)
                dve.wait_ge(moe["silu_done"], i + 1)
                dve.wait_ge(moe["h3_ready"], i + 1)
                dve.tensor_tensor(AT, SL1, H3T, ALU.mult).then_inc(moe["at_ready"], 1)
                dve.wait_ge(moe["y_added"], i * 8 + 2)
                for m in range(8):
                    add_out(m, i)
                dve.wait_ge(moe["sct_copied"], i + 2)
                for c in range(4):
                    ins = dve.tensor_scalar(SJ[:, c, :], ST, K("group", c, 1), None, ALU.mult)
                ins.then_inc(moe["scj_ready"], 1)
                weigh(i + 1)
            dve.wait_ge(moe["y_added"], tiles * 8 + 2)
            for m in range(8):
                add_out(m, tiles)
            dve.wait_ge(moe["y_added"], tiles * 8 + 10)
            dve.wait_ge(moe["j_ready"], tiles + 2)
            run(1, BC)




def _unit(w):
    k, n = w.shape
    return w.reshape(k // P, P, n).transpose(1, 0, 2).reshape(P, -1)


def _stream(order, part):
    out = np.zeros((len(order.units), P, UNIT), np.float32)
    for u, (key, floats, _) in enumerate(order.units):
        out[u, :, 0:floats] = part(key)
    return out


def kernel(**inputs):
    import concourse.bacc as bacc
    from concourse.bass_utils import run_bass_kernel_spmd

    a = {k: np.ascontiguousarray(v) for k, v in inputs.items()}
    w_in, w_out, w_ada = a["w_in"][0], a["w_out"][0], a["w_ada"][0]
    off = {"q": 0, "k": 1024, "v": 1280, "qi": 1536, "ki": 2560, "wi": 2624, "p": 2640}
    off_b = {"lx": 0, "lg": 1024, "bq": 2048, "bk": 3072, "bv": 3200, "bs": 3328}
    off_c = {"cq": 0, "ckv": 768, "kr": 1280, "mg": 1344, "dq": 2368, "dk": 3392, "dv": 4416, "dg": 5440}
    e_in, o_in = a["l0_w_in_2"], a["l1_w_in_2"]
    uq = a["l1_w_uq_2"].reshape(768, 8, 192)
    uq = np.concatenate([uq[:, :, 0:128].reshape(768, 1024), uq[:, :, 128:].reshape(768, 512)], axis=1)
    ukv = a["l1_w_ukv_2"].reshape(512, 8, 2, 128)

    def twice(w):
        return np.concatenate([w, w], axis=1)

    def part_a(key):
        name, n = key[0], key[1]
        if name == "ada":
            w = w_ada[512 * key[2]:512 * key[2] + 512, 512 * n:512 * n + 512]
            return w.reshape(4, P, 512).transpose(1, 0, 2).reshape(P, -1)
        if name == "wo":
            return _unit(w_out[:, P * n:P * n + P])
        if name == "ki":
            return _unit(twice(w_in[:, off["ki"]:off["ki"] + 64]))
        width = 16 if name == "wi" else P
        return _unit(w_in[:, off[name] + width * n:off[name] + width * (n + 1)])

    def part_bc(key):
        name, n = key
        if name in ("bk", "bv"):
            return _unit(twice(e_in[:, off_b[name] + 64 * n:off_b[name] + 64 * n + 64]))
        if name in off_b:
            return _unit(e_in[:, off_b[name] + P * n:off_b[name] + P * n + P])
        if name == "wb":
            return _unit(a["l0_w_out_2"][:, P * n:P * n + P])
        if name == "wc":
            return _unit(a["l1_w_out_2"][:, P * n:P * n + P])
        if name == "kr":
            return _unit(twice(o_in[:, off_c["kr"]:off_c["kr"] + 64]))
        if name == "uq":
            return np.concatenate([_unit(uq[:, P * c:P * c + P]) for c in (2 * n, 2 * n + 1)], axis=1)
        if name == "ukv":
            return np.concatenate([_unit(ukv[:, h, kv]) for kv in range(2) for h in (2 * n, 2 * n + 1)], axis=1)
        return _unit(o_in[:, off_c[name] + P * n:off_c[name] + P * n + P])

    def column(v):
        return v.reshape(-1, P).T

    def rows(v):
        return np.broadcast_to(v.reshape(1, -1), (P, v.size))

    cols = np.concatenate([
        column(a["c"]), column(a["b_ada"]), column(a["norm1_g"]), column(a["q_norm_g"]), column(a["k_norm_g"]),
        column(a["pool_scale"]), column(a["norm2_g"]), column(a["norm_gains_2"][0]), column(a["norm_gains_2"][1]),
        column(a["final_norm_gain_2"]),
        a["l0_conv_w_2"].reshape(4, 8, P).transpose(2, 1, 0).reshape(P, 32), column(a["l0_conv_b_2"]),
        column(a["l0_gate_x_b_2"]), column(a["l0_gate_a_b_2"]), column(a["l0_lru_lambda_2"]),
        column(a["l1_q_norm_2"]), column(a["l1_kv_norm_2"]), column(a["l1_subln_2"]), rows(a["l0_sinks_2"]),
        rows(a["l1_lambda_q1_2"]), rows(a["l1_lambda_k1_2"]), rows(a["l1_lambda_q2_2"]), rows(a["l1_lambda_k2_2"]),
    ], axis=1)
    route = np.concatenate([a["w_grp"][0], a["w_exp"][0]], axis=1)
    up = lambda w: w[0].reshape(N_EXPERTS, 4, 4, P, DE).transpose(0, 1, 3, 2, 4).reshape(N_EXPERTS, 4, P, UNIT)
    arrays = {
        "const": constants(),
        "cols": cols,
        "xT": a["x"][0].T.reshape(KD, P, S).transpose(1, 0, 2),
        "stream_a": _stream(A, part_a),
        "stream_bc": _stream(BC, part_bc),
        "w_pool": a["w_pool"][0].reshape(4, 2, P, 256).transpose(2, 0, 1, 3).reshape(P, UNIT),
        "w_route": _unit(route),
        "w_gates": np.stack([a["l0_gate_x_w_2"], a["l0_gate_a_w_2"]]).transpose(2, 0, 1, 3).reshape(P, UNIT),
        "w1": up(a["w1"]),
        "w3": up(a["w3"]),
        "w2": a["w2"][0].reshape(N_EXPERTS, 4, P, UNIT),
    }
    arrays = {k: np.ascontiguousarray(v) for k, v in arrays.items()}
    nc = bacc.Bacc("TRN2", target_bir_lowering=False, num_devices=1)
    t = {k: nc.dram_tensor(f"in_{k}", v.shape, F32, kind="ExternalInput").ap() for k, v in arrays.items()}
    t["out"] = nc.dram_tensor("out_0", (P, KD, S), F32, kind="ExternalOutput").ap()
    program(nc, t)
    r = run_bass_kernel_spmd(nc, [{f"in_{k}": v for k, v in arrays.items()}], core_ids=[0])
    return r.results[0]["out_0"].transpose(2, 1, 0).reshape(1, S, D)
```

```python
from contextlib import ExitStack

import numpy as np

import concourse.bass as bass
from concourse import mybir

ALU = mybir.AluOpType
ACT = mybir.ActivationFunctionType
AX = mybir.AxisListType
F32 = mybir.dt.float32
F32R = mybir.dt.float32r
I32 = mybir.dt.int32

P = 128
D = 2048
S = 256
NT = S // P
KD = D // P
EPS = 1e-6
UNIT = 2048
HALF = UNIT // 2
LAND = (9, 7)
PARTS = 4
SLOTS = 12
NEG = -1.0e38
TAKEN = -3.0e38
N_EXPERTS, N_GROUPS, PER_GROUP, DE = 32, 4, 8, 512
CAP = 32
MAX_TILES = 2 * S // CAP + N_EXPERTS - 1
LAMBDA_INIT = 0.8 - 0.6 * float(np.exp(-0.3))
LRU_C = 8.0
POOL_WINDOWS = (2, 4, 8, 16)

COLS = {}


def _cols():
    at = 0
    for name, n in (("c", 16), ("b_ada", 96), ("norm1_g", 16), ("q_norm_g", 1), ("k_norm_g", 1),
                    ("pool_scale", 8), ("norm2_g", 16), ("gain0", 16), ("gain1", 16), ("gain_f", 16),
                    ("conv_w", 32), ("conv_b", 8), ("gx_b", 8), ("ga_b", 8), ("lam", 8),
                    ("q_norm", 6), ("kv_norm", 4), ("subln", 1), ("sinks", 16), ("dl", 256)):
        COLS[name] = (at, n)
        at += n
    return at


NCOLS = _cols()

CONST = {}


def _const_cols():
    at = 0
    for name, n in (("ident", 128), ("tri", 128), ("rot1", 128), ("rot2", 128), ("rot3", 128),
                    ("cos1", 256), ("sin1", 256), ("cos2", 256), ("sin2", 256), ("cos3", 256),
                    ("sin3", 256), ("causal", 512), ("band", 256), ("icount", 64), ("slot", 128),
                    ("group", 4), ("rev", 8), ("tile", 48), ("cap", 8)):
        CONST[name] = (at, n)
        at += n
    return at


NCONST = _const_cols()


def constants():
    t = np.zeros((P, NCONST), np.float32)

    def put(name, a):
        lo, n = CONST[name]
        t[:, lo:lo + n] = np.asarray(a, np.float32).reshape(P, n)

    p = np.arange(P)
    put("ident", np.eye(P))
    put("tri", p[:, None] < p[None, :])
    pos = np.arange(S, dtype=np.float32)
    for n, (head, rd, theta) in enumerate(((128, 32, 500000.0), (64, 16, 500000.0), (64, 64, 10000.0))):
        half = rd // 2
        rot = np.zeros((P, P))
        cos, sin = np.ones((P, S)), np.zeros((P, S))
        j = np.arange(half, dtype=np.float32)
        if n < 2:
            inv = np.float32(theta) ** (-(j * np.float32(2.0)) / np.float32(rd))
        else:
            inv = np.float32(theta) ** (-j / np.float32(half))
        ang = (pos[None, :] * inv.astype(np.float32)[:, None]).astype(np.float32)
        for b in range(0, P, head):
            for q in range(half):
                rot[b + half + q, b + q] = -1.0
                rot[b + q, b + half + q] = 1.0
                for r in (b + q, b + half + q):
                    cos[r], sin[r] = np.cos(ang[q]), np.sin(ang[q])
        put(f"rot{n + 1}", rot)
        put(f"cos{n + 1}", cos)
        put(f"sin{n + 1}", sin)
    q = p[:, None, None] + P * np.arange(NT)[None, :, None]
    k = np.arange(S)[None, None, :]
    put("causal", np.where(k <= q, 0.0, NEG))
    put("band", np.where((k <= q) & (q - k < 128), 0.0, NEG)[:, 1])
    tok = np.arange(16)
    put("icount", np.broadcast_to(np.stack([1.0 / np.minimum(tok + 1, w) for w in POOL_WINDOWS])[None], (P, 4, 16)))
    put("slot", np.broadcast_to(np.tile(np.arange(CAP), P // CAP)[None], (P, P)))
    put("group", (p[:, None] // CAP) == np.arange(P // CAP)[None])
    put("rev", np.broadcast_to(np.arange(8, 0, -1)[None], (P, 8)))
    put("tile", np.broadcast_to(np.arange(48)[None], (P, 48)))
    put("cap", np.broadcast_to(CAP * np.arange(8)[None], (P, 8)))
    return t


LAGS = {"a": (1, 2, 3, 4), "b": (1, 2, 3, 4), "d": (1, 2, 3, 4), "m": (1, 3, 5, 6)}

class Order:

    def __init__(self):
        self.steps = {"pe": [], "act": [], "dve": []}
        self.at = {"pe": {}, "act": {}, "dve": {}}
        self.units = []
        self.pieces = []
        self.pieces_of = {}
        self.freed_by = []
        self.halves = []
        self.halves_of = {}
        self.last_use = {}
        self.acc = []
        self.misc = []
        self.small_bank = set()
        self.early = []
        self.lagged = []
        self.ahead = []

    def add(self, engine, *step):
        assert step not in self.at[engine], step
        self.steps[engine].append(step)
        self.at[engine][step] = len(self.steps[engine])

    def piece(self, key, h, floats, engine, *step):
        if h == 0:
            self.units.append(key)
        self.pieces_of.setdefault(key, []).append(len(self.pieces))
        self.pieces.append((self.units.index(key), h * floats, floats))
        self.freed_by.append((engine, step))

    def will_split_mix(self, name):
        self.ahead += [((name, n), h) for h in range(2) for n in range(2)]
        self.will_split([(name, n) for n in range(2, KD)])

    def will_split(self, keys):
        self.ahead += [(key, h) for key in keys for h in range(2)]

    def load(self, n=1):
        for key, h in self.ahead[:n]:
            q = len(self.halves)
            self.halves.append(len(self.pieces))
            self.halves_of.setdefault(key, []).append(q)
            self.piece(key, h, 6 * P if key[0] == "uq" else HALF, "dve", "lo", q)
            self.add("act", "hi", q)
            self.add("dve", "lo", q)
        del self.ahead[:n]

    def tick(self):
        now, self.lagged = self.lagged, []
        for n, what, x in now:
            if n > 1:
                self.lagged.append((n - 1, what, x))
            else:
                what(x)

    def drain(self):
        while self.lagged:
            self.tick()

    def mix_head(self, name, *groups):
        for n in range(2):
            self.add("pe", "part", (name, n), 0)
            self.last_use[self.halves_of[name, n][0]] = ("part", (name, n), 0)
            self.load()
            self.tick()
        self.drain()
        self.split_mix(name, *groups)
        self.misc.append(("ssum", name))

    def proj(self, x, halves=None, post=None, loads=1, between=None, first=0):
        if halves is None:
            keys = [(*x, 0), (*x, 1)] if x[0] in PAIRS else [x]
            halves = [q for key in keys for q in self.halves_of[key]]
        for i, q in enumerate(halves):
            if i < first:
                continue
            step = ("proj", x) if i == len(halves) - 1 else ("part", x, i)
            self.add("pe", *step)
            self.last_use[q] = step
            if i < len(halves) - 1:
                self.load()
                if between:
                    between()
        self.acc.append(("proj", x))
        self.add("act", "evac", x)
        if x[0] == "wi":
            self.add("pe", "wiT")
            self.misc.append(("wiT",))
            self.add("dve", "wi")
        if post == "res":
            self.add("dve", "res", x)
            self.add("act", "sq", x)
        self.load(loads)
        if between:
            between()
        self.tick()
        if post == "nr":
            self.lagged.append((1, self.norm_head, x))
            self.lagged.append((2, self.norm_tail, x))
            self.lagged.append((3, self.rotate, x))
        if post == "r":
            self.lagged.append((1, self.rotate, x))
        if post == "res":
            self.lagged.append((1, self.add_squares, x))

    def add_squares(self, x):
        if x[1]:
            self.add("dve", "sqsum", x)
        if x[1] == KD - 1:
            self.sum_squares(x)

    def sum_squares(self, x):
        self.add("pe", "ss", x)

    def norm_input(self, name):
        self.add("dve", "ssum", name)
        self.add("act", "sqrtn", name)
        self.add("dve", "rstd", name)
        self.add("dve", "scaled", name, 0)
        for g in range(4):
            if g < 3:
                self.add("dve", "scaled", name, g + 1)
            for c in range(4 * g, 4 * g + 4):
                self.add("act", "hh", name, c)
                self.add("dve", "hl", name, c)

    def split_mix(self, name, *groups):
        for c in groups:
            self.add("act", "mh", name, c)
            self.add("dve", "ml", name, c)

    def norm_head(self, x):
        self.add("pe", "nrm", x)
        self.misc.append(("nrm", x))
        self.add("dve", "nrm", x)

    def norm_tail(self, x):
        self.add("act", "sqrt", x)
        self.add("dve", "qn", x)

    def rotate(self, x):
        self.add("pe", "rot", x)
        (self.early if x[0] in ("k", "ki", "qi", "q") else self.misc).append(("rot", x))
        self.add("dve", "rot", x)

    def job(self, j):
        self.add("pe", "S", j)
        self.add("dve", "soft", j)
        kind = j[0] if isinstance(j, tuple) else "a"
        for lag, stage in zip(LAGS[kind], (self.exponents, self.scale, self.turn, self.values)):
            self.lagged.append((lag, stage, j))

    def exponents(self, j):
        self.add("act", "exp", j)

    def scale(self, j):
        self.add("dve", "scale", j)

    def turn(self, j):
        self.add("pe", "T", j)
        self.add("act", "pt", j)

    def values(self, j):
        self.add("pe", "O", j)
        self.add("dve", "out", j)


ADA_RATE = (0.75, 1.0, 0.75)

PAIRS = ("v", "bv", "dv")


def order_a():
    o = Order()
    o.add("dve", "setup")
    o.add("act", "silu_c")
    o.add("dve", "spread_c")

    shared = [False]

    def ada_t(b):
        o.add("pe", "adaT", b)
        o.add("dve", "adaT", b)

    def ada(b, q):
        if q == 1 and ("adaT", b - 1) not in o.at["pe"] and b:
            ada_t(b - 1)
        if q == 0 and shared[0]:
            o.small_bank.add(b)
            o.misc.append(("adaT", b))
        for h in range(2):
            o.piece(("ada", b, q), h, HALF, "pe", "ada", b, q)
        o.add("pe", "ada", b, q)
        if q == 3:
            o.add("act", "evac", ("ada", b))

    o.add("dve", "softplus0")
    o.add("act", "softplus1")
    o.add("dve", "softplus2")
    o.add("act", "lambda")
    o.add("dve", "lambda")
    for b in range(8):
        for q in range(4):
            ada(b, q)
        if b == 2:
            o.add("act", "sqx")
            o.add("pe", "ssx")
            o.misc.append(("ssx",))
            o.add("dve", "ssx")
            o.add("act", "sqrtx")
            o.add("dve", "xr")
    ada_t(7)
    rest = [(("k", 0), "nr"), (("k", 1), "nr"), (("v", 0), None), (("ki", 0), "r"), (("wi", 0), None)]
    rest += [(("qi", n), "r") for n in range(8)] + [(("q", n), "nr") for n in range(8)]
    for x, _ in rest:
        o.will_split([(*x, 0), (*x, 1)] if x[0] in PAIRS else [x])
    o.will_split([("p", n) for n in range(8)])
    o.will_split_mix("wo")
    o.load(2)
    o.add("dve", "h1")
    for c in range(KD + 1):
        if c < KD:
            o.add("dve", "h", "x", c)
            o.add("act", "hh", "x", c)
        if c:
            o.add("dve", "hl", "x", c - 1)
    o.load(2)
    left = [(b, q) for b in range(8, 24) for q in range(4)]
    owed = [0.0]

    def between(rate=ADA_RATE[0]):
        owed[0] += rate
        b = left[0][0] - 1 if left and left[0][1] == 0 else None
        if shared[0] and b is not None and ("adaT", b) not in o.at["pe"]:
            ada_t(b)
            return
        while owed[0] >= 1 and left:
            owed[0] -= 1
            b, q = left.pop(0)
            ada(b, q)

    idx = [(qt, c) for qt in range(2) for c in range(8)]
    for x, post in rest:
        o.proj(x, post=post, between=between)
        if x[0] == "q":
            for _ in range(2):
                i = idx.pop(0)
                o.add("pe", "idx", i)
                o.acc.append(("idx", i))
                o.add("act", "evac", ("idx", i))
                o.add("dve", "idx", i)
    def close():
        while len(left) % 4:
            ada(*left.pop(0))
        ada_t(23 - len(left) // 4)

    close()
    o.add("dve", "topk", 0)
    o.proj(("p", 0))
    o.proj(("p", 1))
    o.job(0)
    shared[0], owed[0] = True, 0.0

    def among():
        between(ADA_RATE[1])

    def after():
        between(ADA_RATE[2])

    o.proj(("p", 2), between=among)
    o.add("dve", "pool", 0)
    o.proj(("p", 3), between=among)
    o.job(1)
    o.add("dve", "pool", 1)
    o.proj(("p", 4), between=among)
    o.add("dve", "topk", 1)
    o.proj(("p", 5), between=among)
    o.job(2)
    o.proj(("p", 6), between=among)
    o.add("dve", "pool", 2)
    o.tick()
    o.proj(("p", 7), between=among)
    o.job(3)
    o.add("dve", "pool", 3)
    o.tick()
    close()
    shared[0], owed[0] = False, 0.0
    o.tick()
    for g in range(4):
        for dc in range(2):
            o.add("pe", "pmm", (g, dc))
            o.acc.append(("pmm", (g, dc)))
            o.add("act", "evac", ("pmm", (g, dc)))
    o.split_mix("wo", 2, 3, 0)
    o.mix_head("wo", 1)
    for n in range(KD):
        o.proj(("wo", n), post="res", between=after, first=int(n < 2))
    while left:
        ada(*left.pop(0))
    ada_t(23)
    o.add("dve", "cols")
    o.drain()
    o.add("dve", "ssum", "wo")
    o.add("act", "sqrtn", "wo")
    o.add("dve", "rstd", "wo")
    o.acc.append(("router",))
    for c in range(KD):
        o.add("dve", "h2", c)
        o.add("act", "h2", c)
    o.add("pe", "router")
    o.add("act", "evac", ("router",))
    o.add("pe", "routeT")
    o.misc.append(("routeT",))
    for tt in range(NT):
        for q in range(4):
            o.add("pe", "h2t", (tt, q))
            o.acc.append(("h2t", (tt, q)))
            o.add("act", "evac", ("h2t", (tt, q)))
    o.add("dve", "top1")
    o.add("act", "pexp")
    o.add("dve", "top2")
    o.add("pe", "cum")
    o.misc.append(("cum",))
    o.add("dve", "place")
    return o


def order_bc():
    o = Order()
    ahead = [("bk", n) for n in range(2)] + [("bv", 0, n) for n in range(2)] + [("bq", n) for n in range(8)]
    rest = [(name, n) for name in ("bs", "lx", "lg") for n in range(8)]
    ahead += rest
    o.will_split(ahead)
    o.will_split_mix("wb")
    ahead = [("cq", n) for n in range(6)] + [("ckv", n) for n in range(4)] + [("kr", 0)]
    ahead += [(name, n) for name in ("dk", "dq") for n in range(8)]
    ahead += [("dv", n, h) for n in range(4) for h in range(2)]
    ahead += [(name, n) for name in ("dg", "mg") for n in range(8)]
    ahead += [("uq", 4), ("uq", 5), ("uq", 0), ("uq", 1), ("ukv", 0), ("ukv", 1)]
    ahead += [("uq", 2), ("uq", 3)]
    o.will_split(ahead)
    o.ahead += [(("ukv", n), h) for h in range(2) for n in (2, 3)]
    o.will_split_mix("wc")
    o.load(1)
    o.misc.append(("ssum", "moe"))
    for n in range(KD):
        o.add("dve", "res", ("moe", n))
        o.add("act", "sq", ("moe", n))
        o.add("pe", "ss", ("moe", n))
    o.load(1)
    o.norm_input("moe")
    o.load(2)
    for n in range(2):
        o.proj(("bk", n))
    o.proj(("bv", 0))
    for n in range(8):
        o.proj(("bq", n))
    jobs = [("b", g, hh, qt) for g in range(2) for hh in range(2) for qt in range(2)]

    def lru_gates(p):
        for n in (2 * p, 2 * p + 1):
            o.add("pe", "lgate", n)
            if n % 2:
                o.acc.append(("lgate", n))
            o.add("act", "evac", ("lgate", n))
            o.add("dve", "lruA", n)

    def lru_decay(p):
        o.add("act", "lruB", p)
        o.add("dve", "lruC", p)

    def lru_scan(p):
        o.add("act", "lruD", p)
        for n in (2 * p, 2 * p + 1):
            o.add("dve", "lruE", n)

    for k, x in enumerate(rest):
        o.proj(x)
        if k >= 5 and k % 2 and jobs:
            o.job(jobs.pop(0))
        if x == ("bs", 7):
            o.add("act", "silu", "bs", 0, 8)
        if x[0] == "lx":
            o.add("dve", "conv", x[1])
        if k in (11, 14, 17, 20):
            p = (k - 11) // 3
            lru_gates(p)
            o.lagged.append((1, lru_decay, p))
            o.lagged.append((2, lru_scan, p))
        if x == ("lg", 3):
            o.add("act", "silu", "lg", 0, 4)
            o.add("dve", "lmul", 0)
    o.split_mix("wb", 2, 3, 0)
    o.add("act", "silu", "lg", 4, 4)
    o.add("dve", "lmul", 1)
    o.mix_head("wb", 1)
    for n in range(KD):
        o.proj(("wb", n), post="res", first=int(n < 2))
    o.drain()
    o.norm_input("wb")
    o.misc.append(("ssum", "cq"))
    for n in range(6):
        o.proj(("cq", n))
        o.lagged.append((1, o.sum_squares, ("cq", n)))
    o.drain()
    o.add("dve", "ssum", "cq")
    o.add("act", "sqrtn", "cq")
    o.misc.append(("ssum", "ckv"))
    for n in range(4):
        o.proj(("ckv", n))
        o.lagged.append((1, o.sum_squares, ("ckv", n)))
        if n == 0:
            o.add("dve", "cqn")
    o.drain()
    o.add("dve", "ssum", "ckv")
    o.add("act", "sqrtn", "ckv")
    o.add("dve", "ckvn")
    o.proj(("kr", 0), post="r")
    for n in range(8):
        o.proj(("dk", n))
    for n in range(8):
        o.proj(("dq", n))
    for n in range(4):
        o.proj(("dv", n))
    djobs = [("d", p, qt) for p in range(4) for qt in range(2)]

    def dkz(p):
        o.add("dve", "dkz", p)

    def dnorm_squares(p):
        o.add("act", "dsq", p)

    def dnorm_sums(p):
        o.add("pe", "dn", p)
        o.misc.append(("dn", p))
        o.add("dve", "dn", p)

    def dnorm_apply(p):
        o.add("act", "dsqrt", p)
        o.add("dve", "dfin", p)

    dkz(0)
    for k, x in enumerate([(name, n) for name in ("dg", "mg") for n in range(8)]):
        o.proj(x)
        if k % 2 == 0:
            j = djobs.pop(0)
            o.job(j)
            if j[2] == 1:
                o.lagged.append((5, dnorm_squares, j[1]))
                o.lagged.append((6, dnorm_sums, j[1]))
                o.lagged.append((7, dnorm_apply, j[1]))
                if djobs:
                    o.lagged.append((1, dkz, j[1] + 1))
        if x == ("dg", 7):
            o.add("act", "silu", "dg", 0, 8)
    mjobs = [("m", hg, qt) for hg in range(2) for qt in range(2)]

    def q_up(u):
        for h, c in enumerate((2 * u, 2 * u + 1)):
            o.proj(("qn", c) if c < 8 else ("qr", c - 8), halves=[o.halves_of["uq", u][h]],
                   post=None if c < 8 else "r")

    def kv_up(u):
        for c in (2 * u, 2 * u + 1):
            o.proj(("kn", c), halves=[o.halves_of["ukv", u][0]], loads=c % 2)
        o.proj(("vm", u), halves=[o.halves_of["ukv", u][1]])

    for name, n in (("cq", 6), ("ckv", 4)):
        for c in range(n):
            o.add("act", "ch", name, c)
            o.add("dve", "cl", name, c)
    o.add("act", "silu", "mg", 0, 8)
    for u in (4, 5, 0, 1):
        q_up(u)
    for u in (0, 1):
        kv_up(u)
    o.drain()
    o.job(mjobs[0])
    q_up(2)
    o.job(mjobs[1])
    q_up(3)
    for c in range(4, 8):
        o.proj(("kn", c), halves=[o.halves_of["ukv", c // 2][0]], loads=c % 2)
    o.job(mjobs[2])
    for u in (2, 3):
        o.proj(("vm", u), halves=[o.halves_of["ukv", u][1]])
    o.split_mix("wc", 2, 3)
    o.job(mjobs[3])
    o.mix_head("wc", 0, 1)
    for n in range(KD):
        o.proj(("wc", n), post="res", first=int(n < 2))
    o.drain()
    o.add("dve", "ssum", "wc")
    o.add("act", "sqrtn", "wc")
    o.add("dve", "rstd", "wc")
    for g in range(4):
        o.add("dve", "final", g)
    return o


A = order_a()
BC = order_bc()


def program(nc, t):
    with ExitStack() as ctx:
        def sb(name, shape, dt=F32):
            return ctx.enter_context(nc.sbuf_tensor(name, shape, dt))

        def sem(name):
            return ctx.enter_context(nc.semaphore(name))

        X = sb("X", [P, KD, S])
        low = sb("low", [P, 48, S])
        cst = sb("cst", [P, NCONST])
        col = sb("col", [P, NCOLS])
        SB = sb("SB", [P, 2, 4, S])
        PTS = sb("PTS", [P, NT, 4, P])
        ones = sb("ones", [P, P])
        ada = sb("ada", [P, 96])
        small = sb("small", [P, 256])
        sti = sb("sti", [P, 64], I32)

        arena_at = (nc.sbuf_base + 31) // 32 * 32
        parts_kib, land_kib = 2 * 4 * PARTS + 2 * KD, [4 * n for n in LAND]
        arena_kib = parts_kib + land_kib[1] + 20
        assert arena_kib == parts_kib + land_kib[0] + 12 and arena_kib >= 8 * SLOTS
        sb("arena", [P, arena_kib * 1024 // 4])

        def inside(name, shape, dt, kib):
            return nc.alloc_sbuf_tensor_at(name, shape, dt, offset=arena_at + 1024 * kib)

        WH = inside("WH", [P, PARTS, HALF], F32R, 0)
        WL = inside("WL", [P, PARTS, HALF], F32R, 4 * PARTS)
        HH = inside("HH", [P, KD, S], F32R, 8 * PARTS)
        HL = inside("HL", [P, KD, S], F32R, 8 * PARTS + KD)
        land = [inside(f"land{k}", [P, LAND[k], HALF], F32, parts_kib) for k in range(2)]
        high_a = inside("high_a", [P, 12, S], F32, parts_kib + land_kib[0])
        high_bc = inside("high_bc", [P, 20, S], F32, parts_kib + land_kib[1])
        ring = inside("ring", [P, SLOTS, UNIT], F32, 0)

        def W(a, n=1):
            if a >= 68:
                return high_a[:, a - 68:a - 68 + n, :]
            if a >= 48:
                return high_bc[:, a - 48:a - 48 + n, :]
            assert a + n <= 48
            return low[:, a:a + n, :]

        def K(name, lo=0, n=None):
            at, size = CONST[name]
            return cst[:, at + lo:at + lo + (size - lo if n is None else n)]

        def C(name, lo=0, n=None):
            at, size = COLS[name]
            return col[:, at + lo:at + lo + (size - lo if n is None else n)]

        acc = [ctx.enter_context(nc.psum_tensor(f"acc{i}", [P, 512], F32)) for i in range(2)]
        psS = ctx.enter_context(nc.psum_tensor("psS", [P, 4, S], F32))
        psT = ctx.enter_context(nc.psum_tensor("psT", [P, NT, 4, P], F32))
        psO = ctx.enter_context(nc.psum_tensor("psO", [P, 4, P], F32))
        psM = ctx.enter_context(nc.psum_tensor("psM", [P, 512], F32))
        bankS = [psS[:, 0:2, :].rearrange("p a b -> p (a b)"), psS[:, 2:4, :].rearrange("p a b -> p (a b)")]
        bankT = [psT[:, n, :, :].rearrange("p a b -> p (a b)") for n in range(2)]
        bankO = psO[:, :, :].rearrange("p a b -> p (a b)")

        table_in = sem("table_in")
        x_in, rest_in = sem("x_in"), sem("rest_in")
        aux_in = sem("aux_in")
        unit_in = [[sem(f"unit_in{k}_{i}") for i in range(LAND[k])] for k in range(2)]
        done = [{e: sem(f"{e}_done{k}") for e in ("pe", "act", "dve")} for k in range(2)]
        act_link, dve_link = sem("act_link"), sem("dve_link")
        tile_in = [sem(f"tile_in{i}") for i in range(SLOTS)]
        moe = {n: sem(n) for n in ("pick_ready", "g_full", "g_copied", "gt_full", "xg_ready", "w_used",
                                   "h_copied", "ht_full", "hs_ready", "silu_done", "at_ready", "oe_ready",
                                   "sct_full", "sct_copied", "scj_ready", "scw_ready", "y_full", "y_added",
                                   "j_ready", "pick_half", "weigh_half", "h3_ready")}
        out_done = sem("out_done")

        MIX = 0
        aQ, aK, aV, aQI, aKI, aAD, aKR, aWR, aRT, aT2 = 16, 24, 26, 28, 36, 38, 40, 41, 44, 45
        aPR, aSC, aWK, aRL, aPS, aTM, aSQ, aHT, aWI, aPW, aCB, aSA = 28, 46, 68, 70, 70, 70, 74, 76, 76, 16, 78, 77
        mYT, mH2, mGS, mXG, mHS, mOE, mST, mSJ, mSW = 0, 16, 32, 34, 36, 40, 42, 43, 47
        bK, bV, bQ, bGW, bY, bLX, bGI, bGR, bLA, bTH = 16, 20, 22, 30, 38, 46, 48, 50, 52, 54
        cQN, cKN, cVM, cCQ, cCKV, cKR, cDZ, cQR, cOR, cDS = 16, 24, 32, 40, 46, 50, 52, 52, (56, 64), 66
        cDQ, cDK = 16, 24
        dRT, dT2, dTM, dSQ, dSA, dKX = 58, 59, 60, 62, 64, 66
        V_a = W(aV, 2).rearrange("p k (g d) -> p k g d", d=P)
        V_b = W(bV, 2).rearrange("p k (g d) -> p k g d", d=P)
        V_c = W(cVM, 8).rearrange("p a s -> p (a s)").rearrange("p (k h d) -> p k h d", k=NT, d=P)
        PW = W(aPW, 8).rearrange("p a s -> p (a s)").rearrange("p (g k d) -> p g k d", g=4, k=2)
        GW = W(bGW, 8).rearrange("p a s -> p (a s)").rearrange("p (w n d) -> p w n d", w=2, n=8)
        WR = W(aWR, 3).rearrange("p a s -> p (a s)")[:, 0:KD * 36].rearrange("p (k n) -> p k n", n=36)
        AD = W(aAD, 2).rearrange("p a s -> p (a s)")
        cB = W(aCB, 2).rearrange("p a s -> p (a s)").rearrange("p (k m) -> p k m", m=CAP)
        S1, S2 = 0, 1

        cs, g1, g2, sub = small[:, 0:16], small[:, 16:32], small[:, 32:48], small[:, 48:49]
        lamn, wi, top = small[:, 49:50], small[:, 64:96], small[:, 96:112]
        lam2 = small[:, 50:56]
        jst = small[:, 112:144].rearrange("p (b k h) -> p b k h", b=2, k=4)
        cL, tsp = small[:, 144:152], small[:, 152:192]
        wis = small[:, 208:240]
        pos_w = small[:, 192:200]
        sh1, sc1, gt1, sh2, sc2, gt2 = (ada[:, 16 * n:16 * n + 16] for n in range(6))

        scr = SB[:, :, :, :].rearrange("p a b s -> p (a b s)")
        SG = scr[:, 0:64].rearrange("p (t c) -> p t c", t=NT)
        SG2 = scr[:, 64:128].rearrange("p (t c) -> p t c", t=NT)
        J = scr[:, 128:256]
        SWA_ = scr[:, 256:512].rearrange("p (t c) -> p t c", t=NT)
        H1T = scr[:, 512:640].rearrange("p (c m) -> p c m", m=CAP)
        H3T = scr[:, 640:768].rearrange("p (c m) -> p c m", m=CAP)
        AT = scr[:, 768:896].rearrange("p (c m) -> p c m", m=CAP)
        SL1 = scr[:, 896:1024].rearrange("p (c m) -> p c m", m=CAP)

        ident = K("ident")

        def jobs_of(o):
            return [s[1] for s in o.steps["pe"] if s[0] == "S"]

        def keys_of(j):
            return P * ((j[-1] if isinstance(j, tuple) else j // 2) + 1)

        def qt_of(j):
            return j[-1] if isinstance(j, tuple) else j // 2

        def rot_of(x):
            return {"k": "rot1", "q": "rot1", "ki": "rot2", "qi": "rot2"}.get(x[0], "rot3")

        def rot_chunk(x):
            at = {"k": aK, "q": aQ, "ki": aKR, "qi": aQI, "kr": dKX, "qr": cQR}[x[0]]
            return W(at + x[1])[:, 0, :]

        def scaled_at(c):
            return 60 + c % 8

        def pooled(g):
            return W(aPR + 2 * g, 2)

        rt = W(68, 12).rearrange("p a s -> p (a s)")
        RTS = W(aKR).rearrange("p a s -> p (a s)")
        LG = rt[:, 0:72].rearrange("p (t n) -> p t n", t=NT)
        gd, gk, goh = (rt[:, 80 + 8 * n:88 + 8 * n].rearrange("p (t n) -> p t n", t=NT) for n in range(3))
        r1 = rt[:, 112:144].rearrange("p (k t) -> p k t", t=NT)
        els, els2, ek, oh1, oh2 = (rt[:, 160 + 16 * n:176 + 16 * n].rearrange("p (t n) -> p t n", t=NT) for n in range(5))
        sel = rt[:, 256:320].rearrange("p (t g e) -> p t g e", t=NT, g=4)
        A12 = rt[:, 320:448].rearrange("p (k t g e) -> p k t g e", k=2, t=NT, g=4)
        MM = rt[:, 448:512].rearrange("p (t n) -> p t n", t=NT)
        cumS = rt[:, 512:608]
        nt, incl, excl, zero32 = (rt[:, 608 + 32 * n:640 + 32 * n] for n in range(4))
        cmp8 = rt[:, 768:1024].rearrange("p (e c) -> p e c", c=8)
        slotp = rt[:, 1024:1088].rearrange("p (t n) -> p t n", t=NT)
        tmp2 = rt[:, 1088:1216].rearrange("p (k t n) -> p k t n", k=2, t=NT)
        eid = rt[:, 1216:1280]
        cmp48 = rt[:, 1536:3072].rearrange("p (i e) -> p i e", e=32)

        def M_of(tt):
            return MM[:, tt, :]

        block = ctx.enter_context(nc.Block())

        @block.sync
        def _(sp):
            sp.dma_start(col[:, :], t["cols"]).then_inc(table_in, 16)
            sp.dma_start(cst[:, 0:P], t["const"][:, 0:P]).then_inc(table_in, 16)

            def stream(k, o, src, tiles=None):
                for p, (u, lo, floats) in enumerate(o.pieces):
                    slot = p % LAND[k]
                    if p >= LAND[k]:
                        engine, step = o.freed_by[p - LAND[k]]
                        sp.wait_ge(done[k][engine], o.at[engine][step])
                    sp.dma_start(land[k][:, slot, 0:floats], src[u, :, lo:lo + floats]).then_inc(unit_in[k][slot], 16)
                    if k == 0 and p == LAND[0] - 1:
                        sp.dma_start(X[:, :, :], t["xT"]).then_inc(x_in, 16)
                    if o.units[u] == ("ada", 7, 3) and lo:
                        sp.dma_start(cst[:, P:NCONST], t["const"][:, P:NCONST]).then_inc(rest_in, 16)
                    if o.units[u] == ("bs", 0) and lo:
                        sp.wait_ge(moe["y_added"], tiles * 8 + 10)
                        sp.dma_start(GW.rearrange("p w n d -> p (w n d)"), t["w_gates"]).then_inc(aux_in, 16)
                    if o.units[u] == ("wo", 2) and not lo:
                        sp.dma_start(WR.rearrange("p k n -> p (k n)"), t["w_route"]).then_inc(aux_in, 16)
                        sp.wait_ge(done[0]["pe"], A.at["pe"][("S", 3)])
                        sp.dma_start(PW.rearrange("p g k d -> p (g k d)"), t["w_pool"]).then_inc(aux_in, 16)

            stream(0, A, t["stream_a"])
            sp.wait_ge(done[0]["pe"], max(A.at["pe"][("proj", ("wo", KD - 1))], A.at["pe"][("adaT", 23)]))
            for s in range(SLOTS):
                sp.dma_start(ring[:, s, :], (t["w1"], t["w3"], t["w2"])[s // 4][0, s % 4, :, :]).then_inc(tile_in[s], 16)
            sp.wait_ge(done[0]["dve"], A.at["dve"][("place",)])
            sp.wait_ge(done[0]["act"], len(A.steps["act"]))
            sp.wait_ge(done[0]["pe"], len(A.steps["pe"]))
            tiles = sp.value_load(sti[0:1, 48:49], min_val=1, max_val=MAX_TILES)

            with sp.Fori(1, tiles) as i:
                e = sp.value_load(sti[0:1, bass.ds(i, 1)], min_val=0, max_val=N_EXPERTS - 1)
                for s in range(SLOTS):
                    sp.wait_ge(moe["w_used"], i * SLOTS + (s + 1 - SLOTS))
                    src = (t["w1"], t["w3"], t["w2"])[s // 4]
                    sp.dma_start(ring[:, s, :],
                                 src[bass.ds(e, 1), s % 4, :, :].rearrange("e p n -> (e p) n")).then_inc(tile_in[s], 16)
            sp.wait_ge(moe["w_used"], tiles * SLOTS)
            stream(1, BC, t["stream_bc"], tiles)
            for g in range(4):
                sp.wait_ge(done[1]["dve"], BC.at["dve"][("final", g)])
                sp.dma_start(t["out"][:, 4 * g:4 * g + 4, :], W(MIX + 4 * g, 4)).then_inc(out_done, 16)
            sp.wait_ge(out_done, 64)

        @block.tensor
        def _(pe):
            def needs(k, engine, o, *step):
                pe.wait_ge(done[k][engine], o.at[engine][step])

            def landed(k, o, p):
                pe.wait_ge(unit_in[k][p % LAND[k]], 16 * (p // LAND[k] + 1))
                return land[k][:, p % LAND[k], :]

            def attention(k, o, kind, j, jobs):
                n = jobs.index(j)
                qt, nk = qt_of(j), keys_of(j)
                q = slice(P * qt, P * qt + P)
                if kind == "S":
                    if n:
                        needs(k, "dve", o, "soft", jobs[n - 1])
                    if k == 0:
                        g = j % 2
                        needs(k, "dve", o, "rot", ("q", 4 * g + 3))
                        for h in range(4):
                            mm = pe.matmul(psS[:, h, 0:nk], W(aQ + 4 * g + h)[:, 0, q], W(aK + g)[:, 0, 0:nk],
                                           start=True, stop=True)
                    elif j[0] == "b":
                        _, g, hh, _ = j
                        for c in range(2):
                            mm = pe.matmul(psS[:, 2 * c:2 * c + 2, 0:nk], W(bQ + 4 * g + 2 * hh + c)[:, 0, q],
                                           W(bK + 2 * g, 2)[:, :, 0:nk], start=True, stop=True)
                    elif j[0] == "d":
                        needs(k, "dve", o, "dkz", j[1])
                        for c in range(2):
                            mm = pe.matmul(psS[:, 2 * c:2 * c + 2, 0:nk], W(cDQ + 2 * j[1] + c)[:, 0, q],
                                           W(cDZ + 2 * c, 2)[:, :, 0:nk], start=True, stop=True)
                    else:
                        needs(k, "act", o, "evac", ("kn", 4 * j[1] + 3))
                        needs(k, "dve", o, "rot", ("qr", 3))
                        for c in range(4):
                            h = 4 * j[1] + c
                            pe.matmul(psS[:, c, 0:nk], W(cQN + h)[:, 0, q], W(cKN + h)[:, 0, 0:nk],
                                      start=True, stop=False)
                            mm = pe.matmul(psS[:, c, 0:nk], W(cQR + h // 2)[:, 0, q],
                                           W(cKR + h % 2)[:, 0, 0:nk], start=False, stop=True)
                if kind == "T":
                    if k == 0 and n == 0:
                        needs(k, "dve", o, *o.early[-1])
                        needs(k, "dve", o, "adaT", max(s[1] for s in o.steps["pe"][:o.at["pe"][("T", 0)]] if s[0] == "adaT"))
                    needs(k, "dve", o, "scale", j)
                    if n:
                        needs(k, "act", o, "pt", jobs[n - 1])
                    heads = 2 if k and j[0] == "d" else 4
                    for kt in range(qt + 1):
                        for h in range(heads):
                            src = 2 * h if heads == 2 else h
                            mm = pe.transpose(psT[:, kt, h, :], SB[:, n % 2, src, P * kt:P * kt + P], ident)
                if kind == "O":
                    needs(k, "act", o, "pt", j)
                    if n:
                        needs(k, "dve", o, "out", jobs[n - 1])
                    if k == 0 or j[0] == "b":
                        v = V_a[:, :, j % 2, :] if k == 0 else V_b[:, :, j[1], :]
                        for kt in range(qt + 1):
                            mm = pe.matmul(psO[:, :, :], v[:, kt, :], PTS[:, kt, :, :], start=(kt == 0), stop=(kt == qt))
                    else:
                        heads = 2 if j[0] == "d" else 4
                        for h in range(heads):
                            for kt in range(qt + 1):
                                mm = pe.matmul(psO[:, h, :], V_c[:, kt, heads * j[1] + h, :], PTS[:, kt, h, :],
                                               start=(kt == 0), stop=(kt == qt))
                mm.then_inc(done[k]["pe"], 1)

            def product(k, o, x, i, bank):
                name, n = x
                last = True
                if name in ("qn", "qr"):
                    c = n if name == "qn" else 8 + n
                    q, rows, cols, wide = o.halves_of["uq", c // 2][c % 2], range(6), slice(0, 6 * P), False
                elif name == "kn":
                    q, rows, cols, wide = o.halves_of["ukv", n // 2][0], range(6, 10), slice(512 * (n % 2), 512 * (n % 2) + 512), False
                elif name == "vm":
                    q, rows, cols, wide = o.halves_of["ukv", n][1], range(6, 10), slice(0, HALF), True
                elif name in PAIRS:
                    q, rows, cols, wide = o.halves_of[(*x, i // 2)][i % 2], range(4 * i, 4 * i + 4), slice(0, HALF), True
                    last = i == 3
                else:
                    q, rows, cols, wide = o.halves_of[x][i], range(8 * i, 8 * i + 8), slice(0, HALF), False
                    if name in ("wo", "wb", "wc"):
                        rows = range(8 - 8 * i, 16 - 8 * i)
                    last = i == 1
                needs(k, "dve", o, "lo", q)
                wh, wl = (z[:, q % PARTS, cols].rearrange("p (k m) -> p k m", k=len(rows)) for z in (WH, WL))
                terms = [(a, b, c, kk) for kk in range(len(rows)) for a, b, c in ((wh, HH, 0), (wl, HH, 1), (wh, HL, 2))]
                normed = {("k", 0): "x", ("bk", 0): "moe", ("cq", 0): "wb"}.get(x)
                for tt in range(NT if wide else 1):
                    for z, (w, h, term, kk) in enumerate(terms):
                        if normed and term == 0:
                            needs(k, "dve", o, "hl", normed, rows[kk])
                        if x in (("qr", 0), ("kn", 0)) and term == 0:
                            needs(k, "dve", o, "cl", *(("cq", kk) if name == "qr" else ("ckv", kk)))
                        if x in (("wo", 0), ("wb", 0), ("wc", 0)) and term == 0 and kk % 4 == 0:
                            needs(k, "dve", o, "ml", name, rows[kk] // 4)
                        stop = last and z == len(terms) - 1
                        if wide:
                            mm = pe.matmul(bank[:, S * tt:S * tt + S], h[:, rows[kk], P * tt:P * tt + P], w[:, kk, :],
                                           start=(z == 0 and i == 0 and tt == 0), stop=stop, skip_group_check=True)
                        else:
                            mm = pe.matmul(bank[:, 0:S], w[:, kk, :], h[:, rows[kk], :], start=(z == 0 and i == 0), stop=stop)
                mm.then_inc(done[k]["pe"], 1)

            READ = {"adaT": "adaT", "wiT": "wi", "routeT": "top1", "ssx": "ssx", "nrm": "nrm", "rot": "rot", "cum": "place", "ssum": "ssum", "dn": "dn"}
            FIRST_SS = (("wo", KD - 1), ("moe", 0), ("wb", KD - 1), ("cq", 0), ("ckv", 0), ("wc", KD - 1))
            LAST = {"cq": 5, "ckv": 3}

            def run(k, o):
                jobs = jobs_of(o)
                nr = [s[1] for s in o.steps["pe"] if s[0] == "nrm"]

                def bank_of(step):
                    n = o.acc.index(step)
                    if n >= 2:
                        prev = o.acc[n - 2]
                        needs(k, "act", o, "evac", prev[1] if prev[0] == "proj" else prev)
                    return acc[n % 2]

                def misc_free(item):
                    n = o.misc.index(item)
                    if n:
                        prev = o.misc[n - 1]
                        needs(k, "dve", o, READ[prev[0]], *prev[1:])

                for step in o.steps["pe"]:
                    what = step[0]
                    if what in ("S", "T", "O"):
                        attention(k, o, what, step[1], jobs)
                        continue
                    if what in ("proj", "part"):
                        x = step[1]
                        i = step[2] if what == "part" else {"v": 3, "bv": 3, "dv": 3, "qn": 0, "qr": 0, "kn": 0, "vm": 0}.get(x[0], 1)
                        product(k, o, x, i, bank_of(("proj", x)))
                        continue
                    if what == "ada":
                        if step[1:] == (0, 0):
                            needs(k, "dve", o, "spread_c")
                        _, b, q = step
                        bank = psM[:, :] if b in o.small_bank else bankO
                        if q == 0 and b in o.small_bank:
                            misc_free(("adaT", b))
                        if q == 0 and b:
                            needs(k, "act", o, "evac", ("ada", b - 1))
                        if q == 0 and ("O", 3) in o.at["pe"] and o.at["pe"][("O", 3)] < o.at["pe"][step]:
                            needs(k, "dve", o, "out", 3)
                        w = [landed(k, o, p).rearrange("p (c n) -> p c n", c=2) for p in o.pieces_of["ada", b, q]]
                        for c in range(4):
                            mm = pe.matmul(bank[CAP * c:CAP * c + CAP, :], cB[:, 4 * q + c, :], w[c // 2][:, c % 2, :],
                                           start=(q == 0), stop=(q == 3), tile_position=(0, CAP * c))
                    elif what == "adaT":
                        needs(k, "act", o, "evac", ("ada", step[1]))
                        if step[1]:
                            needs(k, "dve", o, "adaT", step[1] - 1)
                        if o.at["pe"][("T", 3)] < o.at["pe"][step]:
                            needs(k, "act", o, "pt", 3)
                        bank = psM[:, :] if step[1] in o.small_bank else bankT[1]
                        for c in range(4):
                            mm = pe.transpose(bank[:, P * c:P * c + P], AD[:, P * c:P * c + P], ident)
                    elif what == "wiT":
                        misc_free(step)
                        needs(k, "act", o, "evac", ("wi", 0))
                        for tt in range(NT):
                            mm = pe.transpose(psM[:, P * tt:P * tt + P], W(aWI)[:, 0, P * tt:P * tt + P], ident)
                    elif what == "ssx":
                        needs(k, "dve", o, "setup")
                        needs(k, "act", o, "sqx")
                        for c in range(KD):
                            mm = pe.matmul(psM[:, 0:S], ones[:, :], W(MIX + c)[:, 0, :], start=(c == 0), stop=(c == KD - 1))
                    elif what == "ss":
                        x = step[1]
                        if x in FIRST_SS:
                            misc_free(("ssum", x[0]))
                        sq = W((aSQ if k == 0 else dSQ) + x[1] % 2)[:, 0, :]
                        if x[0] in ("wo", "wb", "wc"):
                            needs(k, "dve", o, "sqsum", x)
                            sq = W(aSA if k == 0 else dSA)[:, 0, :]
                        else:
                            needs(k, "act", o, "sq" if x[0] == "moe" else "evac", x)
                        mm = pe.matmul(psM[:, 0:S], ones[:, :], sq, start=(x in FIRST_SS), stop=(x[1] == LAST.get(x[0], KD - 1)))
                    elif what == "nrm":
                        x = step[1]
                        misc_free(step)
                        needs(k, "act", o, "evac", x)
                        mm = pe.matmul(psM[:, 0:S], ones[:, :], W(aSQ + nr.index(x) % 2)[:, 0, :], start=True, stop=True)
                    elif what == "rot":
                        x = step[1]
                        n = o.early.index(step) if step in o.early else None
                        if n == 0:
                            pe.wait_ge(rest_in, 16)
                        if n is None:
                            misc_free(step)
                        elif n:
                            needs(k, "dve", o, *o.early[n - 1])
                        if x[0] in ("k", "q"):
                            needs(k, "dve", o, "qn", x)
                        else:
                            needs(k, "act", o, "evac", x)
                        mm = pe.matmul((psM if n is None else bankT[0])[:, 0:S], K(rot_of(x)), rot_chunk(x), start=True, stop=True)
                    elif what == "idx":
                        qt, c = step[1]
                        if c == 0 and qt == 0:
                            needs(k, "dve", o, "rot", ("qi", 7))
                        bank = bank_of(step)
                        nk = P * (qt + 1)
                        mm = pe.matmul(bank[:, 0:2 * nk].rearrange("p (a s) -> p a s", a=2),
                                       W(aQI + c)[:, 0, P * qt:P * qt + P], W(aKI, 2)[:, :, 0:nk], start=True, stop=True)
                    elif what == "pmm":
                        g, dc = step[1]
                        needs(k, "dve", o, "pool", g)
                        if (g, dc) == (0, 0):
                            pe.wait_ge(aux_in, 32)
                        bank = bank_of(step)
                        for c in range(2):
                            mm = pe.matmul(bank[:, 0:S], PW[:, g, c, P * dc:P * dc + P], pooled(g)[:, c, :],
                                           start=(c == 0), stop=(c == 1))
                    elif what == "router":
                        pe.wait_ge(aux_in, 32)
                        bank = bank_of(step)
                        for c in range(KD):
                            needs(k, "act", o, "h2", c)
                            mm = pe.matmul(bank[0:36, 0:S], WR[:, c, :], W(MIX + c)[:, 0, :],
                                           start=(c == 0), stop=(c == KD - 1))
                    elif what == "routeT":
                        misc_free(step)
                        needs(k, "act", o, "evac", ("router",))
                        for tt in range(NT):
                            mm = pe.transpose(psM[:, 36 * tt:36 * tt + 36], RTS[0:36, P * tt:P * tt + P], ident[0:36, 0:36])
                    elif what == "cum":
                        misc_free(step)
                        needs(k, "dve", o, "top2")
                        tri = K("tri")
                        pe.matmul(psM[:, 0:32], tri, M_of(0), start=True, stop=True)
                        pe.matmul(psM[:, 32:64], ones[:, :], M_of(0), start=True, stop=False)
                        pe.matmul(psM[:, 32:64], tri, M_of(1), start=False, stop=True)
                        pe.matmul(psM[:, 64:96], ones[:, :], M_of(0), start=True, stop=False)
                        mm = pe.matmul(psM[:, 64:96], ones[:, :], M_of(1), start=False, stop=True)
                    elif what == "h2t":
                        tt, q = step[1]
                        bank = bank_of(step)
                        for c in range(4):
                            mm = pe.transpose(bank[:, P * c:P * c + P], W(MIX + 4 * q + c)[:, 0, P * tt:P * tt + P], ident)
                    elif what == "lgate":
                        n = step[1]
                        if n == 0:
                            pe.wait_ge(aux_in, 48)
                        needs(k, "dve", o, "conv", n)
                        if n % 2:
                            bank = bank_of(step)
                        else:
                            bank = psM[:, :]
                            if n:
                                needs(k, "act", o, "evac", ("lgate", n - 2))
                        for g in range(2):
                            mm = pe.matmul(bank[:, S * g:S * g + S], GW[:, g, n, :], W(bY + n)[:, 0, :],
                                           start=True, stop=True)
                    elif what == "dn":
                        p = step[1]
                        misc_free(step)
                        needs(k, "act", o, "dsq", p)
                        mm = pe.matmul(psM[:, :], ones[:, :], W(cDS, 2)[:, :, :], start=True, stop=True)
                    else:
                        raise AssertionError(step)
                    mm.then_inc(done[k]["pe"], 1)

            pe.wait_ge(table_in, 32)
            run(0, A)

            needs(0, "dve", A, "place")
            needs(0, "act", A, "evac", ("h2t", (1, 3)))
            tiles = pe.value_load(sti[0:1, 48:49], min_val=1, max_val=MAX_TILES)
            bG, bGT, bH, bHT, bW2, bY2 = acc[0][:, :], acc[1][:, :], bankS, bankT, bankO, psM[:, :]
            ybank = [bY2, bGT]
            GS = W(mGS, 2).rearrange("p a s -> p (a s)")
            XG = W(mXG, 2).rearrange("p a s -> p (a s)").rearrange("p (c n m) -> p c n m", c=4, m=CAP)
            HS = W(mHS, 4).rearrange("p (b a) s -> p b (a s)", b=2)
            OE = W(mOE, 2).rearrange("p a s -> p (a s)")
            SJ = W(mSJ, 4)
            SW = W(mSW).rearrange("p a s -> p (a s)").rearrange("p (t c) -> p t c", t=NT)
            H2 = W(mH2, 16).rearrange("p a s -> p (a s)").rearrange("p (t d) -> p t d", t=NT)

            def gather(i):
                pe.wait_ge(moe["pick_ready"], i + 1)
                for tt in range(NT):
                    for n in range(4):
                        mm = pe.matmul(bG[CAP * n:CAP * n + CAP, :], SG[:, tt, :], H2[:, tt, 512 * n:512 * n + 512],
                                       start=(tt == 0), stop=(tt == NT - 1), tile_position=(0, CAP * n))
                mm.then_inc(moe["g_full"], 1)

            def gather_t(i):
                pe.wait_ge(moe["g_copied"], i + 1)
                for c in range(4):
                    mm = pe.transpose(bGT[:, P * c:P * c + P], GS[:, P * c:P * c + P], ident)
                mm.then_inc(moe["gt_full"], 1)

            def spread(i):
                pe.wait_ge(moe["scw_ready"], i + 1)
                for tt in range(NT):
                    mm = pe.transpose(bG[:, P * tt:P * tt + P], SW[:, tt, :], ident)
                mm.then_inc(moe["sct_full"], 1)

            def scatter(i):
                pe.wait_ge(moe["oe_ready"], i + 1)
                pe.wait_ge(moe["scj_ready"], i + 1)
                for m in range(8):
                    c, half = m // 2, m % 2
                    pe.wait_ge(moe["y_added"], i * 8 + m + 1)
                    pe.matmul(ybank[m % 2], OE[:, P * c:P * c + P], SJ[:, 2 * half:2 * half + 2, :],
                              start=True, stop=True).then_inc(moe["y_full"], 1)

            gather(0)
            gather_t(0)
            with pe.Fori(0, tiles) as i:
                pe.wait_ge(moe["xg_ready"], i + 1)
                pe.wait_ge(moe["h_copied"], i * 2 + 1)
                for s in range(8):
                    pe.wait_ge(tile_in[s], i * 16 + 16)
                    for c in range(4):
                        k = 4 * (s % 4) + c
                        mm = pe.matmul(bH[s // 4][CAP * c:CAP * c + CAP, :], XG[:, k % 4, k // 4, :],
                                       ring[:, s, 512 * c:512 * c + 512], start=(s % 4 == 0), stop=(s % 4 == 3),
                                       tile_position=(0, CAP * c))
                    mm.then_inc(moe["w_used"], 1)
                pe.wait_ge(moe["sct_copied"], i + 1)
                gather(i + 1)
                pe.wait_ge(moe["h_copied"], i * 2 + 3)
                pe.wait_ge(moe["at_ready"], i + 1)
                for b in range(2):
                    for c in range(4):
                        mm = pe.transpose(bHT[b][:, P * c:P * c + P], HS[:, b, P * c:P * c + P], ident)
                mm.then_inc(moe["ht_full"], 1)
                scatter(i)
                pe.wait_ge(moe["at_ready"], i + 2)
                for s in range(8, 12):
                    pe.wait_ge(tile_in[s], i * 16 + 16)
                    for c in range(4):
                        mm = pe.matmul(bW2[CAP * c:CAP * c + CAP, :], AT[:, s - 8, :], ring[:, s, 512 * c:512 * c + 512],
                                       start=(s == 8), stop=(s == 11), tile_position=(0, CAP * c))
                    mm.then_inc(moe["w_used"], 1)
                pe.wait_ge(moe["y_added"], i * 8 + 10)
                gather_t(i + 1)
                spread(i)
            scatter(tiles)
            run(1, BC)

        @block.scalar
        def _(act):
            link = [0]

            def then(ins):
                link[0] += 1
                ins.then_inc(act_link, 1)
                act.wait_ge(act_link, link[0])

            def run(k, o):
                jobs = jobs_of(o)
                count = 0
                nr = [s[1] for s in o.steps["pe"] if s[0] == "nrm"]
                idx = [s[1] for s in o.steps["pe"] if s[0] == "idx"]

                def needs(engine, *step):
                    act.wait_ge(done[k][engine], o.at[engine][step])

                def evac(x):
                    item = ("proj", x) if ("proj", x) in o.at["pe"] else (*x, 3) if x[0] == "ada" else x
                    bank = None if x[0] == "ada" else psM if item not in o.acc else acc[o.acc.index(item) % 2]
                    needs("pe", *item)
                    name, n = x if len(x) > 1 else (x[0], 0)
                    if name == "ada":
                        if n:
                            needs("pe", "adaT", n - 1)
                        return act.activation(AD, psM[:, :] if n in o.small_bank else bankO, ACT.Copy)
                    a = bank[:, 0:S]
                    if name in ("k", "q"):
                        i = nr.index(x)
                        if i >= 2:
                            needs("pe", "nrm", nr[i - 2])
                        act.activation(rot_chunk(x), a, ACT.Copy)
                        return act.activation(W(aSQ + i % 2)[:, 0, :], a, ACT.Square)
                    if name in ("qi", "ki", "qr"):
                        return act.activation(rot_chunk(x), a, ACT.Copy)
                    if name == "kr":
                        return act.activation(rot_chunk(x), a, ACT.Copy)
                    if name in ("v", "bv", "dv", "vm"):
                        v = {"v": V_a, "bv": V_b}.get(name, V_c)
                        return act.activation(v[:, :, 2 * n:2 * n + 2, :],
                                              bank[:, :].rearrange("p (k g d) -> p k g d", k=NT, d=P), ACT.Copy)
                    if name == "wi":
                        return act.activation(W(aWI)[:, 0, :], a, ACT.Copy)
                    if name == "idx":
                        qt, c = n
                        i = idx.index(n)
                        if i >= 2:
                            needs("dve", "idx", idx[i - 2])
                        nk = P * (qt + 1)
                        return act.activation(W(aRL + 2 * (i % 2), 2)[:, :, 0:nk],
                                              bank[:, 0:2 * nk].rearrange("p (a s) -> p a s", a=2), ACT.Relu)
                    if name == "p":
                        needs("pe", "idx", idx[-1])
                        return act.activation(W(aPR + n)[:, 0, :], a, ACT.Copy)
                    if name == "pmm":
                        c = 2 * n[0] + n[1]
                        return act.activation(W(MIX + 8 + c)[:, 0, :], a, ACT.Copy, scale=C("pool_scale", c, 1))
                    if name in ("wo", "wb", "wc"):
                        if n >= 2:
                            needs("dve", "res", (name, n - 2))
                        tm = W((aTM if k == 0 else dTM) + n % 2)[:, 0, :]
                        if name == "wo":
                            return act.activation(tm, a, ACT.Copy, scale=gt1[:, n:n + 1])
                        return act.activation(tm, a, ACT.Copy)
                    if name == "router":
                        return act.activation(RTS[0:36, :], bank[0:36, 0:S], ACT.Copy)
                    if name == "h2t":
                        tt, q = n
                        H2 = W(mH2, 16).rearrange("p a s -> p (a s)").rearrange("p (t d) -> p t d", t=NT)
                        return act.activation(H2[:, tt, 512 * q:512 * q + 512], bank[:, :], ACT.Copy)
                    if name == "bk":
                        z = W(bK + 2 * n, 2)
                        act.activation(z[0:64, 0, :], bank[0:64, 0:S], ACT.Copy)
                        return act.activation(z[64:128, 1, :], bank[64:128, 0:S], ACT.Copy)
                    if name == "bq":
                        return act.activation(W(bQ + n)[:, 0, :], a, ACT.Copy)
                    if name == "lx":
                        if n >= 2:
                            needs("dve", "conv", n - 2)
                        return act.activation(W(bLX + n % 2)[:, 0, :], a, ACT.Copy)
                    if name == "lg":
                        return act.activation(W(MIX + n)[:, 0, :], a, ACT.Copy)
                    if name in ("bs", "dg"):
                        if name == "dg" and n == 0:
                            needs("pe", "proj", ("wb", KD - 1))
                        return act.activation(W(MIX + 8 + n)[:, 0, :], a, ACT.Copy)
                    if name == "mg":
                        return act.activation(W(MIX + n)[:, 0, :], a, ACT.Copy)
                    if name == "lgate":
                        if n >= 2:
                            needs("dve", "lruE", n - 2)
                        act.activation(W(bGI + n % 2)[:, 0, :], a, ACT.Sigmoid, bias=C("gx_b", n, 1))
                        return act.activation(W(bGR + n % 2)[:, 0, :], bank[:, S:2 * S], ACT.Sigmoid, bias=C("ga_b", n, 1))
                    if name in ("cq", "ckv"):
                        if n >= 2:
                            needs("pe", "ss", (name, n - 2))
                        act.activation(W((cCQ if name == "cq" else cCKV) + n)[:, 0, :], a, ACT.Copy)
                        return act.activation(W(dSQ + n % 2)[:, 0, :], a, ACT.Square)
                    if name in ("dk", "dq"):
                        return act.activation(W((cDK if name == "dk" else cDQ) + n)[:, 0, :], a, ACT.Copy)
                    if name in ("qn", "kn"):
                        return act.activation(W((cQN if name == "qn" else cKN) + n)[:, 0, :], a, ACT.Copy)
                    raise AssertionError(x)

                for step in o.steps["act"]:
                    what = step[0]
                    if count:
                        act.wait_ge(done[k]["act"], count)
                    if what == "evac":
                        ins = evac(step[1])
                    elif what == "silu_c":
                        ins = act.activation(cs, C("c"), ACT.Silu)
                    elif what == "sqx":
                        act.wait_ge(x_in, 16)
                        ins = act.activation(W(MIX, KD), X[:, :, :], ACT.Square)
                    elif what == "hi":
                        q = step[1]
                        p = o.halves[q]
                        n = o.pieces[p][2]
                        act.wait_ge(unit_in[k][p % LAND[k]], 16 * (p // LAND[k] + 1))
                        if q >= PARTS:
                            needs("pe", *o.last_use[q - PARTS])
                        ins = act.activation(WH[:, q % PARTS, 0:n], land[k][:, p % LAND[k], 0:n], ACT.Copy)
                    elif what == "hh":
                        _, name, c = step
                        if k == 0:
                            needs("dve", "h", name, c)
                            ins = act.activation(HH[:, c, :], W(aHT + c % 2)[:, 0, :], ACT.Copy)
                        else:
                            needs("dve", "scaled", name, c // 4)
                            g = C("gain0" if name == "moe" else "gain1", c, 1)
                            ins = act.activation(HH[:, c, :], W(scaled_at(c))[:, 0, :], ACT.Copy, scale=g)
                    elif what == "mh":
                        _, name, c = step
                        needs("pe", "proj", {"wo": ("p", 7), "wb": ("lg", 7), "wc": ("vm", 3)}[name])
                        made_by = {("wo", 0): ("out", 2), ("wo", 1): ("out", 3), ("wb", 0): ("lmul", 0), ("wb", 1): ("lmul", 1),
                                   ("wb", 2): ("out", ("b", 0, 1, 1)), ("wb", 3): ("out", ("b", 1, 1, 1)),
                                   ("wc", 0): ("out", ("m", 0, 1)), ("wc", 1): ("out", ("m", 1, 1)),
                                   ("wc", 2): ("dfin", 1), ("wc", 3): ("dfin", 3)}.get((name, c))
                        if made_by:
                            needs("dve", *made_by)
                        ins = act.activation(HH[:, 4 * c:4 * c + 4, :], W(MIX + 4 * c, 4), ACT.Copy)
                    elif what == "ch":
                        _, name, c = step
                        if c == 0:
                            needs("pe", "proj", ("mg", 7))
                            needs("dve", "cqn" if name == "cq" else "ckvn")
                        src, at = (cCQ, 0) if name == "cq" else (cCKV, 6)
                        ins = act.activation(HH[:, at + c, :], W(src + c)[:, 0, :], ACT.Copy)
                    elif what == "silu":
                        _, name, n, size = step
                        z = W(MIX + n + (8 if name in ("bs", "dg") else 0), size)
                        ins = act.activation(z, z, ACT.Silu)
                    elif what == "h2":
                        c = step[1]
                        z = W(MIX + c)[:, 0, :]
                        needs("dve", "h2", c)
                        ins = act.activation(z, z, ACT.Identity, bias=sh2[:, c:c + 1])
                    elif what == "sqrtx":
                        needs("dve", "ssx")
                        ins = act.activation(W(aRT)[:, 0, :], W(aRT)[:, 0, :], ACT.Sqrt)
                    elif what == "sqrt":
                        needs("dve", "nrm", step[1])
                        ins = act.activation(W(aRT)[:, 0, :], W(aRT)[:, 0, :], ACT.Sqrt)
                    elif what == "sqrtn":
                        needs("dve", "ssum", step[1])
                        r = W(aRT if k == 0 else dRT)[:, 0, :]
                        ins = act.activation(r, r, ACT.Sqrt)
                    elif what == "sq":
                        x = step[1]
                        n = x[1]
                        needs("dve", "res", x)
                        sq = W((aSQ if k == 0 else dSQ) + n % 2)[:, 0, :]
                        if x[0] == "moe":
                            if n >= 2:
                                needs("pe", "ss", (x[0], n - 2))
                        elif n == 0:
                            sq = W(aSA if k == 0 else dSA)[:, 0, :]
                        elif n >= 3:
                            needs("dve", "sqsum", (x[0], n - 2))
                        if n == KD - 2:
                            act.activation(small[:, 201:202], ones[:, 0:1], ACT.Sqrt)
                        ins = act.activation(sq, X[:, n, :], ACT.Square)
                    elif what == "exp":
                        j = step[1]
                        n, nk = jobs.index(j), keys_of(j)
                        needs("dve", "soft", j)
                        st = jst[:, n % 2, :, :]
                        for h in range(4):
                            s = SB[:, n % 2, h, 0:nk]
                            ins = act.activation(s, s, ACT.Exp, bias=st[:, 1, h:h + 1], accum_out=st[:, 2, h:h + 1])
                        if k and j[0] == "b":
                            ins = act.activation(st[:, 3, :], st[:, 3, :], ACT.Exp)
                    elif what == "pt":
                        j = step[1]
                        n = jobs.index(j)
                        needs("pe", "T", j)
                        if n:
                            needs("pe", "O", jobs[n - 1])
                        heads = 2 if k and j[0] == "d" else 4
                        qt = qt_of(j)
                        ins = act.activation(PTS[:, 0:qt + 1, 0:heads, :], psT[:, 0:qt + 1, 0:heads, :], ACT.Copy)
                    elif what == "pexp":
                        needs("dve", "top1")
                        act.activation(gk, gd, ACT.Exp)
                        ins = act.activation(r1[:, 5, :], r1[:, 4, :], ACT.Exp)
                    elif what == "softplus1":
                        needs("dve", "softplus0")
                        ins = act.activation(tsp[:, 8:16], tsp[:, 0:8], ACT.Exp)
                    elif what == "lambda":
                        needs("dve", "softplus2")
                        ins = act.activation(lam2[:, 2:4], lam2[:, 0:2], ACT.Exp)
                    elif what == "lruB":
                        p = step[1]
                        needs("dve", "lruA", 2 * p + 1)
                        act.activation(W(bLA, 2), W(bGR, 2), ACT.Exp, scale=-1.0)
                        ins = act.activation(W(bTH, 2), W(bGR, 2), ACT.Tanh)
                    elif what == "lruD":
                        needs("dve", "lruC", step[1])
                        ins = act.activation(W(bTH, 2), W(bTH, 2), ACT.Sqrt)
                    elif what == "dsq":
                        p = step[1]
                        needs("dve", "out", ("d", p, 1))
                        if p:
                            needs("dve", "dfin", p - 1)
                        ins = act.activation(W(cDS, 2), W(cOR[p % 2], 2), ACT.Square)
                    elif what == "dsqrt":
                        needs("dve", "dn", step[1])
                        ins = act.activation(W(cDS, 2), W(cDS, 2), ACT.Sqrt)
                    else:
                        raise AssertionError(step)
                    ins.then_inc(done[k]["act"], 1)
                    count += 1

            act.wait_ge(table_in, 32)
            run(0, A)
            act.wait_ge(done[0]["act"], len(A.steps["act"]))
            act.wait_ge(done[0]["dve"], A.at["dve"][("place",)])
            tiles = act.value_load(sti[0:1, 48:49], min_val=1, max_val=MAX_TILES)
            GS = W(mGS, 2).rearrange("p a s -> p (a s)")
            XG = W(mXG, 2).rearrange("p a s -> p (a s)")
            HS = W(mHS, 4).rearrange("p (b a) s -> p b (a s)", b=2)
            OE = W(mOE, 2).rearrange("p a s -> p (a s)")
            ST = W(mST).rearrange("p a s -> p (a s)")

            def copy_gather(i, first=False):
                act.wait_ge(moe["g_full"], i + 1)
                if not first:
                    act.wait_ge(moe["gt_full"], i)
                act.activation(GS, acc[0][:, :], ACT.Copy).then_inc(moe["g_copied"], 1)

            def copy_inputs(i):
                act.wait_ge(moe["gt_full"], i + 1)
                act.activation(XG, acc[1][:, :], ACT.Copy).then_inc(moe["xg_ready"], 1)

            copy_gather(0, True)
            copy_inputs(0)
            with act.Fori(0, tiles) as i:
                for b in range(2):
                    act.wait_ge(moe["w_used"], i * 12 + 4 * (b + 1))
                    if b == 0:
                        act.wait_ge(moe["ht_full"], i + 1)
                    act.activation(HS[:, b, :], bankS[b], ACT.Copy).then_inc(moe["h_copied"], 1)
                copy_gather(i + 1)
                act.wait_ge(moe["hs_ready"], i + 1)
                act.activation(SL1, H1T, ACT.Silu).then_inc(moe["silu_done"], 1)
                act.wait_ge(moe["w_used"], i * 12 + 12)
                act.wait_ge(moe["y_full"], i * 8 + 8)
                act.activation(OE, bankO, ACT.Copy).then_inc(moe["oe_ready"], 1)
                copy_inputs(i + 1)
                act.wait_ge(moe["sct_full"], i + 1)
                act.wait_ge(moe["scj_ready"], i + 1)
                act.activation(ST, acc[0][:, 0:S], ACT.Copy).then_inc(moe["sct_copied"], 1)
            act.wait_ge(moe["y_added"], tiles * 8 + 10)
            run(1, BC)

        @block.vector
        def _(dve):
            link = [0]

            def then(ins):
                link[0] += 1
                ins.then_inc(dve_link, 1)
                dve.wait_ge(dve_link, link[0])

            def shifted_add(out, a, d):
                dve.tensor_copy(out[:, :, 0:d], a[:, :, 0:d])
                then(dve.tensor_tensor(out[:, :, d:S], a[:, :, d:S], a[:, :, 0:S - d], ALU.add))

            def first_max(x, m, key, one, n, lead):
                then(dve.tensor_tensor(key, x, m[:, :, None].to_broadcast([P, NT, n]), ALU.is_equal))
                then(dve.tensor_tensor(key, key, lead[:, None, :].to_broadcast([P, NT, n]), ALU.mult))
                then(dve.tensor_reduce(r1[:, 7, :], key, AX.X, ALU.max))
                then(dve.tensor_tensor(one, key, r1[:, 7, :][:, :, None].to_broadcast([P, NT, n]), ALU.is_equal))

            def run(k, o):
                jobs = jobs_of(o)
                count = 0
                idx = [s[1] for s in o.steps["pe"] if s[0] == "idx"]
                RT = W(aRT if k == 0 else dRT)[:, 0, :]
                T2 = W(aT2 if k == 0 else dT2)[:, 0, :]

                def needs(engine, *step):
                    dve.wait_ge(done[k][engine], o.at[engine][step])

                def softmax_head(j):
                    n, nk, qt = jobs.index(j), keys_of(j), qt_of(j)
                    st = jst[:, n % 2, :, :]
                    s = SB[:, n % 2, :, 0:nk]
                    needs("pe", "S", j)
                    if n >= 2:
                        needs("pe", "T", jobs[n - 2])
                    if k == 0:
                        scale, mask = P ** -0.5, W(aSC + qt)[:, 0, 0:nk]
                    elif j[0] == "b":
                        scale, mask = 64 ** -0.5, K("band") if qt else K("causal", 0, nk)
                    elif j[0] == "d":
                        scale, mask = 64 ** -0.5, K("causal", S * qt, nk)
                    else:
                        scale, mask = 192 ** -0.5, K("causal", S * qt, nk)
                    then(dve.scalar_tensor_tensor(out=s, in0=psS[:, :, 0:nk], scalar=scale,
                                                  in1=mask[:, None, :].to_broadcast([P, 4, nk]),
                                                  op0=ALU.mult, op1=ALU.add))
                    then(dve.tensor_reduce(st[:, 0, :], s, AX.X, ALU.max))
                    if k and j[0] == "b":
                        sink = C("sinks", 8 * j[1] + 4 * j[2], 4)
                        then(dve.tensor_tensor(st[:, 0, :], st[:, 0, :], sink, ALU.max))
                        dve.tensor_tensor(st[:, 3, :], sink, st[:, 0, :], ALU.subtract)
                    return dve.tensor_scalar(st[:, 1, :], st[:, 0, :], -1.0, None, ALU.mult)

                def softmax_tail(j):
                    n, nk = jobs.index(j), keys_of(j)
                    st = jst[:, n % 2, :, :]
                    needs("act", "exp", j)
                    if k and j[0] == "b":
                        then(dve.tensor_tensor(st[:, 2, :], st[:, 2, :], st[:, 3, :], ALU.add))
                    then(dve.reciprocal(st[:, 0, :], st[:, 2, :]))
                    if k and j[0] == "d":
                        then(dve.tensor_tensor(st[:, 1, :], st[:, 0, :], lamn.to_broadcast([P, 4]), ALU.mult))
                        for h in range(2):
                            a, b = SB[:, n % 2, 2 * h, 0:nk], SB[:, n % 2, 2 * h + 1, 0:nk]
                            ins = dve.tensor_scalar(a, a, st[:, 0, 2 * h:2 * h + 1], None, ALU.mult)
                        then(ins)
                        for h in range(2):
                            a, b = SB[:, n % 2, 2 * h, 0:nk], SB[:, n % 2, 2 * h + 1, 0:nk]
                            ins = dve.scalar_tensor_tensor(out=a, in0=b, scalar=st[:, 1, 2 * h + 1:2 * h + 2], in1=a,
                                                           op0=ALU.mult, op1=ALU.add)
                        return ins
                    for h in range(4):
                        a = SB[:, n % 2, h, 0:nk]
                        ins = dve.tensor_scalar(a, a, st[:, 0, h:h + 1], None, ALU.mult)
                    return ins

                def attention_out(j):
                    n, qt = jobs.index(j), qt_of(j)
                    q = slice(P * qt, P * qt + P)
                    needs("pe", "O", j)
                    if k == 0:
                        return dve.tensor_copy(W(MIX + 4 * (j % 2), 4)[:, :, q], psO[:, :, :])
                    if j[0] == "b":
                        for half in range(2):
                            r = slice(64 * half, 64 * half + 64)
                            mix = W(MIX + 8 + 4 * j[1] + 2 * j[2], 2)[r, :, q]
                            ins = dve.tensor_tensor(mix, psO[r, half:4:2, :], mix, ALU.mult)
                        return ins
                    if j[0] == "d":
                        return dve.tensor_copy(W(cOR[j[1] % 2], 2)[:, :, q], psO[:, 0:2, :])
                    mix = W(MIX + 4 * j[1], 4)[:, :, q]
                    return dve.tensor_tensor(mix, psO[:, :, :], mix, ALU.mult)

                def rms(n, width):
                    return dve.tensor_scalar(RT, psM[:, 0:S], 1.0 / width, EPS, ALU.mult, ALU.add)

                for step in o.steps["dve"]:
                    what = step[0]
                    if count:
                        dve.wait_ge(done[k]["dve"], count)
                    if what == "setup":
                        dve.memset(ones[:, :], 1.0)
                        dve.memset(W(aKI, 2), 0.0)
                        ins = dve.memset(W(aSC, 2), 0.0)
                    elif what == "spread_c":
                        needs("act", "silu_c")
                        ins = dve.tensor_copy(cB, cs[:, :, None].to_broadcast([P, KD, CAP]))
                    elif what == "ssx":
                        needs("pe", "ssx")
                        ins = rms(0, D)
                    elif what == "xr":
                        needs("act", "sqrtx")
                        then(dve.reciprocal(RT, RT))
                        ins = dve.tensor_tensor(W(MIX, KD), X[:, :, :], RT[:, None, :].to_broadcast([P, KD, S]), ALU.mult)
                    elif what == "lo":
                        q = step[1]
                        p = o.halves[q]
                        n = o.pieces[p][2]
                        needs("act", "hi", q)
                        ins = dve.tensor_tensor(WL[:, q % PARTS, 0:n], land[k][:, p % LAND[k], 0:n],
                                                WH[:, q % PARTS, 0:n].bitcast(F32), ALU.subtract)
                    elif what == "hl":
                        _, name, c = step
                        needs("act", "hh", name, c)
                        hh = HH[:, c, :].bitcast(F32)
                        if k == 0:
                            ins = dve.tensor_tensor(HL[:, c, :], W(aHT + c % 2)[:, 0, :], hh, ALU.subtract)
                        else:
                            g = C("gain0" if name == "moe" else "gain1", c, 1)
                            ins = dve.scalar_tensor_tensor(out=HL[:, c, :], in0=W(scaled_at(c))[:, 0, :], scalar=g, in1=hh,
                                                           op0=ALU.mult, op1=ALU.subtract)
                    elif what == "scaled":
                        _, name, g = step
                        if g > 1:
                            needs("act", "hh", name, 4 * g - 5)
                        ins = dve.tensor_tensor(W(scaled_at(4 * g), 4), X[:, 4 * g:4 * g + 4, :],
                                                RT[:, None, :].to_broadcast([P, 4, S]), ALU.mult)
                    elif what == "ml":
                        _, name, c = step
                        needs("act", "mh", name, c)
                        ins = dve.tensor_tensor(HL[:, 4 * c:4 * c + 4, :], W(MIX + 4 * c, 4),
                                                HH[:, 4 * c:4 * c + 4, :].bitcast(F32), ALU.subtract)
                    elif what == "cl":
                        _, name, c = step
                        needs("act", "ch", name, c)
                        src, at = (cCQ, 0) if name == "cq" else (cCKV, 6)
                        ins = dve.tensor_tensor(HL[:, at + c, :], W(src + c)[:, 0, :], HH[:, at + c, :].bitcast(F32), ALU.subtract)
                    elif what == "adaT":
                        b = step[1]
                        needs("pe", "adaT", b)
                        a = ada[:, 4 * b:4 * b + 4]
                        then(dve.tensor_reduce(a, (psM[:, :] if b in o.small_bank else bankT[1]).rearrange("p (c r m) -> p c r m", c=4, m=CAP)[:, :, :, 0],
                                               AX.X, ALU.add))
                        ins = dve.tensor_tensor(a, a, C("b_ada", 4 * b, 4), ALU.add)
                    elif what == "h1":
                        ins = dve.scalar_tensor_tensor(out=g1, in0=sc1, scalar=1.0, in1=C("norm1_g"), op0=ALU.add, op1=ALU.mult)
                    elif what == "cols":
                        ins = dve.scalar_tensor_tensor(out=g2, in0=sc2, scalar=1.0, in1=C("norm2_g"), op0=ALU.add, op1=ALU.mult)
                    elif what == "wi":
                        needs("pe", "wiT")
                        ins = dve.tensor_scalar(wis.rearrange("p (t h) -> p t h", t=NT),
                                                psM[:, 0:S].rearrange("p (t n) -> p t n", t=NT)[:, :, 0:16],
                                                (64 ** -0.5) * (16 ** -0.5), None, ALU.mult)
                    elif what == "nrm":
                        needs("pe", "nrm", step[1])
                        ins = rms(0, P)
                    elif what == "qn":
                        x = step[1]
                        needs("act", "sqrt", x)
                        then(dve.reciprocal(RT, RT))
                        g = C("k_norm_g" if x[0] == "k" else "q_norm_g")
                        z = rot_chunk(x)
                        ins = dve.scalar_tensor_tensor(out=z, in0=z, scalar=g, in1=RT, op0=ALU.mult, op1=ALU.mult)
                    elif what == "rot":
                        x = step[1]
                        r = rot_of(x)[-1]
                        z = rot_chunk(x)
                        needs("pe", "rot", x)
                        if step in o.early and not o.early.index(step):
                            dve.wait_ge(rest_in, 16)
                        dve.tensor_tensor(T2, (bankT[0] if step in o.early else psM)[:, 0:S], K("sin" + r), ALU.mult)
                        then(dve.tensor_tensor(z, z, K("cos" + r), ALU.mult))
                        if x[0] in ("ki", "kr"):
                            kz = W(aKI if x[0] == "ki" else cKR, 2)
                            dve.tensor_tensor(kz[0:64, 0, :], z[0:64, :], T2[0:64, :], ALU.add)
                            ins = dve.tensor_tensor(kz[64:128, 1, :], z[64:128, :], T2[64:128, :], ALU.add)
                        else:
                            ins = dve.tensor_tensor(z, z, T2, ALU.add)
                    elif what == "idx":
                        qt, c = step[1]
                        needs("act", "evac", ("idx", step[1]))
                        nk = P * (qt + 1)
                        sc = W(aSC + qt)[:, 0, 0:nk]
                        for h in range(2):
                            at = 16 * qt + 2 * c + h
                            ins = dve.scalar_tensor_tensor(out=sc, in0=W(aRL + 2 * (idx.index(step[1]) % 2) + h)[:, 0, 0:nk],
                                                           scalar=wis[:, at:at + 1], in1=sc, op0=ALU.mult, op1=ALU.add)
                            if h == 0:
                                then(ins)
                    elif what == "topk":
                        qt = step[1]
                        nk = P * (qt + 1)
                        wk, causal = W(aWK + qt)[:, 0, 0:nk], K("causal", S * qt, nk)
                        then(dve.tensor_tensor(wk, W(aSC + qt)[:, 0, 0:nk], causal, ALU.add))
                        for r in range(8):
                            m8 = top[:, 8 * (r % 2):8 * (r % 2) + 8]
                            then(dve.max(m8, wk))
                            then(dve.match_replace(wk, m8, wk, TAKEN))
                        mb = W(aSC + qt)[:, 0, 0:nk]
                        then(dve.tensor_scalar(mb, wk, 2 * NEG, NEG, ALU.is_gt, ALU.mult))
                        ins = dve.tensor_tensor(mb, mb, causal, ALU.add)
                    elif what == "pool":
                        g = step[1]
                        win = POOL_WINDOWS[g]
                        p = W(aPR + 2 * g, 2)
                        needs("act", "evac", ("p", 2 * g + 1))
                        a, b = W(aPS, 2), W(aPS + 2, 2)
                        shifted_add(a, p, 1)
                        d = 2
                        while d < win:
                            shifted_add(b, a, d)
                            a, b = b, a
                            d *= 2
                        dve.tensor_tensor(b[:, :, 0:16], a[:, :, 0:16],
                                          K("icount", 16 * g, 16)[:, None, :].to_broadcast([P, 2, 16]), ALU.mult)
                        then(dve.tensor_scalar(b[:, :, 16:S], a[:, :, 16:S], 1.0 / win, None, ALU.mult))
                        ins = dve.tensor_tensor(p, b, p, ALU.subtract)
                    elif what == "soft":
                        ins = softmax_head(step[1])
                    elif what == "scale":
                        ins = softmax_tail(step[1])
                    elif what == "out":
                        ins = attention_out(step[1])
                    elif what == "res":
                        name, n = step[1]
                        if step[1] == ("moe", 0):
                            dve.memset(W(bK, 4), 0.0)
                        if step[1] == ("wb", 0):
                            dve.memset(W(cDZ, 4), 0.0)
                            dve.memset(W(cKR, 2), 0.0)
                        if name == "moe":
                            ins = dve.scalar_tensor_tensor(out=X[:, n, :], in0=W(mYT + n)[:, 0, :], scalar=gt2[:, n:n + 1],
                                                           in1=X[:, n, :], op0=ALU.mult, op1=ALU.add)
                        else:
                            needs("act", "evac", step[1])
                            tm = W((aTM if k == 0 else dTM) + n % 2)[:, 0, :]
                            ins = dve.tensor_tensor(X[:, n, :], X[:, n, :], tm, ALU.add)
                    elif what == "sqsum":
                        x = step[1]
                        needs("act", "sq", x)
                        total = W(aSA if k == 0 else dSA)[:, 0, :]
                        ins = dve.tensor_tensor(total, total, W((aSQ if k == 0 else dSQ) + x[1] % 2)[:, 0, :], ALU.add)
                    elif what == "ssum":
                        name = step[1]
                        width = {"cq": 768, "ckv": 512}.get(name, D)
                        needs("pe", "ss", (name, width // P - 1))
                        ins = rms(0, width)
                    elif what == "rstd":
                        needs("act", "sqrtn", step[1])
                        ins = dve.reciprocal(RT, RT)
                    elif what == "h":
                        _, name, c = step
                        if c >= 2:
                            needs("act", "hh", name, c - 2)
                        ins = dve.tensor_scalar(W(aHT + c % 2)[:, 0, :], W(MIX + c)[:, 0, :], g1[:, c:c + 1], sh1[:, c:c + 1],
                                                ALU.mult, ALU.add)
                    elif what in ("h2", "final"):
                        g = g2 if what == "h2" else C("gain_f")
                        for c in [step[1]] if what == "h2" else range(4 * step[1], 4 * step[1] + 4):
                            ins = dve.scalar_tensor_tensor(out=W(MIX + c)[:, 0, :], in0=X[:, c, :], scalar=g[:, c:c + 1],
                                                           in1=RT, op0=ALU.mult, op1=ALU.mult)
                    elif what in ("cqn", "ckvn"):
                        name = what[:-1]
                        needs("act", "sqrtn", name)
                        then(dve.reciprocal(RT, RT))
                        g, at, n = (C("q_norm"), cCQ, 6) if name == "cq" else (C("kv_norm"), cCKV, 4)
                        for c in range(n):
                            z = W(at + c)[:, 0, :]
                            ins = dve.scalar_tensor_tensor(out=z, in0=z, scalar=g[:, c:c + 1], in1=RT,
                                                           op0=ALU.mult, op1=ALU.mult)
                    elif what == "top1":
                        needs("pe", "routeT")
                        then(dve.tensor_copy(rt[:, 0:72], psM[:, 0:72]))
                        gl = LG[:, :, 0:4]
                        then(dve.tensor_reduce(r1[:, 0, :], gl, AX.X, ALU.max))
                        dve.tensor_tensor(gd, gl, r1[:, 0, :][:, :, None].to_broadcast([P, NT, 4]), ALU.subtract)
                        first_max(gl, r1[:, 0, :], gk, goh, 4, K("rev", 4, 4))
                        for g in range(4):
                            ins = dve.tensor_tensor(sel[:, :, g, :], LG[:, :, 4 + 8 * g:12 + 8 * g],
                                                    goh[:, :, g:g + 1].to_broadcast([P, NT, 8]), ALU.mult)
                        then(ins)
                        then(dve.tensor_tensor(els, sel[:, :, 0, :], sel[:, :, 1, :], ALU.add))
                        then(dve.tensor_tensor(els, els, sel[:, :, 2, :], ALU.add))
                        then(dve.tensor_tensor(els, els, sel[:, :, 3, :], ALU.add))
                        then(dve.tensor_reduce(r1[:, 1, :], els, AX.X, ALU.max))
                        first_max(els, r1[:, 1, :], ek, oh1, 8, K("rev"))
                        then(dve.scalar_tensor_tensor(out=els2, in0=oh1, scalar=TAKEN, in1=els, op0=ALU.mult, op1=ALU.add))
                        then(dve.tensor_reduce(r1[:, 2, :], els2, AX.X, ALU.max))
                        first_max(els2, r1[:, 2, :], ek, oh2, 8, K("rev"))
                        ins = dve.tensor_tensor(r1[:, 4, :], r1[:, 2, :], r1[:, 1, :], ALU.subtract)
                    elif what == "top2":
                        needs("act", "pexp")
                        then(dve.tensor_reduce(r1[:, 3, :], gk, AX.X, ALU.add))
                        then(dve.tensor_scalar(r1[:, 6, :], r1[:, 5, :], 1.0, None, ALU.add))
                        then(dve.tensor_tensor(r1[:, 6, :], r1[:, 6, :], r1[:, 3, :], ALU.mult))
                        then(dve.reciprocal(pos_w[:, 4:6], r1[:, 6, :]))
                        dve.tensor_tensor(pos_w[:, 6:8], pos_w[:, 4:6], r1[:, 5, :], ALU.mult)
                        for kk, one in enumerate((oh1, oh2)):
                            for g in range(4):
                                ins = dve.tensor_tensor(A12[:, kk, :, g, :], one, goh[:, :, g:g + 1].to_broadcast([P, NT, 8]),
                                                        ALU.mult)
                        then(ins)
                        ins = dve.tensor_tensor(MM.rearrange("p t n -> p (t n)"),
                                                A12[:, 0].rearrange("p t g e -> p (t g e)"),
                                                A12[:, 1].rearrange("p t g e -> p (t g e)"), ALU.add)
                    elif what == "place":
                        needs("pe", "cum")
                        dve.memset(zero32, 0.0)
                        then(dve.tensor_copy(cumS, psM[:, 0:96]))
                        cnt = cumS[:, 64:96]
                        then(dve.tensor_tensor(cmp8, cnt[:, :, None].to_broadcast([P, 32, 8]),
                                               K("cap")[:, None, :].to_broadcast([P, 32, 8]), ALU.is_gt))
                        then(dve.tensor_reduce(nt, cmp8, AX.X, ALU.add))
                        then(dve.tensor_scalar(nt[:, 0:1], nt[:, 0:1], 1.0, None, ALU.max))
                        then(dve.tensor_tensor_scan(incl, nt, zero32, 0.0, ALU.add, ALU.add))
                        then(dve.tensor_tensor(excl, incl, nt, ALU.subtract))
                        for tt in range(NT):
                            ins = dve.scalar_tensor_tensor(out=slotp[:, tt, :], in0=excl, scalar=float(CAP),
                                                           in1=cumS[:, 32 * tt:32 * tt + 32], op0=ALU.mult, op1=ALU.add)
                        then(ins)
                        for kk in range(2):
                            ins = dve.tensor_tensor(tmp2[:, kk].rearrange("p t n -> p (t n)"),
                                                    A12[:, kk].rearrange("p t g e -> p (t g e)"),
                                                    slotp.rearrange("p t n -> p (t n)"), ALU.mult)
                        then(ins)
                        for kk in range(2):
                            dve.tensor_reduce(pos_w[:, 2 * kk:2 * kk + 2], tmp2[:, kk], AX.X, ALU.add)
                        then(dve.tensor_tensor(cmp48, incl[:, None, :].to_broadcast([P, 48, 32]),
                                               K("tile")[:, :, None].to_broadcast([P, 48, 32]), ALU.is_le))
                        dve.tensor_copy(eid[:, 48:49], incl[:, 31:32])
                        then(dve.tensor_reduce(eid[:, 0:48], cmp48, AX.X, ALU.add))
                        ins = dve.tensor_copy(sti[:, 0:49], eid[:, 0:49])
                    elif what == "softplus0":
                        then(dve.tensor_scalar(tsp[:, 16:24], C("lam"), -1.0, None, ALU.mult))
                        then(dve.tensor_tensor(tsp[:, 24:32], tsp[:, 16:24], C("lam"), ALU.max))
                        ins = dve.tensor_scalar(tsp[:, 0:8], tsp[:, 24:32], -1.0, None, ALU.mult)
                    elif what == "softplus2":
                        needs("act", "softplus1")
                        e, y, y2, pl = tsp[:, 8:16], tsp[:, 24:32], tsp[:, 32:40], tsp[:, 0:8]
                        then(dve.tensor_scalar(y2, e, 2.0, None, ALU.add))
                        then(dve.reciprocal(y2, y2))
                        then(dve.tensor_tensor(y, e, y2, ALU.mult))
                        then(dve.tensor_tensor(y2, y, y, ALU.mult))
                        then(dve.memset(pl, 1.0 / 17))
                        for m in (15, 13, 11, 9, 7, 5, 3, 1):
                            then(dve.tensor_tensor(pl, pl, y2, ALU.mult))
                            then(dve.tensor_scalar(pl, pl, 1.0 / m, None, ALU.add))
                        then(dve.tensor_tensor(pl, pl, y, ALU.mult))
                        then(dve.tensor_scalar(tsp[:, 16:24], tsp[:, 16:24], 0.0, None, ALU.max))
                        then(dve.scalar_tensor_tensor(out=cL, in0=pl, scalar=2.0, in1=tsp[:, 16:24], op0=ALU.mult, op1=ALU.add))
                        dl = C("dl").rearrange("p (a b d) -> p a b d", a=2, b=2)
                        prod = W(aQI)[:, 0, 0:128].rearrange("p (a d) -> p a d", a=2)
                        dve.tensor_scalar(cL, cL, LRU_C, None, ALU.mult)
                        then(dve.tensor_tensor(prod, dl[:, :, 0, :], dl[:, :, 1, :], ALU.mult))
                        ins = dve.tensor_reduce(lam2[:, 0:2], prod, AX.X, ALU.add)
                    elif what == "lambda":
                        needs("act", "lambda")
                        dve.tensor_scalar(sub, C("subln"), 1.0 - LAMBDA_INIT, None, ALU.mult)
                        then(dve.tensor_tensor(lamn, lam2[:, 3:4], lam2[:, 2:3], ALU.subtract))
                        ins = dve.tensor_scalar(lamn, lamn, -LAMBDA_INIT, None, ALU.add)
                    elif what == "conv":
                        n = step[1]
                        needs("act", "evac", ("lx", n))
                        x, y = W(bLX + n % 2)[:, 0, :], W(bY + n)[:, 0, :]
                        cw = C("conv_w", 4 * n, 4)
                        then(dve.tensor_scalar(y, x, cw[:, 3:4], C("conv_b", n, 1), ALU.mult, ALU.add))
                        for d in (1, 2, 3):
                            ins = dve.scalar_tensor_tensor(out=y[:, d:S], in0=x[:, 0:S - d], scalar=cw[:, 3 - d:4 - d],
                                                           in1=y[:, d:S], op0=ALU.mult, op1=ALU.add)
                            if d < 3:
                                then(ins)
                    elif what == "lruA":
                        n = step[1]
                        needs("act", "evac", ("lgate", n))
                        g = W(bGR + n % 2)[:, 0, :]
                        dve.tensor_tensor(W(bGI + n % 2)[:, 0, :], W(bGI + n % 2)[:, 0, :], W(bY + n)[:, 0, :], ALU.mult)
                        ins = dve.tensor_scalar(g, g, cL[:, n:n + 1], None, ALU.mult)
                    elif what == "lruC":
                        needs("act", "lruB", step[1])
                        a, th, q = W(bLA, 2), W(bTH, 2), W(bGR, 2)
                        then(dve.tensor_tensor(q, a, a, ALU.mult))
                        ins = dve.scalar_tensor_tensor(out=th, in0=q, scalar=1.0, in1=th, op0=ALU.add, op1=ALU.mult)
                    elif what == "lruE":
                        n = step[1]
                        needs("act", "lruD", n // 2)
                        gi, th, a = (W(z + n % 2)[:, 0, :] for z in (bGI, bTH, bLA))
                        then(dve.tensor_tensor(gi, gi, th, ALU.mult))
                        ins = dve.tensor_tensor_scan(W(bY + n)[:, 0, :], a, gi, 0.0, ALU.mult, ALU.add)
                    elif what == "lmul":
                        g = step[1]
                        needs("act", "silu", "lg", 4 * g, 4)
                        ins = dve.tensor_tensor(W(MIX + 4 * g, 4), W(MIX + 4 * g, 4), W(bY + 4 * g, 4), ALU.mult)
                    elif what == "dkz":
                        p = step[1]
                        needs("act", "evac", ("dk", 2 * p + 1))
                        if p:
                            needs("pe", "S", ("d", p - 1, 1))
                        for h in range(2):
                            z = W(cDZ + 2 * h, 2)
                            src = W(cDK + 2 * p + h)[:, 0, :]
                            dve.tensor_copy(z[0:64, 0, :], src[0:64, :])
                            ins = dve.tensor_copy(z[64:128, 1, :], src[64:128, :])
                    elif what == "dn":
                        needs("pe", "dn", step[1])
                        ins = dve.tensor_scalar(W(cDS, 2), psM[:, :].rearrange("p (a s) -> p a s", a=2), 1.0 / P, EPS,
                                                ALU.mult, ALU.add)
                    elif what == "dfin":
                        p = step[1]
                        needs("act", "dsqrt", p)
                        r, z, mix = W(cDS, 2), W(cOR[p % 2], 2), W(MIX + 8 + 2 * p, 2)
                        then(dve.reciprocal(r, r))
                        then(dve.scalar_tensor_tensor(out=z, in0=z, scalar=sub, in1=r, op0=ALU.mult, op1=ALU.mult))
                        ins = dve.tensor_tensor(mix, mix, z, ALU.mult)
                    else:
                        raise AssertionError(step)
                    ins.then_inc(done[k]["dve"], 1)
                    count += 1

            dve.wait_ge(table_in, 32)
            run(0, A)
            dve.wait_ge(done[0]["dve"], len(A.steps["dve"]))
            dve.wait_ge(done[0]["pe"], len(A.steps["pe"]))
            tiles = dve.value_load(sti[0:1, 48:49], min_val=1, max_val=MAX_TILES)
            OE = W(mOE, 2).rearrange("p a s -> p (a s)")
            ST = W(mST).rearrange("p a s -> p (a s)")
            SJ = W(mSJ, 4)
            SW = W(mSW).rearrange("p a s -> p (a s)").rearrange("p (t c) -> p t c", t=NT)
            YT = W(mYT, 16)
            slot, weight = (lambda kk, tt: pos_w[:, 2 * kk + tt:2 * kk + tt + 1]), (lambda kk, tt: pos_w[:, 4 + 2 * kk + tt:5 + 2 * kk + tt])
            dve.memset(OE, 0.0).then_inc(moe["oe_ready"], 1)
            dve.memset(SJ, 0.0).then_inc(moe["scj_ready"], 1)
            dve.memset(YT[:, 0:8, :], 0.0).then_inc(moe["y_added"], 1)
            dve.memset(YT[:, 8:16, :], 0.0).then_inc(moe["y_added"], 1)
            dve.memset(AT, 0.0).then_inc(moe["at_ready"], 1)
            dve.memset(H1T, 0.0).then_inc(moe["ht_full"], 1)
            dve.memset(H3T, 0.0).then_inc(moe["h_copied"], 1)
            dve.memset(SL1, 0.0).then_inc(moe["sct_copied"], 1)
            dve.tensor_copy(J, K("slot")).then_inc(moe["j_ready"], 1)

            def pick(i, first=False):
                dve.wait_ge(moe["j_ready"], i + 1)
                if not first:
                    dve.wait_ge(moe["g_full"], i)
                for tt in range(NT):
                    dve.tensor_scalar(SG2[:, tt, :], J[:, 0:CAP], slot(0, tt), None, ALU.is_equal)
                    ins = dve.tensor_scalar(SG[:, tt, :], J[:, 0:CAP], slot(1, tt), None, ALU.is_equal)
                ins.then_inc(moe["pick_half"], 1)
                dve.wait_ge(moe["pick_half"], i + 1)
                dve.tensor_tensor(SG, SG, SG2, ALU.add).then_inc(moe["pick_ready"], 1)

            def weigh(i, first=False):
                if not first:
                    dve.wait_ge(moe["sct_full"], i)
                for tt in range(NT):
                    dve.tensor_scalar(SWA_[:, tt, :], J, slot(0, tt), weight(0, tt), ALU.is_equal, ALU.mult)
                    ins = dve.tensor_scalar(SW[:, tt, :], J, slot(1, tt), weight(1, tt), ALU.is_equal, ALU.mult)
                ins.then_inc(moe["weigh_half"], 1)
                dve.wait_ge(moe["weigh_half"], i + 1)
                dve.tensor_tensor(SW, SW, SWA_, ALU.add).then_inc(moe["scw_ready"], 1)
                dve.wait_ge(moe["scw_ready"], i + 1)
                dve.tensor_scalar(J, J, float(CAP), None, ALU.add).then_inc(moe["j_ready"], 1)

            def add_out(m, i):
                c, half = m // 2, m % 2
                y = YT[:, 8 * half + c:8 * half + c + 5:4, :]
                src = [psM, acc[1]][m % 2][:, :].rearrange("p (a s) -> p a s", a=2)
                dve.wait_ge(moe["y_full"], i * 8 + m + 1)
                dve.tensor_tensor(y, src, y, ALU.add).then_inc(moe["y_added"], 1)

            pick(0, True)
            weigh(0, True)
            dve.wait_ge(moe["y_added"], 2)
            with dve.Fori(0, tiles) as i:
                pick(i + 1)
                dve.wait_ge(moe["ht_full"], i + 2)
                dve.wait_ge(moe["at_ready"], i + 1)
                dve.tensor_reduce(H1T, psT[:, 0, :, :].rearrange("p c (r m) -> p c m r", m=CAP), AX.X, ALU.add)\
                    .then_inc(moe["hs_ready"], 1)
                dve.tensor_reduce(H3T, psT[:, 1, :, :].rearrange("p c (r m) -> p c m r", m=CAP), AX.X, ALU.add)\
                    .then_inc(moe["h3_ready"], 1)
                dve.wait_ge(moe["silu_done"], i + 1)
                dve.wait_ge(moe["h3_ready"], i + 1)
                dve.tensor_tensor(AT, SL1, H3T, ALU.mult).then_inc(moe["at_ready"], 1)
                dve.wait_ge(moe["y_added"], i * 8 + 2)
                for m in range(8):
                    add_out(m, i)
                dve.wait_ge(moe["sct_copied"], i + 2)
                for c in range(4):
                    ins = dve.tensor_scalar(SJ[:, c, :], ST, K("group", c, 1), None, ALU.mult)
                ins.then_inc(moe["scj_ready"], 1)
                weigh(i + 1)
            dve.wait_ge(moe["y_added"], tiles * 8 + 2)
            for m in range(8):
                add_out(m, tiles)
            dve.wait_ge(moe["y_added"], tiles * 8 + 10)
            dve.wait_ge(moe["j_ready"], tiles + 2)
            run(1, BC)




def _unit(w):
    k, n = w.shape
    return w.reshape(k // P, P, n).transpose(1, 0, 2).reshape(P, -1)


def _stream(order, part):
    out = np.zeros((len(order.units), P, UNIT), np.float32)
    for u, key in enumerate(order.units):
        a = part(key)
        out[u, :, 0:a.shape[1]] = a
    return out


def kernel(**inputs):
    import concourse.bacc as bacc
    from concourse.bass_utils import run_bass_kernel_spmd

    a = {k: np.ascontiguousarray(v) for k, v in inputs.items()}
    w_in, w_out, w_ada = a["w_in"][0], a["w_out"][0], a["w_ada"][0]
    off = {"q": 0, "k": 1024, "v": 1280, "qi": 1536, "ki": 2560, "wi": 2624, "p": 2640}
    off_b = {"lx": 0, "lg": 1024, "bq": 2048, "bk": 3072, "bv": 3200, "bs": 3328}
    off_c = {"cq": 0, "ckv": 768, "kr": 1280, "mg": 1344, "dq": 2368, "dk": 3392, "dv": 4416, "dg": 5440}
    e_in, o_in = a["l0_w_in_2"], a["l1_w_in_2"]
    uq = a["l1_w_uq_2"].reshape(768, 8, 192)
    uq = np.concatenate([uq[:, :, 0:128].reshape(768, 1024), uq[:, :, 128:].reshape(768, 512)], axis=1)
    ukv = a["l1_w_ukv_2"].reshape(512, 8, 2, 128)

    def twice(w):
        return np.concatenate([w, w], axis=1)

    def part_a(key):
        name, n = key[0], key[1]
        if name == "ada":
            w = w_ada[512 * key[2]:512 * key[2] + 512, 512 * n:512 * n + 512]
            return w.reshape(4, P, 512).transpose(1, 0, 2).reshape(P, -1)
        if name == "wo":
            return _unit(np.roll(w_out[:, P * n:P * n + P], D // 2, 0))
        if name == "ki":
            return _unit(twice(w_in[:, off["ki"]:off["ki"] + 64]))
        if name == "wi":
            return _unit(np.tile(w_in[:, off["wi"]:off["wi"] + 16], (1, 8)))
        if name == "v":
            return _unit(w_in[1024 * key[2]:1024 * key[2] + 1024, off["v"]:off["v"] + 256])
        return _unit(w_in[:, off[name] + P * n:off[name] + P * (n + 1)])

    def part_bc(key):
        name, n = key[0], key[1]
        if name in ("bv", "dv"):
            rows = slice(1024 * key[2], 1024 * key[2] + 1024)
            if name == "dv":
                return _unit(o_in[rows, off_c["dv"] + 256 * n:off_c["dv"] + 256 * n + 256])
            at = off_b["bv"]
            return _unit(np.concatenate([twice(e_in[rows, at:at + 64]), twice(e_in[rows, at + 64:at + 128])], axis=1))
        if name == "bk":
            return _unit(twice(e_in[:, off_b[name] + 64 * n:off_b[name] + 64 * n + 64]))
        if name in off_b:
            return _unit(e_in[:, off_b[name] + P * n:off_b[name] + P * n + P])
        if name == "wb":
            return _unit(np.roll(a["l0_w_out_2"][:, P * n:P * n + P], D // 2, 0))
        if name == "wc":
            return _unit(np.roll(a["l1_w_out_2"][:, P * n:P * n + P], D // 2, 0))
        if name == "kr":
            return _unit(twice(o_in[:, off_c["kr"]:off_c["kr"] + 64]))
        if name == "uq":
            return np.concatenate([_unit(uq[:, P * c:P * c + P]) for c in (2 * n, 2 * n + 1)], axis=1)
        if name == "ukv":
            return np.concatenate([_unit(ukv[:, 2 * n, 0]), _unit(ukv[:, 2 * n + 1, 0]),
                                   _unit(ukv[:, 2 * n:2 * n + 2, 1].reshape(512, 256))], axis=1)
        return _unit(o_in[:, off_c[name] + P * n:off_c[name] + P * n + P])

    def column(v):
        return v.reshape(-1, P).T

    def rows(v):
        return np.broadcast_to(v.reshape(1, -1), (P, v.size))

    cols = np.concatenate([
        column(a["c"]), column(a["b_ada"]), column(a["norm1_g"]), column(a["q_norm_g"]), column(a["k_norm_g"]),
        column(a["pool_scale"]), column(a["norm2_g"]), column(a["norm_gains_2"][0]), column(a["norm_gains_2"][1]),
        column(a["final_norm_gain_2"]),
        a["l0_conv_w_2"].reshape(4, 8, P).transpose(2, 1, 0).reshape(P, 32), column(a["l0_conv_b_2"]),
        column(a["l0_gate_x_b_2"]), column(a["l0_gate_a_b_2"]), column(a["l0_lru_lambda_2"]),
        column(a["l1_q_norm_2"]), column(a["l1_kv_norm_2"]), column(a["l1_subln_2"]), rows(a["l0_sinks_2"]),
        rows(a["l1_lambda_q1_2"]), rows(a["l1_lambda_k1_2"]), rows(a["l1_lambda_q2_2"]), rows(a["l1_lambda_k2_2"]),
    ], axis=1)
    route = np.concatenate([a["w_grp"][0], a["w_exp"][0]], axis=1)
    up = lambda w: w[0].reshape(N_EXPERTS, 4, 4, P, DE).transpose(0, 1, 3, 2, 4).reshape(N_EXPERTS, 4, P, UNIT)
    arrays = {
        "const": constants(),
        "cols": cols,
        "xT": a["x"][0].T.reshape(KD, P, S).transpose(1, 0, 2),
        "stream_a": _stream(A, part_a),
        "stream_bc": _stream(BC, part_bc),
        "w_pool": a["w_pool"][0].reshape(4, 2, P, 256).transpose(2, 0, 1, 3).reshape(P, UNIT),
        "w_route": _unit(route),
        "w_gates": np.stack([a["l0_gate_x_w_2"], a["l0_gate_a_w_2"]]).transpose(2, 0, 1, 3).reshape(P, UNIT),
        "w1": up(a["w1"]),
        "w3": up(a["w3"]),
        "w2": a["w2"][0].reshape(N_EXPERTS, 4, P, UNIT),
    }
    arrays = {k: np.ascontiguousarray(v) for k, v in arrays.items()}
    nc = bacc.Bacc("TRN2", target_bir_lowering=False, num_devices=1)
    t = {k: nc.dram_tensor(f"in_{k}", v.shape, F32, kind="ExternalInput").ap() for k, v in arrays.items()}
    t["out"] = nc.dram_tensor("out_0", (P, KD, S), F32, kind="ExternalOutput").ap()
    program(nc, t)
    r = run_bass_kernel_spmd(nc, [{f"in_{k}": v for k, v in arrays.items()}], core_ids=[0])
    return r.results[0]["out_0"].transpose(2, 1, 0).reshape(1, S, D)
```
